# Optimizing a Trainium2 kernel written in Bass

```python
import jax
import jax.numpy as jnp
from jax import lax
import numpy as np

D_MODEL = 1024
BATCH = 1
SEQ = 1024
DEPTH = 1
DEC_BATCH = 1
DEC_SEQ = 256
PAST_LEN = 128

F32 = jnp.float32
HEAD_DIM = 64
MIX_WIDTH = D_MODEL
N_HEADS_A = MIX_WIDTH // (2 * HEAD_DIM)
WIDTH_A = N_HEADS_A * HEAD_DIM
N_HEADS_B = MIX_WIDTH // (2 * HEAD_DIM)
N_KV_B = N_HEADS_B // 4
WIDTH_B = N_HEADS_B * HEAD_DIM
KV_WIDTH_B = N_KV_B * HEAD_DIM
IN_COLS = 3 * WIDTH_A + WIDTH_B + 2 * KV_WIDTH_B
SPLITS = (WIDTH_A, 2 * WIDTH_A, 3 * WIDTH_A, 3 * WIDTH_A + WIDTH_B, 3 * WIDTH_A + WIDTH_B + KV_WIDTH_B)
DILATED_PATTERNS = ((128, 1), (512, 4), (2048, 16))
ROPE_THETA = 500000.0
ROPE_DIMS_A = HEAD_DIM // 4
AXIAL_THETA = 10000.0
GRID_W = 64
Q_BLOCK = 128
N_GROUPS = 4
EXPERTS_PER_GROUP = 8
N_EXPERTS = N_GROUPS * EXPERTS_PER_GROUP
TOP_K_IN_GROUP = 2
D_EXPERT = D_MODEL // 2
MOE_BLOCK = 128
EPS = 1e-6
NEG = -1e30

kernel_name = 'hybrid_dilated_axial_hmoe_encoder'

def rmsnorm(x, g):
    xf = x.astype(F32)
    y = xf * lax.rsqrt(jnp.mean(xf * xf, axis=-1, keepdims=True) + EPS)
    return (y * g.astype(F32)).astype(x.dtype)

def rope_tables(pos, n_dims, theta):
    inv = theta ** (-jnp.arange(0, n_dims, 2, dtype=F32) / n_dims)
    ang = pos.astype(F32)[:, None] * inv[None, :]
    return jnp.cos(ang), jnp.sin(ang)

def apply_rope(x, cos, sin):
    n2 = x.shape[-1] // 2
    x1 = x[..., :n2].astype(F32)
    x2 = x[..., n2:].astype(F32)
    c = cos[:, None, :]
    s = sin[:, None, :]
    return jnp.concatenate([x1 * c - x2 * s, x1 * s + x2 * c], axis=-1).astype(x.dtype)

def partial_rope(x, cos, sin):
    return jnp.concatenate([apply_rope(x[..., :ROPE_DIMS_A], cos, sin), x[..., ROPE_DIMS_A:]], axis=-1)

def axial_rope(x, cos_r, sin_r, cos_c, sin_c):
    half = HEAD_DIM // 2
    return jnp.concatenate([apply_rope(x[..., :half], cos_r, sin_r), apply_rope(x[..., half:], cos_c, sin_c)], axis=-1)

def dilated_branch(q, k, v, window, dil):
    B, S, H, Dh = q.shape
    W = window // (2 * dil)
    L = S // dil
    nb = -(-L // W)
    Lp = nb * W
    qr = q.reshape(B, L, dil, H, Dh)
    kr = k.reshape(B, L, dil, H, Dh)
    vr = v.reshape(B, L, dil, H, Dh)
    qb = jnp.pad(qr, ((0, 0), (0, Lp - L), (0, 0), (0, 0), (0, 0))).reshape(B, nb, W, dil, H, Dh)
    pad_kv = ((0, 0), (W, Lp - L + W), (0, 0), (0, 0), (0, 0))
    kp = jnp.pad(kr, pad_kv)
    vp = jnp.pad(vr, pad_kv)

    def bands(a):
        return jnp.concatenate([a[:, o:o + Lp].reshape(B, nb, W, dil, H, Dh) for o in (0, W, 2 * W)], axis=2)

    kb = bands(kp)
    vb = bands(vp)
    i = jnp.arange(W)[:, None]
    m = jnp.arange(3 * W)[None, :]
    delta = m - W - i
    jk = jnp.arange(nb)[:, None, None] * W - W + m[None]
    valid = (jnp.abs(delta) <= W)[None] & (jk >= 0) & (jk < L)
    s = jnp.einsum('bnqrhd,bnkrhd->bnrhqk', qb, kb, preferred_element_type=F32) * (Dh ** -0.5)
    s = jnp.where(valid[None, :, None, None], s, NEG)
    mx = jnp.max(s, axis=-1, keepdims=True)
    p = jnp.exp(s - mx)
    den = jnp.sum(p, axis=-1, keepdims=True)
    o = jnp.einsum('bnrhqk,bnkrhd->bnqrhd', (p / den).astype(v.dtype), vb, preferred_element_type=F32)
    lse = (mx + jnp.log(den))[..., 0]
    o = o.reshape(B, Lp, dil, H, Dh)[:, :L].reshape(B, S, H, Dh)
    lse = jnp.transpose(lse, (0, 1, 4, 2, 3)).reshape(B, Lp, dil, H)[:, :L].reshape(B, S, H)
    return o, lse

def mixer_dilated(q, k, v):
    B, S, H, Dh = q.shape
    outs, lses = [], []
    for window, dil in DILATED_PATTERNS:
        o, l = dilated_branch(q, k, v, window, dil)
        outs.append(o)
        lses.append(l)
    w = jax.nn.softmax(jnp.stack(lses, 0), axis=0)
    o = jnp.sum(w[..., None] * jnp.stack(outs, 0), axis=0)
    return o.reshape(B, S, H * Dh).astype(q.dtype)

def mixer_axial_gqa(q, k, v):
    B, S, Hq, Dh = q.shape
    Hkv = k.shape[2]
    G = Hq // Hkv
    nqb = S // Q_BLOCK
    qb = jnp.moveaxis(q.reshape(B, nqb, Q_BLOCK, Hkv, G, Dh), 1, 0)
    scale = Dh ** -0.5

    def block(qblk):
        s = jnp.einsum('bqkgd,bskd->bkgqs', qblk, k, preferred_element_type=F32) * scale
        p = jax.nn.softmax(s, axis=-1).astype(v.dtype)
        return jnp.einsum('bkgqs,bskd->bqkgd', p, v, preferred_element_type=F32).astype(q.dtype)

    o = lax.map(block, qb)
    return jnp.moveaxis(o, 0, 1).reshape(B, S, Hq * Dh)

def moe_dispatch(xs, expert, gate, w1, w3, w2):
    T, D = xs.shape
    K = expert.shape[1]
    A = T * K
    flat_e = expert.reshape(-1)
    flat_tok = jnp.repeat(jnp.arange(T, dtype=jnp.int32), K)
    flat_w = gate.reshape(-1).astype(F32)
    order = jnp.argsort(flat_e)
    se = flat_e[order]
    counts = jnp.bincount(flat_e, length=N_EXPERTS)
    starts = jnp.cumsum(counts) - counts
    pcounts = (counts + MOE_BLOCK - 1) // MOE_BLOCK * MOE_BLOCK
    pends = jnp.cumsum(pcounts)
    pstarts = pends - pcounts
    dest = pstarts[se] + (jnp.arange(A) - starts[se])
    n_blocks = -(-A // MOE_BLOCK) + N_EXPERTS
    P = n_blocks * MOE_BLOCK
    slot_tok = jnp.full((P,), T, jnp.int32).at[dest].set(flat_tok[order])
    slot_w = jnp.zeros((P,), F32).at[dest].set(flat_w[order])
    block_e = jnp.minimum(jnp.searchsorted(pends, jnp.arange(n_blocks) * MOE_BLOCK, side='right'), N_EXPERTS - 1)
    xpad = jnp.concatenate([xs, jnp.zeros((1, D), xs.dtype)], axis=0)
    xb = xpad[slot_tok].reshape(n_blocks, MOE_BLOCK, D)

    def run(args):
        xblk, e = args
        a = jnp.dot(xblk, w1[e])
        b = jnp.dot(xblk, w3[e])
        return jnp.dot(jax.nn.silu(a) * b, w2[e])

    yb = lax.map(run, (xb, block_e)).reshape(P, D)
    out = jnp.zeros((T + 1, D), F32).at[slot_tok].add(yb.astype(F32) * slot_w[:, None])
    return out[:T].astype(xs.dtype)

def hier_moe(h, w_rg, b_rg, w_re, b_re, w1, w3, w2):
    B, S, D = h.shape
    T = B * S
    xs = h.reshape(T, D)
    g_logits = jnp.dot(xs, w_rg, preferred_element_type=F32) + b_rg.astype(F32)
    g_prob = jax.nn.softmax(g_logits, axis=-1)
    g_sel = jnp.argmax(g_logits, axis=-1)
    g_w = jnp.take_along_axis(g_prob, g_sel[:, None], axis=-1)
    e_logits = (jnp.dot(xs, w_re, preferred_element_type=F32) + b_re.astype(F32)).reshape(T, N_GROUPS, EXPERTS_PER_GROUP)
    e_logits = jnp.take_along_axis(e_logits, g_sel[:, None, None], axis=1)[:, 0]
    e_prob = jax.nn.softmax(e_logits, axis=-1)
    top_p, top_i = lax.top_k(e_prob, TOP_K_IN_GROUP)
    gate = g_w * top_p / jnp.sum(top_p, axis=-1, keepdims=True)
    expert = g_sel[:, None].astype(jnp.int32) * EXPERTS_PER_GROUP + top_i.astype(jnp.int32)
    return moe_dispatch(xs, expert, gate, w1, w3, w2).reshape(B, S, D)

def encoder_layer(x, c, ln1_g, ln2_g, w_ada, b_ada, w_in, w_out, qn_g, kn_g, on_a_g, on_b_g,
                  w_rg, b_rg, w_re, b_re, w1, w3, w2):
    B, S, _ = x.shape
    mod = (jnp.dot(jax.nn.silu(c), w_ada, preferred_element_type=F32) + b_ada.astype(F32)).astype(x.dtype)[:, None, :]
    sh1, sc1, g1, sh2, sc2, g2 = jnp.split(mod, 6, axis=-1)
    h = rmsnorm(x, ln1_g) * (1 + sc1) + sh1
    proj = jnp.dot(h, w_in)
    qa, ka, va, qb, kb, vb = jnp.split(proj, SPLITS, axis=-1)
    t = jnp.arange(S)
    cos_a, sin_a = rope_tables(t, ROPE_DIMS_A, ROPE_THETA)
    qa = partial_rope(qa.reshape(B, S, N_HEADS_A, HEAD_DIM), cos_a, sin_a)
    ka = partial_rope(ka.reshape(B, S, N_HEADS_A, HEAD_DIM), cos_a, sin_a)
    va = va.reshape(B, S, N_HEADS_A, HEAD_DIM)
    o_a = mixer_dilated(qa, ka, va)
    rows = S // GRID_W
    row_pos = jnp.repeat(jnp.arange(rows), GRID_W)
    col_pos = jnp.tile(jnp.arange(GRID_W), rows)
    cos_r, sin_r = rope_tables(row_pos, HEAD_DIM // 2, AXIAL_THETA)
    cos_c, sin_c = rope_tables(col_pos, HEAD_DIM // 2, AXIAL_THETA)
    qb = axial_rope(rmsnorm(qb.reshape(B, S, N_HEADS_B, HEAD_DIM), qn_g), cos_r, sin_r, cos_c, sin_c)
    kb = axial_rope(rmsnorm(kb.reshape(B, S, N_KV_B, HEAD_DIM), kn_g), cos_r, sin_r, cos_c, sin_c)
    vb = vb.reshape(B, S, N_KV_B, HEAD_DIM)
    o_b = mixer_axial_gqa(qb, kb, vb)
    o = jnp.concatenate([rmsnorm(o_a, on_a_g), rmsnorm(o_b, on_b_g)], axis=-1)
    x = x + g1 * jnp.dot(o, w_out)
    h2 = rmsnorm(x, ln2_g) * (1 + sc2) + sh2
    x = x + g2 * hier_moe(h2, w_rg, b_rg, w_re, b_re, w1, w3, w2)
    return x

def trunk(x, c, ln1_g, ln2_g, w_ada, b_ada, w_in, w_out, qn_g, kn_g, on_a_g, on_b_g,
          w_rg, b_rg, w_re, b_re, w1, w3, w2, lnf_g, w_adaf, b_adaf):
    for l in range(DEPTH):
        x = encoder_layer(x, c, ln1_g[l], ln2_g[l], w_ada[l], b_ada[l], w_in[l], w_out[l],
                          qn_g[l], kn_g[l], on_a_g[l], on_b_g[l], w_rg[l], b_rg[l], w_re[l], b_re[l],
                          w1[l], w3[l], w2[l])
    modf = (jnp.dot(jax.nn.silu(c), w_adaf, preferred_element_type=F32) + b_adaf.astype(F32)).astype(x.dtype)[:, None, :]
    shf, scf = jnp.split(modf, 2, axis=-1)
    return rmsnorm(x, lnf_g) * (1 + scf) + shf

def setup_inputs(seed: int = 0) -> dict:
    key = jax.random.key(seed)
    ks = jax.random.split(key, 26)
    D = D_MODEL
    nrm = jax.random.normal
    return {
        'x_prompt': nrm(ks[0], (BATCH, SEQ, D), F32),
        'x_sample': nrm(ks[1], (DEC_BATCH, DEC_SEQ, D), F32),
        'c_prompt': nrm(ks[2], (BATCH, D), F32),
        'c_sample': nrm(ks[3], (DEC_BATCH, D), F32),
        'ln1_g': 1.0 + 0.05 * nrm(ks[4], (DEPTH, D), F32),
        'ln2_g': 1.0 + 0.05 * nrm(ks[5], (DEPTH, D), F32),
        'w_ada': 0.5 * D ** -0.5 * nrm(ks[6], (DEPTH, D, 6 * D), F32),
        'b_ada': 0.02 * nrm(ks[7], (DEPTH, 6 * D), F32),
        'w_in': D ** -0.5 * nrm(ks[8], (DEPTH, D, IN_COLS), F32),
        'w_out': MIX_WIDTH ** -0.5 * nrm(ks[9], (DEPTH, MIX_WIDTH, D), F32),
        'qn_g': 1.0 + 0.05 * nrm(ks[10], (DEPTH, HEAD_DIM), F32),
        'kn_g': 1.0 + 0.05 * nrm(ks[11], (DEPTH, HEAD_DIM), F32),
        'on_a_g': 1.0 + 0.05 * nrm(ks[12], (DEPTH, WIDTH_A), F32),
        'on_b_g': 1.0 + 0.05 * nrm(ks[13], (DEPTH, WIDTH_B), F32),
        'w_rg': D ** -0.5 * nrm(ks[14], (DEPTH, D, N_GROUPS), F32),
        'b_rg': 0.01 * nrm(ks[15], (DEPTH, N_GROUPS), F32),
        'w_re': D ** -0.5 * nrm(ks[16], (DEPTH, D, N_EXPERTS), F32),
        'b_re': 0.01 * nrm(ks[17], (DEPTH, N_EXPERTS), F32),
        'w1': D ** -0.5 * nrm(ks[18], (DEPTH, N_EXPERTS, D, D_EXPERT), F32),
        'w3': D ** -0.5 * nrm(ks[19], (DEPTH, N_EXPERTS, D, D_EXPERT), F32),
        'w2': D_EXPERT ** -0.5 * nrm(ks[20], (DEPTH, N_EXPERTS, D_EXPERT, D), F32),
        'lnf_g': 1.0 + 0.05 * nrm(ks[21], (D,), F32),
        'w_adaf': 0.5 * D ** -0.5 * nrm(ks[22], (D, 2 * D), F32),
        'b_adaf': 0.02 * nrm(ks[23], (2 * D,), F32),
    }

def reference(x_prompt, x_sample, c_prompt, c_sample, ln1_g, ln2_g, w_ada, b_ada, w_in, w_out,
              qn_g, kn_g, on_a_g, on_b_g, w_rg, b_rg, w_re, b_re, w1, w3, w2, lnf_g, w_adaf, b_adaf):
    y_prompt = trunk(x_prompt, c_prompt, ln1_g, ln2_g, w_ada, b_ada, w_in, w_out, qn_g, kn_g, on_a_g, on_b_g,
                     w_rg, b_rg, w_re, b_re, w1, w3, w2, lnf_g, w_adaf, b_adaf)
    y_sample = trunk(x_sample, c_sample, ln1_g, ln2_g, w_ada, b_ada, w_in, w_out, qn_g, kn_g, on_a_g, on_b_g,
                     w_rg, b_rg, w_re, b_re, w1, w3, w2, lnf_g, w_adaf, b_adaf)
    return (y_prompt, y_sample)


_drawn_inputs = setup_inputs


def setup_inputs(seed=0):
    import zlib

    import numpy as np

    out = dict(_drawn_inputs(seed))
    spreads = {}
    factors = {'ln1_g': 4.974,
     'ln2_g': 3.299,
     'qn_g': 8.0,
     'kn_g': 8.0,
     'on_a_g': 4.43,
     'on_b_g': 4.625,
     'b_rg': 37.895,
     'b_re': 8.0}
    for name, (base, spread) in spreads.items():
        noise = np.random.default_rng([zlib.crc32(name.encode()), seed]).standard_normal(out[name].shape)
        drawn = base * np.exp(spread * noise) if base else spread * noise
        out[name] = jnp.asarray(drawn.astype(out[name].dtype))
    for name, factor in factors.items():
        out[name] = (out[name] * factor).astype(out[name].dtype)
    return out
```

```python
from contextlib import ExitStack

import numpy as np

import concourse.bass as bass
from concourse import mybir

F32 = mybir.dt.float32
F32R = mybir.dt.float32r
BF16 = mybir.dt.bfloat16
I32 = mybir.dt.int32
ALU = mybir.AluOpType
ACT = mybir.ActivationFunctionType
AX = mybir.AxisListType

P = 128
D = 1024
KC = D // P
S0, S1 = 1024, 256
T = S0 + S1
NT = T // P
NT0 = S0 // P
HD = 64
NHA = NHB = 8
NKVB = 2
NKH = NHA + NKVB
WA = NHA * HD
IN_COLS = 3 * WA + WA + 2 * NKVB * HD
EPS = 1e-6
NG, EPG, NE, FE = 4, 8, 32, 512
HALF = 512
SCALE = HD ** -0.5
MSPAN = S0 + S0 - P
NOV = (2 * T) // P - 1
NBLK = NE + NOV
BLOCKS = [(0, 512), (512, 1024), (1024, 1536), (1536, 2048), (2048, 2304)]


class Steps:

    def __init__(self, eng, sem):
        self.eng, self.sem, self.base, self.n = eng, sem, 0, 0

    def did(self, ins):
        ins.then_inc(self.sem, 1)
        self.n += 1

    def wait(self):
        self.eng.wait_ge(self.sem, self.base + self.n)

    def enter(self, i, per):
        self.kept, self.per = self.base + self.n, per
        self.base, self.n = i * per + self.kept, 0

    def leave(self, times):
        assert self.n == self.per, (self.n, self.per)
        self.base, self.n = self.kept + times * self.per, 0


class Memory:

    def __init__(self, nc, ctx, prefix):
        self.nc, self.ctx, self.prefix, self.owned = nc, ctx, prefix, []
        ctx.callback(self.release)

    def release(self):
        if self.owned:
            self.nc.clear_and_free_semaphores(self.owned)
            self.nc.all_engine_barrier()

    def sb(self, name, shape, dt=F32):
        return self.ctx.enter_context(self.nc.sbuf_tensor(f"{self.prefix}_{name}", shape, dt))

    def ps(self, name, shape=(P, 512), dt=F32):
        return self.ctx.enter_context(self.nc.psum_tensor(f"{self.prefix}_{name}", list(shape), dt))

    def sem(self, name):
        self.owned.append(self.nc.alloc_semaphore(f"{self.prefix}_{name}"))
        return self.owned[-1]

    def sems(self, name, n):
        return [self.sem(f"{name}{i}") for i in range(n)]


def make_identity(nc, eng, ident, sem):
    eng.memset(ident[:], 0.0).then_inc(sem, 1)
    eng.wait_ge(sem, 1)
    eng.affine_select(out=ident[:], in_=ident[:], compare_op=ALU.not_equal, fill=1.0, base=0,
                      pattern=[[-1, P]], channel_multiplier=1).then_inc(sem, 1)


def stage_modulation(nc, w_hi, w_lo, c_all, w_ada, b_ada, w_adaf, b_adaf, ln1_g, ln2_g, lnf_g, w_in, mods):
    GW = 2 * D
    NR, NW = 3, 2
    WHALF = IN_COLS // 2
    groups = [(w_ada, b_ada, 0, (0, 1), 1, ln1_g), (w_ada, b_ada, GW, (2, 3), None, None),
              (w_ada, b_ada, 2 * GW, (4, 5), 0, ln2_g), (w_adaf, b_adaf, 0, (6, 7), 1, lnf_g)]
    with ExitStack() as ctx:
        m = Memory(nc, ctx, "mod")
        ring = m.sb("ring", [P, NR, GW])
        wraw = m.sb("wraw", [P, NW, WHALF])
        c_sb = m.sb("c", [2, D])
        cT = m.sb("cT", [P, KC, 2])
        ident = m.sb("ident", [2, 2])
        brow = m.sb("brow", [2, GW])
        grow = m.sb("grow", [2, D])
        row = m.sb("row", [2, GW])
        pc = m.ps("pc")
        pm = m.ps("pm", [2, GW])
        c_loaded, silued, id_made = m.sem("c_loaded"), m.sem("silued"), m.sem("id_made")
        cT_ready, cT_copied = m.sem("cT_ready"), m.sem("cT_copied")
        ring_loaded, ring_used = m.sems("ring_loaded", NR), m.sem("ring_used")
        raw_loaded, hi_ready, lo_ready = m.sems("raw_loaded", NW), m.sem("hi_ready"), m.sem("lo_ready")
        row_ready, scaled, rows_stored = (m.sem(n) for n in ("row_ready", "scaled", "rows_stored"))
        bias_loaded = m.sem("bias_loaded")
        block = ctx.enter_context(nc.Block())

        @block.sync
        def _(sp):
            sp.dma_start(c_sb[:], c_all).then_inc(c_loaded, 16)

            def load_bias(g):
                w, b, col, _, _, ln = groups[g]
                if g:
                    sp.wait_ge(rows_stored, 16 * g)
                sp.dma_start(brow[:], b[col:col + GW].unsqueeze(0).to_broadcast([2, GW])).then_inc(bias_loaded, 16)
                sp.dma_start(grow[:], (lnf_g if ln is None else ln)[:].unsqueeze(0).to_broadcast([2, D])).then_inc(bias_loaded, 16)

            def load_w_in(n):
                k, half = divmod(n, 2)
                if n >= NW:
                    sp.wait_ge(lo_ready, n - NW + 1)
                sp.dma_start(wraw[:, n % NW, :], w_in.rearrange("(p k) n -> p k n", k=KC)[:, k, half * WHALF:(half + 1) * WHALF]
                             ).then_inc(raw_loaded[n % NW], 16)

            load_bias(0)
            for g, (w, b, col, _, _, _) in enumerate(groups):
                for k in range(KC):
                    n = g * KC + k
                    if n >= NR:
                        sp.wait_ge(ring_used, n - NR + 1)
                    sp.dma_start(ring[:, n % NR, :], w.rearrange("(p k) n -> p k n", k=KC)[:, k, col:col + GW]
                                 ).then_inc(ring_loaded[n % NR], 16)
                    if g < 2:
                        load_w_in(n)
                sp.wait_ge(scaled, g + 1)
                sp.dma_start(mods[:, groups[g][3][0]:groups[g][3][1] + 1, :], row[:].rearrange("s (v d) -> s v d", v=2)
                             ).then_inc(rows_stored, 16)
                if g + 1 < len(groups):
                    load_bias(g + 1)
            sp.wait_ge(rows_stored, 16 * len(groups))

        @block.gpsimd
        def _(pool):
            pool.memset(ident[:], 0.0).then_inc(id_made, 1)
            pool.wait_ge(id_made, 1)
            pool.affine_select(out=ident[:], in_=ident[:], compare_op=ALU.not_equal, fill=1.0, base=0,
                               pattern=[[-1, 2]], channel_multiplier=1).then_inc(id_made, 1)

        @block.scalar
        def _(act):
            act.wait_ge(c_loaded, 16)
            act.activation(row[:, 0:D], c_sb[:], ACT.Silu).then_inc(silued, 1)
            for n in range(2 * KC):
                k, half = divmod(n, 2)
                act.wait_ge(raw_loaded[n % NW], 16 * (n // NW + 1))
                act.copy(w_hi[:, k, half * WHALF:(half + 1) * WHALF], wraw[:, n % NW, :]).then_inc(hi_ready, 1)

        @block.vector
        def _(dve):
            dve.wait_ge(cT_ready, 1)
            dve.tensor_copy(cT[:].rearrange("p k s -> p (k s)"), pc[:, 0:2 * KC]).then_inc(cT_copied, 1)

            def split_lo(n):
                k, half = divmod(n, 2)
                cols = slice(half * WHALF, (half + 1) * WHALF)
                dve.wait_ge(hi_ready, n + 1)
                dve.tensor_tensor(w_lo[:, k, cols], wraw[:, n % NW, :], w_hi[:, k, cols].bitcast(F32),
                                  ALU.subtract).then_inc(lo_ready, 1)

            for g in range(4):
                for n in range(8 * g, 8 * g + 8) if g < 2 else ():
                    split_lo(n)
                dve.wait_ge(ring_used, (g + 1) * KC)
                dve.wait_ge(bias_loaded, 32 * (g + 1))
                if g:
                    dve.wait_ge(rows_stored, 16 * g)
                dve.tensor_tensor(row[:], pm[:], brow[:], ALU.add).then_inc(row_ready, 1)
                dve.wait_ge(row_ready, g + 1)
                which = groups[g][4]
                half = row[:, (which or 0) * D:(which or 0) * D + D]
                if which is None:
                    dve.tensor_copy(half, half).then_inc(scaled, 1)
                else:
                    dve.scalar_tensor_tensor(out=half, in0=half, scalar=1.0, in1=grow[:], op0=ALU.add,
                                             op1=ALU.mult).then_inc(scaled, 1)

        @block.tensor
        def _(pe):
            pe.wait_ge(silued, 1)
            pe.wait_ge(id_made, 2)
            for k in range(KC):
                mm = pe.transpose(pc[:, 2 * k:2 * k + 2], row[:, k:D:KC], ident[:])
            mm.then_inc(cT_ready, 1)
            pe.wait_ge(cT_copied, 1)
            for g in range(4):
                for k in range(KC):
                    n = g * KC + k
                    pe.wait_ge(ring_loaded[n % NR], 16 * (n // NR + 1))
                    if g and k == 0:
                        pe.wait_ge(row_ready, g)
                    for j in range(GW // HALF):
                        mm = pe.matmul(pm[:, j * HALF:(j + 1) * HALF], cT[:, k, :], ring[:, n % NR, j * HALF:(j + 1) * HALF],
                                       start=(k == 0), stop=(k == KC - 1))
                    mm.then_inc(ring_used, 1)


def stage_projection(nc, w_hi, w_lo, x_all, mods, rope_tab, qn_g, kn_g, q_dram, k_dram, v_dram):
    with ExitStack() as ctx:
        m = Memory(nc, ctx, "prj")
        x = m.sb("x", [P, 2, D])
        rope = m.sb("rope", [P, 2, 160])
        h = m.sb("h", [P, D])
        hT_hi, hT_lo = m.sb("hT_hi", [P, 2, KC, P], F32R), m.sb("hT_lo", [P, 2, KC, P], F32R)
        stage = m.sb("stage", [P, IN_COLS])
        a1, sh1 = m.sb("a1", [P, D]), m.sb("sh1", [P, D])
        sq, t1 = m.sb("sq", [P, 512]), m.sb("t1", [P, 512])
        t1b = m.sb("t1b", [P, 128])
        gqk = m.sb("gqk", [P, 2, HD])
        ident = m.sb("ident", [P, P])
        ss, ms, rstd = m.sb("ss", [P, 2]), m.sb("ms", [P, 2]), m.sb("rstd", [P, 2])
        ss8, ms8, rs8 = m.sb("ss8", [P, 8]), m.sb("ms8", [P, 8]), m.sb("rs8", [P, 8])
        neghalf, eps = m.sb("neghalf", [P, 8]), m.sb("eps", [P, 8])
        tp = m.ps("tp", (P, D))
        pp = [m.ps(f"pp{n}") for n in range(5)]
        names = ("const_made", "mods_loaded", "ss_ready", "ms_ready", "rstd_ready", "h_mul", "h_ready", "tp_ready",
                 "hi_ready", "hT_ready", "reduced", "ms8_ready", "rs8_ready", "dve_own")
        (const_made, mods_loaded, ss_ready, ms_ready, rstd_ready, h_mul, h_ready, tp_ready, hi_ready, hT_ready, reduced,
         ms8_ready, rs8_ready, dve_own) = (m.sem(n) for n in names)
        x_loaded, rope_loaded = m.sems("x_loaded", 2), m.sems("rope_loaded", 2)
        proj_ready, copied, squared = m.sems("proj_ready", 5), m.sems("copied", 5), m.sems("squared", 5)
        staged, stored = m.sems("staged", 5), m.sems("stored", 5)
        block = ctx.enter_context(nc.Block())
        bank_read = copied[:3] + squared[3:]
        LOOPS, LAST = 3, NT - 1

        def tiles(eng, body, steps=None, per=None):
            with eng.Fori(0, LOOPS) as i:
                if steps:
                    steps.enter(i, per)
                for b in range(2):
                    body(2 * i + b, b, i, 0, False)
                if steps:
                    steps.leave(LOOPS)
            for t in range(2 * LOOPS, NT):
                body(t, t % 2, t // 2, int(t + 1 >= NT0), t == LAST)

        stores = [(q_dram, 0, 0, 512), (k_dram, 0, 512, 1024), (v_dram, 0, 1024, 1536), (q_dram, 512, 1536, 2048)]

        @block.sync
        def _(sp):
            def load_x(t, b):
                sp.dma_start(x[:, b, :], x_all[bass.ts(t, P), :]).then_inc(x_loaded[b], 16)

            def load_rope(t, b):
                sp.dma_start(rope[:, b, :], rope_tab[bass.ts(t, P), :]).then_inc(rope_loaded[b], 16)

            def load_mods(s):
                sp.dma_start(sh1[:], mods[s, 0, :].unsqueeze(0).to_broadcast([P, D])).then_inc(mods_loaded, 16)
                sp.dma_start(a1[:], mods[s, 1, :].unsqueeze(0).to_broadcast([P, D])).then_inc(mods_loaded, 16)

            load_x(0, 0)
            load_mods(0)
            load_x(1, 1)
            load_rope(0, 0)
            load_rope(1, 1)
            sp.dma_start(gqk[:, 0, :], qn_g[:].unsqueeze(0).to_broadcast([P, HD])).then_inc(mods_loaded, 16)
            sp.dma_start(gqk[:, 1, :], kn_g[:].unsqueeze(0).to_broadcast([P, HD])).then_inc(mods_loaded, 16)

            def body(t, b, u, s_next, last):
                peeled = isinstance(t, int)
                if not peeled or t + 2 < NT:
                    sp.wait_ge(h_ready, t + 1)
                    load_x(t + 2, b)
                if peeled and t == NT0 - 2:
                    sp.wait_ge(h_ready, NT0)
                    load_mods(1)
                for n, (dst, c, lo, hi) in enumerate(stores):
                    if n == 2:
                        sp.wait_ge(copied[n], t + 2)
                    else:
                        sp.wait_ge(staged[n], t + 1)
                    sp.dma_start(dst[bass.ts(t, P), c:c + hi - lo], stage[:, lo:hi]).then_inc(stored[n], 16)
                sp.wait_ge(staged[4], t + 2)
                sp.dma_start(k_dram[bass.ts(t, P), WA:WA + 128], stage[:, 2048:2176]).then_inc(stored[4], 16)
                sp.dma_start(v_dram[bass.ts(t, P), WA:WA + 128], stage[:, 2176:2304]).then_inc(stored[4], 16)
                if not peeled or t + 2 < NT:
                    load_rope(t + 2, b)

            tiles(sp, body)
            for n in range(4):
                sp.wait_ge(stored[n], 16 * (NT + 1))
            sp.wait_ge(stored[4], 32 * (NT + 1))

        @block.gpsimd
        def _(pool):
            pool.memset(neghalf[:], -0.5)
            pool.memset(eps[:], EPS)
            make_identity(nc, pool, ident, const_made)

            def rstd_of(t, b):
                pool.wait_ge(ss_ready, t + 1)
                pool.tensor_tensor(ms[:, b:b + 1], ss[:, b:b + 1], eps[:, 0:1], ALU.add).then_inc(ms_ready, 1)
                pool.wait_ge(ms_ready, t + 1)
                pool.tensor_tensor(rstd[:, b:b + 1], ms[:, b:b + 1], neghalf[:, 0:1], ALU.pow).then_inc(rstd_ready, 1)

            rstd_of(0, 0)

            def body(t, b, u, s_next, last):
                if not last:
                    rstd_of(t + 1, 1 - b)
                for j in range(2):
                    w = (8, NKVB)[j]
                    pool.wait_ge(reduced, 2 * t + j + 1)
                    pool.tensor_tensor(ms8[:, 0:w], ss8[:, 0:w], eps[:, 0:w], ALU.add).then_inc(ms8_ready, 1)
                    pool.wait_ge(ms8_ready, 2 * t + j + 1)
                    pool.tensor_tensor(rs8[:, 0:w], ms8[:, 0:w], neghalf[:, 0:w], ALU.pow).then_inc(rs8_ready, 1)

            tiles(pool, body)

        @block.scalar
        def _(act):
            def square(t, b, u):
                act.wait_ge(x_loaded[b], (u + 1) * 16)
                if not isinstance(t, int) or t:
                    act.wait_ge(tp_ready, t)
                act.activation(h[:], x[:, b, :], ACT.Square, scale=D ** -0.5, accum_out=ss[:, b:b + 1]).then_inc(ss_ready, 1)

            def split_hi(t, b):
                act.wait_ge(tp_ready, t + 1)
                act.copy(hT_hi[:, b].rearrange("p k t -> p (k t)")[:, 0:HALF], tp[:, 0:HALF])
                act.copy(hT_hi[:, b].rearrange("p k t -> p (k t)")[:, HALF:D], tp[:, HALF:D]).then_inc(hi_ready, 1)

            square(0, 0, 0)
            split_hi(0, 0)

            def body(t, b, u, s_next, last):
                if not last:
                    square(t + 1, 1 - b, u + b)
                for n, (lo, hi) in enumerate(BLOCKS):
                    act.wait_ge(proj_ready[n], t + 1)
                    act.wait_ge(stored[n], (t + 1) * (16 if n < 4 else 32))
                    act.copy(stage[:, lo:hi], pp[n][:, 0:hi - lo]).then_inc(copied[n], 1)
                    if n >= 3:
                        w = (512, 128)[n - 3]
                        act.wait_ge(staged[7 - n], t + 1)
                        act.activation(sq[:, 0:w], pp[n][:, 0:w], ACT.Square, scale=HD ** -0.5).then_inc(squared[n], 1)
                    if n == 2 and not last:
                        split_hi(t + 1, 1 - b)

            for n in range(5):
                act.sem_inc(stored[n], 16 if n < 4 else 32)
            act.sem_inc(staged[4], 1)
            tiles(act, body)

        @block.vector
        def _(dve):
            own = Steps(dve, dve_own)

            def make_h(t, b, u, s):
                dve.wait_ge(rstd_ready, t + 1)
                dve.wait_ge(mods_loaded, 64 + 32 * s)
                dve.scalar_tensor_tensor(out=h[:], in0=x[:, b, :], scalar=rstd[:, b:b + 1], in1=a1[:], op0=ALU.mult,
                                         op1=ALU.mult).then_inc(h_mul, 1)
                dve.wait_ge(h_mul, t + 1)
                dve.tensor_tensor(h[:], h[:], sh1[:], ALU.add).then_inc(h_ready, 1)

            def split_lo(t, b):
                dve.wait_ge(hi_ready, t + 1)
                dve.tensor_tensor(hT_lo[:, b].rearrange("p k t -> p (k t)"), tp[:],
                                  hT_hi[:, b].rearrange("p k t -> p (k t)").bitcast(F32), ALU.subtract).then_inc(hT_ready, 1)

            def rope_a(t, b, u, n):
                v = stage[:, BLOCKS[n][0]:BLOCKS[n][1]].rearrange("p (h d) -> p h d", d=HD)
                a, c = (z[:, 0:128].rearrange("p (h d) -> p h d", d=16) for z in (t1, t1b))
                cos = rope[:, b, 0:16].unsqueeze(1).to_broadcast([P, 8, 16])
                sin = rope[:, b, 16:32].unsqueeze(1).to_broadcast([P, 8, 16])
                dve.wait_ge(copied[n], t + 2)
                dve.wait_ge(staged[(4, 0)[n]], t + 1)
                dve.wait_ge(rope_loaded[b], (u + 1) * 16)
                dve.tensor_tensor(a, v[:, :, 0:16], cos, ALU.mult)
                dve.tensor_tensor(c[:, :, 0:8], v[:, :, 8:16], sin[:, :, 0:8], ALU.mult)
                own.did(dve.tensor_tensor(c[:, :, 8:16], v[:, :, 0:8], sin[:, :, 8:16], ALU.mult))
                own.wait()
                dve.tensor_tensor(v[:, :, 0:16], a, c, ALU.add).then_inc(staged[n], 1)

            def norm_b(t, b, u, n):
                j = n - 3
                H = (8, NKVB)[j]
                W = H * HD
                v = stage[:, BLOCKS[n][0]:BLOCKS[n][0] + W]
                v3 = v.rearrange("p (h d) -> p h d", d=HD)
                dve.wait_ge(squared[n], t + 2)
                dve.tensor_reduce(ss8[:, 0:H], sq[:, 0:W].rearrange("p (h d) -> p h d", d=HD), AX.X, ALU.add).then_inc(reduced, 1)
                dve.wait_ge(rs8_ready, 2 * t + j + 1)
                dve.wait_ge(staged[(1, 3)[j]], t + 1)
                own.did(dve.tensor_tensor(v3, v3, rs8[:, 0:H].unsqueeze(2).to_broadcast([P, H, HD]), ALU.mult))
                own.wait()
                own.did(dve.tensor_tensor(v3, v3, gqk[:, j, :].unsqueeze(1).to_broadcast([P, H, HD]), ALU.mult))
                own.wait()
                cos = rope[:, b, 32:96].unsqueeze(1).to_broadcast([P, H, HD])
                sin = rope[:, b, 96:160].rearrange("p (a c d) -> p a c d", a=2, c=2)
                v5 = v.rearrange("p (h a c d) -> p h a c d", a=2, c=2, d=16)
                s5 = sq[:, 0:W].rearrange("p (h a c d) -> p h a c d", a=2, c=2, d=16)
                dve.tensor_tensor(t1[:, 0:W].rearrange("p (h d) -> p h d", d=HD), v3, cos, ALU.mult)
                for c in range(2):
                    step = dve.tensor_tensor(s5[:, :, :, c, :], v5[:, :, :, 1 - c, :],
                                             sin[:, :, c, :].unsqueeze(1).to_broadcast([P, H, 2, 16]), ALU.mult)
                own.did(step)
                own.wait()
                dve.tensor_tensor(v, t1[:, 0:W], sq[:, 0:W], ALU.add).then_inc(staged[n], 1)

            make_h(0, 0, 0, 0)
            split_lo(0, 0)

            def body(t, b, u, s_next, last):
                if not last:
                    make_h(t + 1, 1 - b, u + b, s_next)
                rope_a(t, b, u, 0)
                rope_a(t, b, u, 1)
                if not last:
                    split_lo(t + 1, 1 - b)
                norm_b(t, b, u, 3)
                norm_b(t, b, u, 4)

            tiles(dve, body, own, 2 * 8)

        @block.tensor
        def _(pe):
            def transposes(t):
                pe.wait_ge(h_ready, t + 1)
                if not isinstance(t, int) or t:
                    pe.wait_ge(hT_ready, t)
                for k in range(KC):
                    mm = pe.transpose(tp[:, k * P:(k + 1) * P], h[:, k:D:KC], ident[:])
                mm.then_inc(tp_ready, 1)

            pe.wait_ge(const_made, 2)
            transposes(0)
            for n in range(5):
                pe.sem_inc(bank_read[n], 1)

            def body(t, b, u, s_next, last):
                pe.wait_ge(hT_ready, t + 1)
                for n, (lo, hi) in enumerate(BLOCKS):
                    pe.wait_ge(bank_read[n], t + 1)
                    for k in range(KC):
                        for a, w in ((hT_hi, w_hi), (hT_hi, w_lo), (hT_lo, w_hi)):
                            mm = pe.matmul(pp[n][:, 0:hi - lo], a[:, b, k, :], w[:, k, lo:hi],
                                           start=(k == 0 and w is w_hi and a is hT_hi),
                                           stop=(k == KC - 1 and a is hT_lo))
                    mm.then_inc(proj_ready[n], 1)
                    if n == 2 and not last:
                        transposes(t + 1)

            tiles(pe, body)


def stage_keys(nc, kT, v_sb, k_dram, v_dram):
    with ExitStack() as ctx:
        m = Memory(nc, ctx, "key")
        KW = NKH * HD
        raw = m.sb("raw", [P, 2, KW])
        parts = m.sb("parts", [P, 2, NKH, 2, HD], F32R)
        ident_f, ident = m.sb("ident_f", [P, P]), m.sb("ident", [P, P], F32R)
        tp = [m.ps(f"tp{i}", (P, 512)) for i in range(3)]
        HEADS = [(0, 4), (4, 8), (8, 10)]
        id_made, id_ready, hi_ready, lo_ready, v_loaded = (m.sem(n) for n in ("id_made", "id_ready", "hi_ready", "lo_ready", "v_loaded"))
        raw_loaded, tp_ready, kept = m.sems("raw_loaded", 2), m.sems("tp_ready", 3), m.sems("kept", 3)
        block = ctx.enter_context(nc.Block())

        @block.sync
        def _(sp):
            def load(t, b):
                sp.dma_start(raw[:, b, :], k_dram[bass.ts(t, P), :]).then_inc(raw_loaded[b], 16)

            load(0, 0)
            load(1, 1)
            sp.dma_start(v_sb[:], v_dram.rearrange("(t p) n -> p t n", p=P)).then_inc(v_loaded, 16)
            with sp.Fori(0, NT // 2 - 1) as i:
                for b in range(2):
                    sp.wait_ge(lo_ready, 2 * i + b + 1)
                    load(2 * i + b + 2, b)
            sp.wait_ge(v_loaded, 16)

        @block.gpsimd
        def _(pool):
            make_identity(nc, pool, ident_f, id_made)

        @block.scalar
        def _(act):
            with act.Fori(0, NT // 2) as i:
                for b in range(2):
                    t = 2 * i + b
                    act.wait_ge(raw_loaded[b], (i + 1) * 16)
                    act.copy(parts[:, b, :, 0, :], raw[:, b, :].rearrange("p (h d) -> p h d", d=HD)).then_inc(hi_ready, 1)
                    for n in (0, 2):
                        h0, h1 = HEADS[n]
                        act.wait_ge(tp_ready[n], t + 1)
                        act.copy(kT[:, h0:h1, bass.ds(t * P, P)],
                                 tp[n][:, 0:(h1 - h0) * P].rearrange("p (h t) -> p h t", t=P)).then_inc(kept[n], 1)

        @block.vector
        def _(dve):
            dve.wait_ge(id_made, 2)
            dve.tensor_copy(ident[:], ident_f[:]).then_inc(id_ready, 1)
            with dve.Fori(0, NT // 2) as i:
                for b in range(2):
                    t = 2 * i + b
                    dve.wait_ge(hi_ready, t + 1)
                    dve.tensor_tensor(parts[:, b, :, 1, :], raw[:, b, :].rearrange("p (h d) -> p h d", d=HD),
                                      parts[:, b, :, 0, :].bitcast(F32), ALU.subtract).then_inc(lo_ready, 1)
                    dve.wait_ge(tp_ready[1], t + 1)
                    dve.tensor_copy(kT[:, 4:8, bass.ds(t * P, P)],
                                    tp[1][:].rearrange("p (h t) -> p h t", t=P)).then_inc(kept[1], 1)

        @block.tensor
        def _(pe):
            pe.wait_ge(id_ready, 1)
            for n in range(3):
                pe.sem_inc(kept[n], 1)
            with pe.Fori(0, NT // 2) as i:
                for b in range(2):
                    t = 2 * i + b
                    pe.wait_ge(lo_ready, t + 1)
                    for n, (h0, h1) in enumerate(HEADS):
                        pe.wait_ge(kept[n], t + 1)
                        for h in range(h0, h1):
                            mm = pe.transpose(tp[n][:, (h - h0) * P:(h - h0 + 1) * P].bitcast(F32R),
                                              parts[:, b, h].rearrange("p a d -> p (a d)"), ident[:])
                        mm.then_inc(tp_ready[n], 1)


def stage_attention(nc, kT, v_sb, q_dram, count_tab, o_dram, y_dram):
    NH = NHA + NHB
    with ExitStack() as ctx:
        m = Memory(nc, ctx, "att")
        q = m.sb("q", [P, 2, NH * HD])
        parts = m.sb("parts", [P, NH, 2, 2, HD], F32R)
        qT = m.sb("qT", [P, 2, NH, 2, P], F32R)
        counts = m.sb("counts", [P, 2, S0])
        s = m.sb("s", [P, 2, S0])
        prob = m.sb("prob", [P, 2, S0])
        pT = m.sb("pT", [P, 2, 2, 4, P])
        o = m.sb("o", [P, 2, WA])
        osq = m.sb("osq", [P, WA])
        zero, zeros = m.sb("zero", [P, 1]), m.sb("zeros", [P, D])
        neg_max = m.sb("neg_max", [P, 2])
        den, rden = m.sb("den", [P, NH]), m.sb("rden", [P, NH])
        sso, mso, rso = m.sb("sso", [P, 2]), m.sb("mso", [P, 2]), m.sb("rso", [P, 2])
        neghalf, eps = m.sb("neghalf", [P, 1]), m.sb("eps", [P, 1])
        ident_f, ident = m.sb("ident_f", [P, P]), m.sb("ident", [P, P], F32R)
        sc = [m.ps(f"sc{i}", (P, S0)) for i in range(2)]
        tp = [m.ps(f"tp{i}") for i in range(2)]
        op, qp = m.ps("op"), m.ps("qp")
        names = ("id_made", "id_ready", "consts", "hi_ready", "parts_ready", "qT_kept", "qp_ready", "scores_ready",
                 "masked", "exped", "pv_ready", "o_read", "rden_ready", "sso_ready", "mso_ready", "rso_ready", "normed", "mask_begun", "load_begun",
                 "zeros_made", "zeros_stored")
        (id_made, id_ready, consts, hi_ready, parts_ready, qT_kept, qp_ready, scores_ready, masked, exped, pv_ready,
         o_read, rden_ready, sso_ready, mso_ready, rso_ready, normed, mask_begun, load_begun,
         zeros_made, zeros_stored) = (m.sem(n) for n in names)
        q_loaded, counts_loaded = m.sems("q_loaded", 2), m.sems("counts_loaded", 2)
        tp_ready, pT_kept, stored = m.sems("tp_ready", 2), m.sems("pT_kept", 2), m.sems("stored", 2)
        block = ctx.enter_context(nc.Block())
        LOOPS = 3

        def keys(t):
            return (0, S0, 0) if not isinstance(t, int) or t < NT0 else (S0, S1, NT0)

        def tiles(eng, body):
            with eng.Fori(0, LOOPS) as i:
                for b in range(2):
                    body(2 * i + b, b, i, 2 * i + b + 1)
            for t in range(2 * LOOPS, NT):
                body(t, t % 2, t // 2, t + 1 if t + 1 < NT else None)

        def ahead(t, nxt, j, n):
            if j + n < NH:
                return t, j + n
            return None if nxt is None else (nxt, j + n - NH)

        @block.sync
        def _(sp):
            def load_q(t, b):
                sp.dma_start(q[:, b, :], q_dram[bass.ts(t, P), :]).then_inc(q_loaded[b], 16)

            def load_counts(t, b):
                _, S, v0 = keys(t)
                sp.dma_start(counts[:, b, 0:S], count_tab[:, bass.ds(S0 - P - (t - v0) * P, S)]).then_inc(counts_loaded[b], 16)

            load_q(0, 0)
            load_counts(0, 0)
            load_q(1, 1)
            load_counts(1, 1)
            sp.wait_ge(zeros_made, 1)
            sp.dma_start(y_dram[NE * P:NBLK * P, :].rearrange("(b p) d -> p b d", p=P), zeros[:].unsqueeze(1).to_broadcast([P, NOV, D])
                         ).then_inc(zeros_stored, 16)

            def body(t, b, u, nxt):
                more = not isinstance(t, int) or t + 2 < NT
                if more:
                    sp.wait_ge(masked, NH * t + NHA)
                    sp.sem_inc(load_begun, 1)
                    sp.wait_ge(parts_ready, t + 1)
                    sp.sem_inc(load_begun, 1)
                    load_q(t + 2, b)
                    load_counts(t + 2, b)
                for g in range(2):
                    sp.wait_ge(normed, 2 * t + g + 1)
                    sp.dma_start(o_dram[bass.ts(t, P), g * WA:(g + 1) * WA], o[:, g, :]).then_inc(stored[g], 16)

            tiles(sp, body)
            for g in range(2):
                sp.wait_ge(stored[g], 16 * (NT + 1))
            sp.wait_ge(zeros_stored, 16)

        @block.gpsimd
        def _(pool):
            make_identity(nc, pool, ident_f, id_made)
            pool.memset(zeros[:], 0.0).then_inc(zeros_made, 1)
            pool.memset(zero[:], 0.0).then_inc(consts, 1)
            pool.memset(neghalf[:], -0.5).then_inc(consts, 1)
            pool.memset(eps[:], EPS).then_inc(consts, 1)
            pool.wait_ge(consts, 3)

            def body(t, b, u, nxt):
                for g in range(2):
                    n = 2 * t + g + 1
                    pool.wait_ge(sso_ready, n)
                    pool.tensor_tensor(mso[:, g:g + 1], sso[:, g:g + 1], eps[:], ALU.add).then_inc(mso_ready, 1)
                    pool.wait_ge(mso_ready, n)
                    pool.tensor_tensor(rso[:, g:g + 1], mso[:, g:g + 1], neghalf[:], ALU.pow).then_inc(rso_ready, 1)

            tiles(pool, body)

        @block.scalar
        def _(act):
            def split_hi(t, b, u):
                act.wait_ge(q_loaded[b], (u + 1) * 16)
                if not isinstance(t, int) or t:
                    act.wait_ge(qp_ready, t * (NH // 2))
                v = q[:, b, :].rearrange("p (h d) -> p h d", d=HD)
                for c in range(2):
                    mm = act.copy(parts[:, :, 0, c, :], v)
                mm.then_inc(hi_ready, 1)

            def keep_qT(t, b, pair):
                act.wait_ge(qp_ready, t * (NH // 2) + pair + 1)
                act.copy(qT[:, b, 2 * pair:2 * pair + 2].rearrange("p h c t -> p (h c t)"), qp[:]).then_inc(qT_kept, 1)

            def exp(t, j):
                n, S = NH * t + j + 1, keys(t)[1]
                act.wait_ge(masked, n)
                act.wait_ge(tp_ready[1], n)
                act.activation(prob[:, j % 2, 0:S], s[:, j % 2, 0:S], ACT.Exp, bias=neg_max[:, j % 2:j % 2 + 1], scale=-1.0,
                               accum_out=den[:, j:j + 1]).then_inc(exped, 1)

            def keep_pT(t, j):
                c = keys(t)[1] // (2 * P)
                act.wait_ge(tp_ready[1], NH * t + j + 3)
                act.copy(pT[:, j % 2, 1, 0:c].rearrange("p c t -> p (c t)"), tp[1][:, 0:c * P]).then_inc(pT_kept[1], 1)

            def square(t, g):
                act.wait_ge(o_read, 2 * t + g + 2)
                act.activation(osq[:], o[:, g, :], ACT.Square, scale=WA ** -0.5, accum_out=sso[:, g:g + 1]).then_inc(sso_ready, 1)

            act.sem_inc(tp_ready[1], 2)
            for g in range(2):
                act.sem_inc(stored[g], 16)
            split_hi(0, 0, 0)
            for pair in range(NH // 2):
                keep_qT(0, 0, pair)
            exp(0, 0)

            def body(t, b, u, nxt):
                for j in range(NH):
                    if j == 0 and nxt is not None:
                        split_hi(t + 1, 1 - b, u + b)
                    nx = ahead(t, nxt, j, 1)
                    if nx:
                        exp(*nx)
                    keep_pT(t, j)
                    if j % 2 and nxt is not None:
                        keep_qT(t + 1, 1 - b, j // 2)
                    if j == 9:
                        square(t, 0)
                square(t, 1)

            tiles(act, body)

        @block.vector
        def _(dve):
            dve.wait_ge(id_made, 2)
            dve.tensor_copy(ident[:], ident_f[:]).then_inc(id_ready, 1)
            dve.sem_inc(exped, 2)
            dve.wait_ge(consts, 3)

            def split_lo(t, b):
                dve.wait_ge(hi_ready, t + 1)
                v = q[:, b, :].rearrange("p (h d) -> p h d", d=HD)
                for c in range(2):
                    step = dve.tensor_tensor(parts[:, :, 1, c, :], v, parts[:, :, 0, c, :].bitcast(F32), ALU.subtract)
                step.then_inc(parts_ready, 1)

            def mask(t, b, u, j):
                n, S = NH * t + j + 1, keys(t)[1]
                if j == 0:
                    dve.wait_ge(counts_loaded[b], (u + 1) * 16)
                dve.wait_ge(scores_ready, n)
                dve.wait_ge(exped, n)
                dve.sem_inc(mask_begun, 1)
                held = counts[:, b, 0:S] if j < NHA else zero[:].to_broadcast([P, S])
                dve.tensor_tensor_reduce(s[:, j % 2, 0:S], sc[j % 2][:, 0:S], held, -SCALE, 3e38, ALU.add, ALU.min,
                                         neg_max[:, j % 2:j % 2 + 1]).then_inc(masked, 1)

            def keep_pT(t, j):
                c = keys(t)[1] // (2 * P)
                dve.wait_ge(tp_ready[0], NH * t + j + 1)
                dve.tensor_copy(pT[:, j % 2, 0, 0:c].rearrange("p c t -> p (c t)"), tp[0][:, 0:c * P]).then_inc(pT_kept[0], 1)

            def take_o(t, g):
                heads = slice(g * NHA, (g + 1) * NHA)
                n = 2 * t + g + 1
                dve.wait_ge(pv_ready, n)
                dve.reciprocal(rden[:, heads], den[:, heads]).then_inc(rden_ready, 1)
                dve.wait_ge(rden_ready, n)
                dve.wait_ge(stored[g], (t + 1) * 16)
                dve.tensor_tensor(o[:, g, :].rearrange("p (h d) -> p h d", d=HD), op[:].rearrange("p (h d) -> p h d", d=HD),
                                  rden[:, heads].unsqueeze(2).to_broadcast([P, NHA, HD]), ALU.mult).then_inc(o_read, 1)

            def norm_o(t, g):
                dve.wait_ge(rso_ready, 2 * t + g + 1)
                dve.tensor_scalar(o[:, g, :], o[:, g, :], rso[:, g:g + 1], None, ALU.mult).then_inc(normed, 1)

            split_lo(0, 0)
            mask(0, 0, 0, 0)
            mask(0, 0, 0, 1)

            def body(t, b, u, nxt):
                for j in range(NH):
                    if j == 0 and nxt is not None:
                        split_lo(t + 1, 1 - b)
                    nx = ahead(t, nxt, j, 2)
                    if nx:
                        if j + 2 < NH:
                            mask(t, b, u, j + 2)
                        else:
                            mask(t + 1, 1 - b, u + b, j + 2 - NH)
                    keep_pT(t, j)
                    if j == 8:
                        take_o(t, 0)
                    if j == 11:
                        norm_o(t, 0)
                take_o(t, 1)
                norm_o(t, 1)

            tiles(dve, body)

        @block.tensor
        def _(pe):
            def q_transposes(t, pair):
                if pair == 0:
                    pe.wait_ge(parts_ready, t + 1)
                n = t * (NH // 2) + pair
                if not isinstance(n, int) or n:
                    pe.wait_ge(qT_kept, n)
                for h in (0, 1):
                    for c in (0, 1):
                        mm = pe.transpose(qp[:, (2 * h + c) * P:(2 * h + c + 1) * P].bitcast(F32R),
                                          parts[:, 2 * pair + h, c].rearrange("p a d -> p (a d)"), ident[:])
                mm.then_inc(qp_ready, 1)

            def scores(t, b, j):
                k0, S, _ = keys(t)
                kh = j if j < NHA else NHA + (j - NHA) // (NHB // NKVB)
                pe.wait_ge(qT_kept, t * (NH // 2) + j // 2 + 1)
                n = NH * t + j - 1
                if not isinstance(n, int) or n > 0:
                    pe.wait_ge(masked, n)
                for c in range(0, S, HALF):
                    w = min(HALF, S - c)
                    for part in (0, 1):
                        mm = pe.matmul(sc[j % 2][:, c:c + w], qT[:, b, j, part, :], kT[:, kh, k0 + c:k0 + c + w],
                                       start=(part == 0), stop=(part == 1))
                mm.then_inc(scores_ready, 1)

            def p_transposes(t, j):
                c = keys(t)[1] // (2 * P)
                pe.wait_ge(exped, NH * t + j + 3)
                for half in (0, 1):
                    pe.wait_ge(pT_kept[half], NH * t + j + 1)
                    for i in range(c):
                        mm = pe.transpose(tp[half][:, i * P:(i + 1) * P], prob[:, j % 2, (half * c + i) * P:(half * c + i + 1) * P],
                                          ident_f[:])
                    mm.then_inc(tp_ready[half], 1)

            def values(t, j):
                _, S, v0 = keys(t)
                c = S // (2 * P)
                h = j % NHA
                col = j * HD if j < NHA else WA + (j - NHA) // (NHB // NKVB) * HD
                if h == 0:
                    pe.wait_ge(o_read, 2 * t + j // NHA + 1)
                for half in (0, 1):
                    pe.wait_ge(pT_kept[half], NH * t + j + 2)
                    for i in range(c):
                        mm = pe.matmul(op[:, h * HD:(h + 1) * HD], pT[:, j % 2, half, i, :],
                                       v_sb[:, v0 + half * c + i, col:col + HD],
                                       start=(half == 0 and i == 0), stop=(half == 1 and i == c - 1))
                if h == NHA - 1:
                    mm.then_inc(pv_ready, 1)

            pe.wait_ge(id_ready, 1)
            pe.sem_inc(pT_kept[0], 1)
            pe.sem_inc(pT_kept[1], 1)
            pe.sem_inc(o_read, 1)
            for pair in range(NH // 2):
                q_transposes(0, pair)
            scores(0, 0, 0)
            scores(0, 0, 1)

            def body(t, b, u, nxt):
                for j in range(NH):
                    nx = ahead(t, nxt, j, 2)
                    if nx:
                        scores(nx[0], b if j + 2 < NH else 1 - b, nx[1])
                    p_transposes(t, j)
                    if j % 2 and nxt is not None:
                        q_transposes(t + 1, j // 2)
                    if j:
                        values(t, j - 1)
                values(t, NH - 1)

            tiles(pe, body)


def stage_output(nc, logits, o_dram, x_all, mods, w_out, on_a_g, on_b_g, w_rg, b_rg, w_re, b_re, x1_dram, h2_dram):
    NL = NG + NE
    with ExitStack() as ctx:
        m = Memory(nc, ctx, "out")
        w_hi, w_lo = m.sb("w_hi", [P, KC, D], F32R), m.sb("w_lo", [P, KC, D], F32R)
        wraw = m.sb("wraw", [P, 2, D])
        gain = m.sb("gain", [P, KC])
        w_r, b_r = m.sb("w_r", [P, KC, NL]), m.sb("b_r", [P, NL])
        o, x = m.sb("o", [P, 2, D]), m.sb("x", [P, 2, D])
        oT_hi, oT_lo = m.sb("oT_hi", [P, 2, KC, P], F32R), m.sb("oT_lo", [P, 2, KC, P], F32R)
        g1, a2, sh2 = m.sb("g1", [P, D]), m.sb("a2", [P, D]), m.sb("sh2", [P, D])
        x1, h2 = m.sb("x1", [P, D]), m.sb("h2", [P, D])
        sq, h2T = m.sb("sq", [P, D]), m.sb("h2T", [P, KC, P])
        ss, ms, rstd = m.sb("ss", [P, 1]), m.sb("ms", [P, 1]), m.sb("rstd", [P, 1])
        neghalf, eps = m.sb("neghalf", [P, 1]), m.sb("eps", [P, 1])
        ident = m.sb("ident", [P, P])
        tp, tp2 = m.ps("tp", (P, D)), m.ps("tp2", (P, D))
        yp = [m.ps(f"yp{i}") for i in range(2)]
        lp = m.ps("lp")
        names = ("id_made", "consts", "w_consts", "hi_ready", "lo_ready", "mods_loaded", "tp_ready", "oT_hi_ready", "oT_ready",
                 "gated", "x1_ready", "ss_ready", "ms_ready", "rstd_ready", "h2_mul", "h2_ready", "tp2_ready", "h2T_ready",
                 "logits_ready", "logits_kept", "x1_stored", "h2_stored")
        (id_made, consts, w_consts, hi_ready, lo_ready, mods_loaded, tp_ready, oT_hi_ready, oT_ready, gated, x1_ready, ss_ready,
         ms_ready, rstd_ready, h2_mul, h2_ready, tp2_ready, h2T_ready, logits_ready, logits_kept, x1_stored, h2_stored
         ) = (m.sem(n) for n in names)
        raw_loaded, o_loaded, x_loaded = m.sems("raw_loaded", 2), m.sems("o_loaded", 2), m.sems("x_loaded", 2)
        yp_ready = m.sems("yp_ready", 2)
        block = ctx.enter_context(nc.Block())
        LOOPS = 3

        def tiles(eng, body):
            body(0, 0, 0, 0)
            with eng.Fori(0, LOOPS) as i:
                body(2 * i + 1, 1, i, 0)
                body(2 * i + 2, 0, i + 1, 0)
            for t in range(2 * LOOPS + 1, NT):
                body(t, t % 2, t // 2, int(t >= NT0))

        def is_last(t):
            return isinstance(t, int) and t == NT - 1

        @block.sync
        def _(sp):
            def load(t, b):
                sp.dma_start(o[:, b, :], o_dram[bass.ts(t, P), :]).then_inc(o_loaded[b], 16)
                sp.dma_start(x[:, b, :], x_all[bass.ts(t, P), :]).then_inc(x_loaded[b], 16)

            def load_mods(s):
                for dst, v in ((g1, 2), (sh2, 3), (a2, 4)):
                    sp.dma_start(dst[:], mods[s, v, :].unsqueeze(0).to_broadcast([P, D])).then_inc(mods_loaded, 16)

            half = P // 2
            sp.dma_start(gain[0:half, :], on_a_g.rearrange("(p k) -> p k", k=KC)).then_inc(w_consts, 16)
            sp.dma_start(gain[half:P, :], on_b_g.rearrange("(p k) -> p k", k=KC)).then_inc(w_consts, 16)
            load(0, 0)
            for k in range(KC):
                if k >= 2:
                    sp.wait_ge(lo_ready, k - 1)
                sp.dma_start(wraw[:, k % 2, :], w_out.rearrange("(p k) n -> p k n", k=KC)[:, k, :]).then_inc(raw_loaded[k % 2], 16)
            load_mods(0)
            load(1, 1)
            sp.dma_start(w_r[:, :, 0:NG], w_rg.rearrange("(p k) n -> p k n", k=KC)).then_inc(w_consts, 16)
            sp.dma_start(w_r[:, :, NG:NL], w_re.rearrange("(p k) n -> p k n", k=KC)).then_inc(w_consts, 16)
            sp.dma_start(b_r[:, 0:NG], b_rg.unsqueeze(0).to_broadcast([P, NG])).then_inc(w_consts, 16)
            sp.dma_start(b_r[:, NG:NL], b_re.unsqueeze(0).to_broadcast([P, NE])).then_inc(w_consts, 16)

            def body(t, b, u, s):
                sp.wait_ge(x1_ready, t + 1)
                sp.dma_start(x1_dram[bass.ts(t, P), :], x1[:]).then_inc(x1_stored, 16)
                if not isinstance(t, int) or t + 2 < NT:
                    load(t + 2, b)
                sp.wait_ge(h2_ready, t + 1)
                sp.dma_start(h2_dram[bass.ts(t, P), :], h2[:]).then_inc(h2_stored, 16)
                if isinstance(t, int) and t == NT0 - 1:
                    load_mods(1)

            tiles(sp, body)
            sp.wait_ge(x1_stored, 16 * (NT + 1))
            sp.wait_ge(h2_stored, 16 * (NT + 1))

        @block.gpsimd
        def _(pool):
            make_identity(nc, pool, ident, id_made)
            pool.memset(neghalf[:], -0.5).then_inc(consts, 1)
            pool.memset(eps[:], EPS).then_inc(consts, 1)
            pool.wait_ge(consts, 2)

            def body(t, b, u, s):
                pool.wait_ge(ss_ready, t + 1)
                pool.tensor_tensor(ms[:], ss[:], eps[:], ALU.add).then_inc(ms_ready, 1)
                pool.wait_ge(ms_ready, t + 1)
                pool.tensor_tensor(rstd[:], ms[:], neghalf[:], ALU.pow).then_inc(rstd_ready, 1)

            tiles(pool, body)

        @block.scalar
        def _(act):
            act.wait_ge(w_consts, 32)
            for k in range(KC):
                act.wait_ge(raw_loaded[k % 2], 16 * (k // 2 + 1))
                act.activation(w_hi[:, k, :], wraw[:, k % 2, :], ACT.Copy, scale=gain[:, k:k + 1]).then_inc(hi_ready, 1)
            act.sem_inc(x1_stored, 16)
            act.sem_inc(h2_stored, 16)

            def split_hi(t, b):
                act.wait_ge(tp_ready, t + 1)
                for c in (0, HALF):
                    step = act.copy(oT_hi[:, b].rearrange("p k t -> p (k t)")[:, c:c + HALF], tp[:, c:c + HALF])
                step.then_inc(oT_hi_ready, 1)

            def keep_h2T(t):
                act.wait_ge(tp2_ready, t + 1)
                for c in (0, HALF):
                    step = act.copy(h2T[:].rearrange("p k t -> p (k t)")[:, c:c + HALF], tp2[:, c:c + HALF])
                step.then_inc(h2T_ready, 1)

            split_hi(0, 0)

            def body(t, b, u, s):
                if not is_last(t):
                    split_hi(t + 1, 1 - b)
                if not isinstance(t, int) or t:
                    keep_h2T(t - 1)
                act.wait_ge(x1_ready, t + 1)
                act.activation(sq[:], x1[:], ACT.Square, scale=D ** -0.5, accum_out=ss[:]).then_inc(ss_ready, 1)

            tiles(act, body)
            keep_h2T(NT - 1)

        @block.vector
        def _(dve):
            for k in range(KC):
                dve.wait_ge(hi_ready, k + 1)
                dve.scalar_tensor_tensor(out=w_lo[:, k, :], in0=wraw[:, k % 2, :], scalar=gain[:, k:k + 1],
                                         in1=w_hi[:, k, :].bitcast(F32), op0=ALU.mult, op1=ALU.subtract).then_inc(lo_ready, 1)
            dve.sem_inc(logits_kept, 1)

            def split_lo(t, b):
                dve.wait_ge(oT_hi_ready, t + 1)
                dve.tensor_tensor(oT_lo[:, b].rearrange("p k t -> p (k t)"), tp[:],
                                  oT_hi[:, b].rearrange("p k t -> p (k t)").bitcast(F32), ALU.subtract).then_inc(oT_ready, 1)

            def keep_logits(t):
                dve.wait_ge(logits_ready, t + 1)
                dve.tensor_tensor(logits[:, bass.ds(t, 1), :], lp[:, 0:NL].unsqueeze(1), b_r[:].unsqueeze(1), ALU.add
                                  ).then_inc(logits_kept, 1)

            dve.wait_ge(w_consts, 96)
            split_lo(0, 0)

            def body(t, b, u, s):
                n = t + 1
                if not isinstance(t, int) or t:
                    dve.wait_ge(ss_ready, t)
                dve.wait_ge(x1_stored, 16 * n)
                dve.wait_ge(mods_loaded, 48 * (s + 1))
                for c in range(2):
                    dve.wait_ge(yp_ready[c], n)
                    dve.tensor_tensor(x1[:, c * HALF:(c + 1) * HALF], yp[c][:], g1[:, c * HALF:(c + 1) * HALF], ALU.mult
                                      ).then_inc(gated, 1)
                    if c == 0 and not is_last(t):
                        split_lo(t + 1, 1 - b)
                dve.wait_ge(x_loaded[b], (u + 1) * 16)
                dve.wait_ge(gated, 2 * n)
                dve.tensor_tensor(x1[:], x1[:], x[:, b, :], ALU.add).then_inc(x1_ready, 1)
                if not isinstance(t, int) or t:
                    keep_logits(t - 1)
                    dve.wait_ge(tp2_ready, t)
                dve.wait_ge(rstd_ready, n)
                dve.wait_ge(h2_stored, 16 * n)
                dve.scalar_tensor_tensor(out=h2[:], in0=x1[:], scalar=rstd[:], in1=a2[:], op0=ALU.mult, op1=ALU.mult
                                         ).then_inc(h2_mul, 1)
                dve.wait_ge(h2_mul, n)
                dve.tensor_tensor(h2[:], h2[:], sh2[:], ALU.add).then_inc(h2_ready, 1)

            tiles(dve, body)
            keep_logits(NT - 1)

        @block.tensor
        def _(pe):
            def transposes(t, b, u):
                pe.wait_ge(o_loaded[b], (u + 1) * 16)
                if not isinstance(t, int) or t:
                    pe.wait_ge(oT_ready, t)
                for k in range(KC):
                    mm = pe.transpose(tp[:, k * P:(k + 1) * P], o[:, b, k:D:KC], ident[:])
                mm.then_inc(tp_ready, 1)

            def router(t):
                pe.wait_ge(h2_ready, t + 1)
                if not isinstance(t, int) or t:
                    pe.wait_ge(h2T_ready, t)
                for k in range(KC):
                    mm = pe.transpose(tp2[:, k * P:(k + 1) * P], h2[:, k:D:KC], ident[:])
                mm.then_inc(tp2_ready, 1)
                pe.wait_ge(logits_kept, t + 1)
                pe.wait_ge(h2T_ready, t + 1)
                for k in range(KC):
                    mm = pe.matmul(lp[:, 0:NL], h2T[:, k, :], w_r[:, k, :], start=(k == 0), stop=(k == KC - 1))
                mm.then_inc(logits_ready, 1)

            pe.wait_ge(id_made, 2)
            transposes(0, 0, 0)
            pe.wait_ge(w_consts, 96)
            pe.wait_ge(lo_ready, KC)

            def body(t, b, u, s):
                pe.wait_ge(oT_ready, t + 1)
                for c in range(2):
                    if not isinstance(t, int) or t:
                        pe.wait_ge(gated, 2 * t - 1 + c)
                    for k in range(KC):
                        for a, w in ((oT_hi, w_hi), (oT_hi, w_lo), (oT_lo, w_hi)):
                            mm = pe.matmul(yp[c][:], a[:, b, k, :], w[:, k, c * HALF:(c + 1) * HALF],
                                           start=(k == 0 and w is w_hi and a is oT_hi), stop=(k == KC - 1 and a is oT_lo))
                    mm.then_inc(yp_ready[c], 1)
                    if c == 0 and not is_last(t):
                        transposes(t + 1, 1 - b, u + b)
                if not isinstance(t, int) or t:
                    router(t - 1)

            tiles(pe, body)
            router(NT - 1)


def stage_route(nc, logits, gates, slots, tokens, overflow, slot_tok):
    NCH = 2
    THR = T // P - 1
    with ExitStack() as ctx:
        m = Memory(nc, ctx, "rt")
        rev4, rev8 = m.sb("rev4", [P, NG]), m.sb("rev8", [P, EPG])
        iota_e, iota_b, thr = m.sb("iota_e", [P, NE]), m.sb("iota_b", [P, NOV]), m.sb("thr", [P, THR])
        tok = m.sb("tok", [P, NT])
        upper, ones = m.sb("upper", [P, P], BF16), m.sb("ones", [P, P], BF16)
        ident = m.sb("ident", [P, P])
        blank = m.sb("blank", [NBLK, P])
        back = m.sb("back", [NBLK, P])
        t4, goh = m.sb("t4", [P, NT, NG]), m.sb("goh", [P, NT, NG])
        v1, v2, v3 = (m.sb(n, [P, NT]) for n in ("v1", "v2", "v3"))
        gsum = m.sb("gsum", [P, NT])
        es, k8, oh = m.sb("es", [P, NT, EPG]), m.sb("k8", [P, NT, EPG]), m.sb("oh", [P, NCH, NT, EPG])
        top = m.sb("top", [P, NCH, NT])
        full = m.sb("full", [P, NCH, NT, NE])
        prod = m.sb("prod", [P, NT, NE])
        sel = m.sb("sel", [P, NT, NE], BF16)
        before = m.sb("before", [P, NT + 1, NE], BF16)
        pos = m.sb("pos", [P, NT + 1, NE])
        over = m.sb("over", [P, NE, THR])
        nblk, inc, adj = m.sb("nblk", [P, NE]), m.sb("inc", [P, 2, NE]), m.sb("adj", [P, NE])
        cmp = m.sb("cmp", [P, NOV, NE])
        ov = m.sb("ov", [P, NOV + 1])
        slot = m.sb("slot", [P, NCH, NT])
        pp = m.ps("pp", (P, (NT + 1) * NE))
        tp = m.ps("tp")
        own_sem, consts, subbed, exped, d_ready, e_ready, sel_ready, pos_ready, slots_ready, blanked, back_ready, back_t = (
            m.sem(n) for n in ("own", "consts", "subbed", "exped", "d_ready", "e_ready", "sel_ready", "pos_ready", "slots_ready",
                               "blanked", "back_ready", "back_t"))
        scattered = m.sem("scattered")
        block = ctx.enter_context(nc.Block())

        @block.gpsimd
        def _(pool):
            steps = Steps(pool, consts)
            steps.did(pool.iota(rev4[:], [[-1, NG]], base=NG, channel_multiplier=0, allow_small_or_imprecise_dtypes=True))
            steps.did(pool.iota(rev8[:], [[-1, EPG]], base=EPG, channel_multiplier=0, allow_small_or_imprecise_dtypes=True))
            steps.did(pool.iota(iota_e[:], [[1, NE]], base=0, channel_multiplier=0, allow_small_or_imprecise_dtypes=True))
            steps.did(pool.iota(iota_b[:], [[1, NOV]], base=0, channel_multiplier=0, allow_small_or_imprecise_dtypes=True))
            steps.did(pool.iota(thr[:], [[P, THR]], base=P, channel_multiplier=0, allow_small_or_imprecise_dtypes=True))
            steps.did(pool.iota(tok[:], [[P, NT]], base=0, channel_multiplier=1, allow_small_or_imprecise_dtypes=True))
            steps.did(pool.memset(ones[:], 1.0))
            steps.did(pool.memset(upper[:], 1.0))
            steps.did(pool.memset(ident[:], 0.0))
            steps.did(pool.memset(blank[:], 0.0))
            steps.wait()
            steps.did(pool.affine_select(out=upper[:], in_=upper[:], compare_op=ALU.is_gt, fill=0.0, base=0,
                                         pattern=[[1, P]], channel_multiplier=-1))
            steps.did(pool.affine_select(out=ident[:], in_=ident[:], compare_op=ALU.not_equal, fill=1.0, base=0,
                                         pattern=[[-1, P]], channel_multiplier=1))
            assert steps.n == 12
            pool.wait_ge(blanked, 16)
            pool.wait_ge(slots_ready, 1)
            for i in range(NCH):
                for t in range(NT):
                    pool.indirect_dma_start(slot_tok, bass.IndirectOffsetOnAxis(ap=slots[:, i, t:t + 1], axis=0),
                                            tok[:, t:t + 1], None).then_inc(scattered, 16)

        @block.sync
        def _(sp):
            sp.wait_ge(consts, 12)
            sp.dma_start(slot_tok.rearrange("(b p) a -> b (p a)", p=P), blank[:]).then_inc(blanked, 16)
            sp.wait_ge(scattered, 16 * NCH * NT)
            sp.dma_start(back[:], slot_tok.rearrange("(b p) a -> b (p a)", p=P)).then_inc(back_ready, 16)
            sp.wait_ge(back_ready, 16)

        @block.scalar
        def _(act):
            act.wait_ge(subbed, 1)
            act.activation(t4[:], t4[:], ACT.Exp).then_inc(exped, 1)
            act.wait_ge(d_ready, 1)
            act.activation(v2[:], v2[:], ACT.Exp).then_inc(e_ready, 1)

        @block.vector
        def _(dve):
            own = Steps(dve, own_sem)

            def do(ins):
                own.did(ins)
                own.wait()

            def first_max(out_onehot, values, best, key, rev, width):
                wide = lambda z: z.unsqueeze(2).to_broadcast([P, NT, width])
                do(dve.tensor_reduce(best, values, AX.X, ALU.max))
                do(dve.tensor_tensor(key, values, wide(best), ALU.is_equal))
                do(dve.tensor_tensor(key, key, rev.unsqueeze(1).to_broadcast([P, NT, width]), ALU.mult))
                do(dve.tensor_reduce(v3[:], key, AX.X, ALU.max))
                do(dve.tensor_tensor(out_onehot, key, wide(v3[:]), ALU.is_equal))

            dve.wait_ge(consts, 12)
            gl = logits[:, :, 0:NG]
            el = logits[:, :, NG:NG + NE].rearrange("p t (g e) -> p t g e", g=NG)
            first_max(goh[:], gl, v1[:], t4[:], rev4[:], NG)
            dve.tensor_tensor(t4[:], gl, v1[:].unsqueeze(2).to_broadcast([P, NT, NG]), ALU.subtract).then_inc(subbed, 1)
            p4 = prod[:].rearrange("p t (g e) -> p t g e", g=NG)
            do(dve.tensor_tensor(p4, el, goh[:].unsqueeze(3).to_broadcast([P, NT, NG, EPG]), ALU.mult))
            do(dve.tensor_reduce(es[:], prod[:].rearrange("p t (g e) -> p t e g", g=NG), AX.X, ALU.add))
            first_max(oh[:, 0], es[:], top[:, 0], k8[:], rev8[:], EPG)
            do(dve.scalar_tensor_tensor(out=es[:], in0=oh[:, 0], scalar=-1e30, in1=es[:], op0=ALU.mult, op1=ALU.add))
            first_max(oh[:, 1], es[:], top[:, 1], k8[:], rev8[:], EPG)
            dve.tensor_tensor(v2[:], top[:, 1], top[:, 0], ALU.subtract).then_inc(d_ready, 1)
            dve.wait_ge(exped, 1)
            do(dve.tensor_reduce(gsum[:], t4[:], AX.X, ALU.add))
            dve.wait_ge(e_ready, 1)
            do(dve.tensor_scalar(v3[:], v2[:], 1.0, None, ALU.add))
            do(dve.tensor_tensor(v3[:], v3[:], gsum[:], ALU.mult))
            do(dve.reciprocal(gates[:, 0], v3[:]))
            do(dve.tensor_tensor(gates[:, 1], gates[:, 0], v2[:], ALU.mult))
            for i in range(NCH):
                f4 = full[:, i].rearrange("p t (g e) -> p t g e", g=NG)
                do(dve.tensor_tensor(f4, goh[:].unsqueeze(3).to_broadcast([P, NT, NG, EPG]),
                                     oh[:, i].unsqueeze(2).to_broadcast([P, NT, NG, EPG]), ALU.mult))
            do(dve.tensor_tensor(sel[:], full[:, 0], full[:, 1], ALU.add))
            do(dve.memset(before[:, 0, :], 0.0))
            for t in range(NT):
                step = dve.tensor_tensor(before[:, t + 1, :], before[:, t, :], sel[:, t, :], ALU.add)
                if t < NT - 1:
                    do(step)
            step.then_inc(sel_ready, 1)
            dve.wait_ge(pos_ready, 1)
            do(dve.tensor_copy(pos[:].rearrange("p t e -> p (t e)"), pp[:]))
            count = pos[:, NT, :]
            do(dve.tensor_tensor(over[:], count.unsqueeze(2).to_broadcast([P, NE, THR]),
                                 thr[:].unsqueeze(1).to_broadcast([P, NE, THR]), ALU.is_gt))
            do(dve.tensor_reduce(nblk[:], over[:], AX.X, ALU.add))
            do(dve.tensor_copy(inc[:, 0, :], nblk[:]))
            shift, cur = 1, 0
            while shift < NE:
                dve.tensor_tensor(inc[:, 1 - cur, shift:NE], inc[:, cur, shift:NE], inc[:, cur, 0:NE - shift], ALU.add)
                do(dve.tensor_copy(inc[:, 1 - cur, 0:shift], inc[:, cur, 0:shift]))
                shift, cur = 2 * shift, 1 - cur
            do(dve.tensor_tensor(adj[:], inc[:, cur, :], nblk[:], ALU.subtract))
            do(dve.tensor_tensor(adj[:], adj[:], iota_e[:], ALU.subtract))
            do(dve.tensor_scalar(adj[:], adj[:], float(NE - 1), float(P), ALU.add, ALU.mult))

            def of_choice(out, table):
                do(dve.tensor_tensor(prod[:], full[:, i], table, ALU.mult))
                do(dve.tensor_reduce(out, prod[:], AX.X, ALU.add))

            for i in range(NCH):
                of_choice(v1[:], pos[:, 0:NT, :])
                of_choice(v2[:], iota_e[:].unsqueeze(1).to_broadcast([P, NT, NE]))
                of_choice(v3[:], adj[:].unsqueeze(1).to_broadcast([P, NT, NE]))
                do(dve.scalar_tensor_tensor(out=v3[:], in0=v1[:], scalar=float(P), in1=v3[:], op0=ALU.is_ge, op1=ALU.mult))
                do(dve.scalar_tensor_tensor(out=v1[:], in0=v2[:], scalar=float(P), in1=v1[:], op0=ALU.mult, op1=ALU.add))
                do(dve.tensor_tensor(slot[:, i], v1[:], v3[:], ALU.add))
            dve.tensor_copy(slots[:], slot[:]).then_inc(slots_ready, 1)
            do(dve.tensor_tensor(cmp[:], inc[:, cur, :].unsqueeze(1).to_broadcast([P, NOV, NE]),
                                 iota_b[:].unsqueeze(2).to_broadcast([P, NOV, NE]), ALU.is_le))
            do(dve.tensor_reduce(ov[:, 0:NOV], cmp[:], AX.X, ALU.add))
            do(dve.tensor_scalar(ov[:, 0:NOV], ov[:, 0:NOV], float(NE - 1), None, ALU.min))
            do(dve.tensor_copy(ov[:, NOV:NOV + 1], inc[:, cur, NE - 1:NE]))
            do(dve.tensor_copy(overflow[:], ov[0:1, :]))
            dve.wait_ge(back_t, 1)
            dve.tensor_copy(tokens[:], tp[:, 0:NBLK])

        @block.tensor
        def _(pe):
            pe.wait_ge(consts, 12)
            pe.wait_ge(sel_ready, 1)
            pe.matmul(pp[:], ones[:], before[:].rearrange("p t e -> p (t e)"), start=True, stop=False, skip_group_check=True)
            pe.matmul(pp[:, 0:NT * NE], upper[:], sel[:].rearrange("p t e -> p (t e)"), start=False, stop=True,
                      skip_group_check=True).then_inc(pos_ready, 1)
            pe.wait_ge(back_ready, 16)
            pe.transpose(tp[:, 0:NBLK], back[:], ident[0:NBLK, 0:NBLK]).then_inc(back_t, 1)


def stage_experts(nc, tokens, h2_dram, w1, w3, w2, y_dram):
    FC = FE // P
    CH, NRAW, NSPL = D, 12, 6
    with ExitStack() as ctx:
        m = Memory(nc, ctx, "exp")
        raw = m.sb("raw", [P, NRAW, CH])
        w_hi, w_lo = m.sb("w_hi", [P, NSPL, CH], F32R), m.sb("w_lo", [P, NSPL, CH], F32R)
        rows = m.sb("rows", [P, 2], I32)
        xg = m.sb("xg", [P, 2, D])
        xT_hi, xT_lo = m.sb("xT_hi", [P, 2, KC, P], F32R), m.sb("xT_lo", [P, 2, KC, P], F32R)
        u, hm = m.sb("u", [P, FE]), m.sb("hm", [P, FE])
        hT_hi, hT_lo = m.sb("hT_hi", [P, FC, P], F32R), m.sb("hT_lo", [P, FC, P], F32R)
        y = m.sb("y", [P, D])
        ident = m.sb("ident", [P, P])
        pa, pb, thp = m.ps("pa"), m.ps("pb"), m.ps("thp")
        py, txp = m.ps("py", (P, D)), m.ps("txp", (P, D))
        names = ("id_made", "rows_ready", "carried", "hi_done", "lo_done", "used", "tx_ready", "xT_hi_ready", "xT_ready",
                 "silued", "hm_ready", "th_ready", "hT_hi_ready", "hT_ready", "y_kept", "y_stored")
        (id_made, rows_ready, carried, hi_done, lo_done, used, tx_ready, xT_hi_ready, xT_ready,
         silued, hm_ready, th_ready, hT_hi_ready, hT_ready, y_kept, y_stored) = (m.sem(n) for n in names)
        raw_loaded, x_loaded = m.sems("raw_loaded", NRAW), m.sems("x_loaded", 2)
        block = ctx.enter_context(nc.Block())
        LOOPS = (NE - 4) // 2

        def experts(eng, body, tail=None):
            body(0, 0, 0)
            body(1, 1, 0)
            with eng.Fori(0, LOOPS) as i:
                body(2 * i + 2, 0, i + 1)
                body(2 * i + 3, 1, i + 1)
            body(NE - 2, 0, NE // 2 - 1)
            body(NE - 1, 1, NE // 2 - 1)
            if tail:
                tail()

        def first(e):
            return isinstance(e, int) and e == 0

        def more(e, n):
            return not isinstance(e, int) or e + n < NE

        def number(e, c):
            if isinstance(e, int) and e in (0, NE):
                return (c if c < 4 else c - 4) + (12 * NE - 4 if e else 0)
            return 12 * e + c - 4

        def place(e, c, size):
            if isinstance(e, int):
                return number(e, c) % size, number(e, c) // size
            return (c + 8) % size, (12 // size) * (e - 1) + (c + 8) // size

        def chunks(e):
            if isinstance(e, int) and e == NE:
                return range(4, 8)
            return [c for c in range(12) if not (first(e) and 4 <= c < 8)]

        @block.sync
        def _(sp):
            def body(e, b=None, turn=None):
                for c in chunks(e):
                    n = number(e, c)
                    slot, _ = place(e, c, NRAW)
                    if not isinstance(n, int) or n >= NRAW:
                        sp.wait_ge(lo_done, n - NRAW + 1)
                        sp.sem_inc(carried, 1)
                    j = c % 4
                    if 4 <= c < 8:
                        src = w2[bass.ds(e - 1, 1)].rearrange("e (p k) n -> (e p) k n", k=FC)[:, j:j + 1, :]
                    else:
                        src = (w1 if c < 4 else w3)[bass.ds(e, 1)].rearrange("e (p k) n -> (e p) k n", k=KC)[:, 2 * j:2 * j + 2, :]
                    sp.dma_start(raw[:, slot, :], src.rearrange("p k n -> p (k n)")).then_inc(raw_loaded[slot], 16)

            experts(sp, body, lambda: body(NE))

        @block.gpsimd
        def _(pool):
            make_identity(nc, pool, ident, id_made)

            def gather(e, b):
                pool.tensor_copy(rows[:, b:b + 1], tokens[:, bass.ds(e, 1)]).then_inc(rows_ready, 1)
                pool.wait_ge(rows_ready, e + 1)
                pool.sem_inc(carried, 1)
                pool.indirect_dma_start(xg[:, b, :], None, h2_dram, bass.IndirectOffsetOnAxis(ap=rows[:, b:b + 1], axis=0)
                                        ).then_inc(x_loaded[b], 16)

            gather(0, 0)
            gather(1, 1)

            def body(e, b, turn):
                if more(e, 2):
                    pool.wait_ge(tx_ready, e + 1)
                    pool.sem_inc(carried, 1)
                    gather(e + 2, b)

            experts(pool, body)

        @block.scalar
        def _(act):
            act.sem_inc(y_stored, 16)

            def split_hi(e, c):
                n = number(e, c)
                (slot, turn), (to, _) = place(e, c, NRAW), place(e, c, NSPL)
                act.wait_ge(raw_loaded[slot], 16 * (turn + 1))
                if not isinstance(n, int) or n >= NSPL:
                    act.wait_ge(used, n - NSPL + 1)
                act.copy(w_hi[:, to, :], raw[:, slot, :]).then_inc(hi_done, 1)

            def split_xT(e, b):
                act.wait_ge(tx_ready, e + 1)
                act.copy(xT_hi[:, b].rearrange("p k t -> p (k t)"), txp[:]).then_inc(xT_hi_ready, 1)

            def split_hT(e):
                act.wait_ge(th_ready, e + 1)
                act.copy(hT_hi[:].rearrange("p k t -> p (k t)"), thp[:]).then_inc(hT_hi_ready, 1)

            def silu(e):
                act.wait_ge(used, number(e, 3) + 1)
                if not first(e):
                    act.wait_ge(hm_ready, e)
                act.activation(u[:], pa[:], ACT.Silu).then_inc(silued, 1)

            def keep_y(e):
                act.wait_ge(used, number(e + 1, 7) + 1)
                act.wait_ge(y_stored, 16 * (e + 1))
                act.copy(y[:], py[:]).then_inc(y_kept, 1)
                act.wait_ge(y_kept, e + 2)
                act.sem_inc(carried, 1)
                act.dma_start(y_dram[bass.ts(e, P), :], y[:]).then_inc(y_stored, 16)

            split_xT(0, 0)

            def body(e, b, turn):
                for c in chunks(e):
                    split_hi(e, c)
                    if c == 0 and not (isinstance(e, int) and e < 2):
                        keep_y(e - 2)
                    if c == 5:
                        split_hT(e - 1)
                    if c == 8:
                        if more(e, 1):
                            split_xT(e + 1, 1 - b)
                        silu(e)

            def tail():
                for c in chunks(NE):
                    split_hi(NE, c)
                    if c == 4:
                        keep_y(NE - 2)
                    if c == 5:
                        split_hT(NE - 1)
                keep_y(NE - 1)
                act.wait_ge(y_stored, 16 * (NE + 1))

            experts(act, body, tail)

        @block.vector
        def _(dve):
            def split_lo(e, c):
                (slot, _), (to, _) = place(e, c, NRAW), place(e, c, NSPL)
                dve.wait_ge(hi_done, number(e, c) + 1)
                dve.tensor_tensor(w_lo[:, to, :], raw[:, slot, :], w_hi[:, to, :].bitcast(F32), ALU.subtract).then_inc(lo_done, 1)

            def split_xT(e, b):
                dve.wait_ge(xT_hi_ready, e + 1)
                dve.tensor_tensor(xT_lo[:, b].rearrange("p k t -> p (k t)"), txp[:],
                                  xT_hi[:, b].rearrange("p k t -> p (k t)").bitcast(F32), ALU.subtract).then_inc(xT_ready, 1)

            def split_hT(e):
                dve.wait_ge(hT_hi_ready, e + 1)
                dve.tensor_tensor(hT_lo[:].rearrange("p k t -> p (k t)"), thp[:],
                                  hT_hi[:].rearrange("p k t -> p (k t)").bitcast(F32), ALU.subtract).then_inc(hT_ready, 1)

            def gate_up(e):
                dve.wait_ge(used, number(e, 11) + 1)
                dve.wait_ge(silued, e + 1)
                if not first(e):
                    dve.wait_ge(th_ready, e)
                dve.tensor_tensor(hm[:], u[:], pb[:], ALU.mult).then_inc(hm_ready, 1)

            dve.sem_inc(y_kept, 1)
            split_xT(0, 0)

            def body(e, b, turn):
                for c in chunks(e):
                    split_lo(e, c)
                    if c == 2 and not first(e):
                        gate_up(e - 1)
                    if c == 5:
                        split_hT(e - 1)
                    if c == 8 and more(e, 1):
                        split_xT(e + 1, 1 - b)

            def tail():
                gate_up(NE - 1)
                for c in chunks(NE):
                    split_lo(NE, c)
                    if c == 5:
                        split_hT(NE - 1)

            experts(dve, body, tail)

        @block.tensor
        def _(pe):
            def tx(e, b, turn):
                pe.wait_ge(x_loaded[b], 16 * (turn + 1))
                if not first(e):
                    pe.wait_ge(xT_ready, e)
                for k in range(KC):
                    mm = pe.transpose(txp[:, k * P:(k + 1) * P], xg[:, b, k:D:KC], ident[:])
                mm.then_inc(tx_ready, 1)

            def th(e):
                pe.wait_ge(hm_ready, e + 1)
                for k in range(FC):
                    mm = pe.transpose(thp[:, k * P:(k + 1) * P], hm[:, k:FE:FC], ident[:])
                mm.then_inc(th_ready, 1)

            def up(e, b, c, out):
                to, _ = place(e, c, NSPL)
                pe.wait_ge(lo_done, number(e, c) + 1)
                for r in range(2):
                    k = 2 * (c % 4) + r
                    for a, w in ((xT_hi, w_hi), (xT_hi, w_lo), (xT_lo, w_hi)):
                        mm = pe.matmul(out[:], a[:, b, k, :], w[:, to, r * FE:(r + 1) * FE],
                                       start=(k == 0 and w is w_hi and a is xT_hi), stop=(k == KC - 1 and a is xT_lo))
                mm.then_inc(used, 1)

            def down(e, c):
                to, _ = place(e, c, NSPL)
                k = c % 4
                pe.wait_ge(lo_done, number(e, c) + 1)
                for a, w in ((hT_hi, w_hi), (hT_hi, w_lo), (hT_lo, w_hi)):
                    for half in range(2):
                        mm = pe.matmul(py[:, half * HALF:(half + 1) * HALF], a[:, k, :], w[:, to, half * HALF:(half + 1) * HALF],
                                       start=(k == 0 and w is w_hi and a is hT_hi), stop=(k == FC - 1 and a is hT_lo))
                mm.then_inc(used, 1)

            def before_down(e):
                pe.wait_ge(hT_ready, e)
                pe.wait_ge(y_kept, e)

            pe.wait_ge(id_made, 2)
            tx(0, 0, 0)

            def body(e, b, turn):
                pe.wait_ge(xT_ready, e + 1)
                if not first(e):
                    pe.wait_ge(silued, e)
                for c in chunks(e):
                    if c == 4:
                        before_down(e)
                    if c == 8 and not first(e):
                        pe.wait_ge(hm_ready, e)
                    if 4 <= c < 8:
                        down(e, c)
                    else:
                        up(e, b, c, pa if c < 4 else pb)
                    if c == 1 and not first(e):
                        th(e - 1)
                    if c == 3 and more(e, 1):
                        tx(e + 1, 1 - b, turn + b)

            def tail():
                th(NE - 1)
                before_down(NE)
                for c in chunks(NE):
                    down(NE, c)

            experts(pe, body, tail)


def stage_overflow(nc, tokens, overflow, h2_dram, w1, w3, w2, y_dram):
    FC = FE // P
    with ExitStack() as ctx:
        m = Memory(nc, ctx, "ovf")
        w1_sb, w3_sb, w2_sb = m.sb("w1", [P, KC, FE]), m.sb("w3", [P, KC, FE]), m.sb("w2", [P, FC, D])
        rows = m.sb("rows", [P, 1], I32)
        xg, xT = m.sb("xg", [P, D]), m.sb("xT", [P, KC, P])
        u, hm, hT, y = m.sb("u", [P, FE]), m.sb("hm", [P, FE]), m.sb("hT", [P, FC, P]), m.sb("y", [P, D])
        ident = m.sb("ident", [P, P])
        pa, pb, thp = m.ps("pa"), m.ps("pb"), m.ps("thp")
        py, txp = m.ps("py", (P, D)), m.ps("txp", (P, D))
        names = ("id_made", "w_loaded", "rows_ready", "x_loaded", "tx_ready", "xT_ready", "ab_ready", "silued", "hm_ready",
                 "th_ready", "hT_ready", "y_ready", "y_kept", "y_stored", "carried")
        (id_made, w_loaded, rows_ready, x_loaded, tx_ready, xT_ready, ab_ready, silued, hm_ready, th_ready, hT_ready, y_ready,
         y_kept, y_stored, carried) = (m.sem(n) for n in names)
        block = ctx.enter_context(nc.Block())

        def blocks(eng, body):
            number = eng.value_load(overflow[0:1, NOV:NOV + 1], min_val=0, max_val=NOV)
            with eng.If(number > 0):
                with eng.Fori(0, NOV) as j:
                    with eng.If(j < number):
                        body(j)

        @block.sync
        def _(sp):
            sp.sem_inc(y_stored, 16)

            def body(j):
                sp.wait_ge(y_stored, 16 * (j + 1))
                sp.sem_inc(carried, 1)
                e = sp.value_load(overflow[0:1, bass.ds(j, 1)], min_val=0, max_val=NE - 1)
                for dst, w, k in ((w1_sb, w1, KC), (w3_sb, w3, KC), (w2_sb, w2, FC)):
                    sp.dma_start(dst[:].rearrange("p k n -> p (k n)"),
                                 w[bass.ds(e, 1)].rearrange("e (p k) n -> (e p) (k n)", k=k)).then_inc(w_loaded, 16)
                sp.wait_ge(y_kept, j + 1)
                sp.sem_inc(carried, 1)
                sp.dma_start(y_dram[bass.ts(NE + j, P), :], y[:]).then_inc(y_stored, 16)
                sp.wait_ge(y_stored, 16 * (j + 2))
                sp.sem_inc(carried, 1)

            blocks(sp, body)

        @block.gpsimd
        def _(pool):
            make_identity(nc, pool, ident, id_made)

            def body(j):
                pool.wait_ge(y_stored, 16 * (j + 1))
                pool.sem_inc(carried, 1)
                pool.tensor_copy(rows[:], tokens[:, bass.ds(NE + j, 1)]).then_inc(rows_ready, 1)
                pool.wait_ge(rows_ready, j + 1)
                pool.sem_inc(carried, 1)
                pool.indirect_dma_start(xg[:], None, h2_dram, bass.IndirectOffsetOnAxis(ap=rows[:], axis=0)
                                        ).then_inc(x_loaded, 16)

            blocks(pool, body)

        @block.scalar
        def _(act):
            def body(j):
                act.wait_ge(ab_ready, 2 * j + 1)
                act.activation(u[:], pa[:], ACT.Silu).then_inc(silued, 1)
                act.wait_ge(y_ready, j + 1)
                act.copy(y[:], py[:]).then_inc(y_kept, 1)

            blocks(act, body)

        @block.vector
        def _(dve):
            def body(j):
                dve.wait_ge(tx_ready, j + 1)
                dve.tensor_copy(xT[:].rearrange("p k t -> p (k t)"), txp[:]).then_inc(xT_ready, 1)
                dve.wait_ge(ab_ready, 2 * j + 2)
                dve.wait_ge(silued, j + 1)
                dve.tensor_tensor(hm[:], u[:], pb[:], ALU.mult).then_inc(hm_ready, 1)
                dve.wait_ge(th_ready, j + 1)
                dve.tensor_copy(hT[:].rearrange("p k t -> p (k t)"), thp[:]).then_inc(hT_ready, 1)

            blocks(dve, body)

        @block.tensor
        def _(pe):
            pe.wait_ge(id_made, 2)

            def body(j):
                pe.wait_ge(x_loaded, 16 * (j + 1))
                for k in range(KC):
                    mm = pe.transpose(txp[:, k * P:(k + 1) * P], xg[:, k:D:KC], ident[:])
                mm.then_inc(tx_ready, 1)
                pe.wait_ge(xT_ready, j + 1)
                pe.wait_ge(w_loaded, 48 * (j + 1))
                for out, w in ((pa, w1_sb), (pb, w3_sb)):
                    for k in range(KC):
                        mm = pe.matmul(out[:], xT[:, k, :], w[:, k, :], start=(k == 0), stop=(k == KC - 1))
                    mm.then_inc(ab_ready, 1)
                pe.wait_ge(hm_ready, j + 1)
                for k in range(FC):
                    mm = pe.transpose(thp[:, k * P:(k + 1) * P], hm[:, k:FE:FC], ident[:])
                mm.then_inc(th_ready, 1)
                pe.wait_ge(hT_ready, j + 1)
                for half in range(2):
                    for k in range(FC):
                        mm = pe.matmul(py[:, half * HALF:(half + 1) * HALF], hT[:, k, :],
                                       w2_sb[:, k, half * HALF:(half + 1) * HALF], start=(k == 0), stop=(k == FC - 1))
                mm.then_inc(y_ready, 1)

            blocks(pe, body)


def stage_combine(nc, gates, slots, x1_dram, y_dram, mods, out):
    with ExitStack() as ctx:
        m = Memory(nc, ctx, "fin")
        g2, shf, af = m.sb("g2", [P, 2, D]), m.sb("shf", [P, 2, D]), m.sb("af", [P, 2, D])
        x1 = m.sb("x1", [P, 2, D])
        ya, yb = m.sb("ya", [P, 2, D]), m.sb("yb", [P, 2, D])
        ys, sq, res = m.sb("ys", [P, 2, D]), m.sb("sq", [P, D]), m.sb("res", [P, 2, D])
        ss, ms, rstd = m.sb("ss", [P, 1]), m.sb("ms", [P, 1]), m.sb("rstd", [P, 1])
        neghalf, eps = m.sb("neghalf", [P, 1]), m.sb("eps", [P, 1])
        rows = m.sb("rows", [P, 2, 2], I32)
        names = ("consts", "mods_loaded", "rows_ready", "weighed", "summed", "gated", "x2_ready", "ss_ready", "ms_ready",
                 "rstd_ready", "scaled", "res_ready", "carried")
        (consts, mods_loaded, rows_ready, weighed, summed, gated, x2_ready, ss_ready, ms_ready, rstd_ready, scaled, res_ready,
         carried) = (m.sem(n) for n in names)
        ya_loaded, yb_loaded, x1_loaded, stored = (m.sems(n, 2) for n in ("ya_loaded", "yb_loaded", "x1_loaded", "stored"))
        block = ctx.enter_context(nc.Block())
        LOOPS = 3

        def tiles(eng, body):
            body(0, 0, 0, 0)
            body(1, 1, 0, 0)
            with eng.Fori(0, LOOPS) as i:
                body(2 * i + 2, 0, i + 1, 0)
                body(2 * i + 3, 1, i + 1, 0)
            body(8, 0, 4, 1)
            body(9, 1, 4, 1)

        def early(t):
            return isinstance(t, int) and t < 2

        @block.sync
        def _(sp):
            def load_x1(t, b):
                sp.dma_start(x1[:, b, :], x1_dram[bass.ts(t, P), :]).then_inc(x1_loaded[b], 16)

            load_x1(0, 0)
            load_x1(1, 1)
            for s in range(2):
                for dst, v in ((g2, 5), (shf, 6), (af, 7)):
                    sp.dma_start(dst[:, s, :], mods[s, v, :].unsqueeze(0).to_broadcast([P, D])).then_inc(mods_loaded, 16)

            def body(t, b, u, s):
                if not isinstance(t, int) or t + 2 < NT:
                    sp.wait_ge(x2_ready, t + 1)
                    sp.sem_inc(carried, 1)
                    load_x1(t + 2, b)
                sp.wait_ge(res_ready, t + 1)
                sp.sem_inc(carried, 1)
                sp.dma_start(out[bass.ts(t, P), :], res[:, b, :]).then_inc(stored[b], 16)

            tiles(sp, body)
            for b in range(2):
                sp.wait_ge(stored[b], 16 * (NT // 2))

        @block.gpsimd
        def _(pool):
            pool.memset(neghalf[:], -0.5).then_inc(consts, 1)
            pool.memset(eps[:], EPS).then_inc(consts, 1)
            pool.wait_ge(consts, 2)

            def gather(t, b):
                pool.tensor_copy(rows[:, b, :].unsqueeze(2), slots[:, :, bass.ds(t, 1)]).then_inc(rows_ready, 1)
                pool.wait_ge(rows_ready, t + 1)
                pool.sem_inc(carried, 1)
                for i, (dst, loaded) in enumerate(((ya, ya_loaded), (yb, yb_loaded))):
                    pool.indirect_dma_start(dst[:, b, :], None, y_dram, bass.IndirectOffsetOnAxis(ap=rows[:, b, i:i + 1], axis=0)
                                            ).then_inc(loaded[b], 16)

            gather(0, 0)
            gather(1, 1)

            def body(t, b, u, s):
                if not isinstance(t, int) or t + 2 < NT:
                    pool.wait_ge(summed, t + 1)
                    pool.sem_inc(carried, 1)
                    gather(t + 2, b)
                pool.wait_ge(ss_ready, t + 1)
                pool.tensor_tensor(ms[:], ss[:], eps[:], ALU.add).then_inc(ms_ready, 1)
                pool.wait_ge(ms_ready, t + 1)
                pool.tensor_tensor(rstd[:], ms[:], neghalf[:], ALU.pow).then_inc(rstd_ready, 1)

            tiles(pool, body)

        @block.scalar
        def _(act):
            def weigh(t, b, u):
                act.wait_ge(ya_loaded[b], (u + 1) * 16)
                if not early(t):
                    act.wait_ge(scaled, t - 1)
                act.sem_inc(carried, 1)
                act.activation(ys[:, b, :], ya[:, b, :], ACT.Copy, scale=gates[:, 0, bass.ds(t, 1)]).then_inc(weighed, 1)

            weigh(0, 0, 0)

            def body(t, b, u, s):
                if not isinstance(t, int) or t + 1 < NT:
                    weigh(t + 1, 1 - b, u + b)
                act.wait_ge(x2_ready, t + 1)
                act.activation(sq[:], ys[:, b, :], ACT.Square, scale=D ** -0.5, accum_out=ss[:]).then_inc(ss_ready, 1)

            tiles(act, body)

        @block.vector
        def _(dve):
            dve.wait_ge(mods_loaded, 96)

            def body(t, b, u, s):
                n = t + 1
                v = ys[:, b, :]
                dve.wait_ge(yb_loaded[b], (u + 1) * 16)
                dve.wait_ge(weighed, n)
                dve.scalar_tensor_tensor(out=v, in0=yb[:, b, :], scalar=gates[:, 1, bass.ds(t, 1)], in1=v, op0=ALU.mult, op1=ALU.add
                                         ).then_inc(summed, 1)
                dve.wait_ge(summed, n)
                dve.tensor_tensor(v, v, g2[:, s, :], ALU.mult).then_inc(gated, 1)
                dve.wait_ge(gated, n)
                dve.wait_ge(x1_loaded[b], (u + 1) * 16)
                dve.tensor_tensor(v, v, x1[:, b, :], ALU.add).then_inc(x2_ready, 1)
                dve.wait_ge(rstd_ready, n)
                if not early(t):
                    dve.wait_ge(stored[b], u * 16)
                dve.scalar_tensor_tensor(out=res[:, b, :], in0=v, scalar=rstd[:], in1=af[:, s, :], op0=ALU.mult, op1=ALU.mult
                                         ).then_inc(scaled, 1)
                dve.wait_ge(scaled, n)
                dve.tensor_tensor(res[:, b, :], res[:, b, :], shf[:, s, :], ALU.add).then_inc(res_ready, 1)

            tiles(dve, body)


def hybrid_encoder_kernel(nc, x_all, c_all, ln1_g, ln2_g, w_ada, b_ada, w_in, w_out, qn_g, kn_g, on_a_g, on_b_g,
                          w_rg, b_rg, w_re, b_re, w1, w3, w2, lnf_g, w_adaf, b_adaf, rope_tab, count_tab, out):
    def scratch(name, shape):
        return nc.dram_tensor(name, shape, F32, kind="Internal").ap()

    mods = scratch("mods", (2, 8, D))
    q, k, v = scratch("q", (T, WA + NHB * HD)), scratch("k", (T, NKH * HD)), scratch("v", (T, NKH * HD))
    o, x1, h2 = scratch("o", (T, D)), scratch("x1", (T, D)), scratch("h2", (T, D))
    slot_tok, y = scratch("slot_tok", (NBLK * P, 1)), scratch("y", (NBLK * P, D))
    with ExitStack() as ctx:
        m = Memory(nc, ctx, "in")
        w_hi, w_lo = m.sb("w_hi", [P, KC, IN_COLS], F32R), m.sb("w_lo", [P, KC, IN_COLS], F32R)
        stage_modulation(nc, w_hi, w_lo, c_all, w_ada, b_ada, w_adaf, b_adaf, ln1_g, ln2_g, lnf_g, w_in, mods)
        stage_projection(nc, w_hi, w_lo, x_all, mods, rope_tab, qn_g, kn_g, q, k, v)
    with ExitStack() as ctx:
        m = Memory(nc, ctx, "kv")
        kT, v_sb = m.sb("kT", [P, NKH, T], F32R), m.sb("v", [P, NT, NKH * HD])
        stage_keys(nc, kT, v_sb, k, v)
        stage_attention(nc, kT, v_sb, q, count_tab, o, y)
    with ExitStack() as ctx:
        m = Memory(nc, ctx, "route")
        logits, gates = m.sb("logits", [P, NT, NG + NE]), m.sb("gates", [P, 2, NT])
        slots, tokens = m.sb("slots", [P, 2, NT], I32), m.sb("tokens", [P, NBLK], I32)
        overflow = m.sb("overflow", [1, NOV + 1], I32)
        stage_output(nc, logits, o, x_all, mods, w_out, on_a_g, on_b_g, w_rg, b_rg, w_re, b_re, x1, h2)
        stage_route(nc, logits, gates, slots, tokens, overflow, slot_tok)
        stage_experts(nc, tokens, h2, w1, w3, w2, y)
        stage_overflow(nc, tokens, overflow, h2, w1, w3, w2, y)
        stage_combine(nc, gates, slots, x1, y, mods, out)


def rope_table():
    def angles(pos, n, theta):
        inv = (theta ** (-np.arange(0, n, 2, dtype=np.float64) / n)).astype(np.float32)
        ang = (pos.astype(np.float32)[:, None] * inv[None, :]).astype(np.float64)
        return np.cos(ang), np.sin(ang)

    parts = []
    for S in (S0, S1):
        pos = np.arange(S)
        c, s = angles(pos, HD // 4, 500000.0)
        cr, sr = angles(pos // 64, HD // 2, 10000.0)
        cc, sc = angles(pos % 64, HD // 2, 10000.0)
        parts.append(np.concatenate([c, c, -s, s, cr, cr, cc, cc, -sr, sr, -sc, sc], axis=1))
    return np.concatenate(parts).astype(np.float32)


def count_table():
    delta = np.arange(MSPAN)[None, :] - (S0 - P) - np.arange(P)[:, None]
    times = sum(((delta % dil == 0) & (np.abs(delta) <= dil * (window // (2 * dil)))).astype(np.float64)
                for window, dil in ((128, 1), (512, 4), (2048, 16)))
    return np.where(times > 0, np.log(np.maximum(times, 1)) / SCALE, -1e30).astype(np.float32)


_LAYER = ("ln1_g", "ln2_g", "w_ada", "b_ada", "w_in", "w_out", "qn_g", "kn_g", "on_a_g", "on_b_g", "w_rg", "b_rg", "w_re",
          "b_re", "w1", "w3", "w2")
_FINAL = ("lnf_g", "w_adaf", "b_adaf")


def kernel(**inputs):
    import concourse.bacc as _bacc
    from concourse.bass_utils import run_bass_kernel_spmd as _run

    arrays = {
        "x_all": np.concatenate([np.asarray(inputs["x_prompt"])[0], np.asarray(inputs["x_sample"])[0]]),
        "c_all": np.concatenate([np.asarray(inputs["c_prompt"]), np.asarray(inputs["c_sample"])]),
    }
    for name in _LAYER:
        arrays[name] = np.ascontiguousarray(np.asarray(inputs[name])[0])
    for name in _FINAL:
        arrays[name] = np.ascontiguousarray(np.asarray(inputs[name]))
    arrays["rope_tab"] = rope_table()
    arrays["count_tab"] = count_table()
    nc = _bacc.Bacc("TRN2", target_bir_lowering=False, num_devices=1)
    args = [nc.dram_tensor(f"in_{n}", a.shape, mybir.dt.from_np(a.dtype), kind="ExternalInput").ap() for n, a in arrays.items()]
    out = nc.dram_tensor("out_all", (T, D), F32, kind="ExternalOutput").ap()
    hybrid_encoder_kernel(nc, *args, out)
    r = _run(nc, [{f"in_{n}": a for n, a in arrays.items()}], core_ids=[0])
    y = r.results[0]["out_all"]
    return y[None, :S0], y[None, S0:]
```

```python
from contextlib import ExitStack

import numpy as np

import concourse.bass as bass
from concourse import mybir

F32 = mybir.dt.float32
F32R = mybir.dt.float32r
BF16 = mybir.dt.bfloat16
I32 = mybir.dt.int32
ALU = mybir.AluOpType
ACT = mybir.ActivationFunctionType
AX = mybir.AxisListType

P = 128
D = 1024
KC = D // P
S0, S1 = 1024, 256
T = S0 + S1
NT = T // P
NT0 = S0 // P
HD = 64
NHA = NHB = 8
NKVB = 2
NKH = NHA + NKVB
WA = NHA * HD
IN_COLS = 3 * WA + WA + 2 * NKVB * HD
EPS = 1e-6
NG, EPG, NE, FE = 4, 8, 32, 512
HALF = 512
SCALE = HD ** -0.5
MSPAN = S0 + S0 - P
NOV = (2 * T) // P - 1
NBLK = NE + NOV
NRAW = 12
BLOCKS = [(0, 512), (512, 1024), (1024, 1536), (1536, 2048), (2048, 2304)]


class Steps:

    def __init__(self, eng, sem):
        self.eng, self.sem, self.base, self.n = eng, sem, 0, 0

    def did(self, ins):
        ins.then_inc(self.sem, 1)
        self.n += 1

    def wait(self):
        self.eng.wait_ge(self.sem, self.base + self.n)

    def enter(self, i, per):
        self.kept, self.per = self.base + self.n, per
        self.base, self.n = i * per + self.kept, 0

    def leave(self, times):
        assert self.n == self.per, (self.n, self.per)
        self.base, self.n = self.kept + times * self.per, 0


class Memory:

    def __init__(self, nc, ctx, prefix):
        self.nc, self.ctx, self.prefix, self.owned = nc, ctx, prefix, []
        ctx.callback(self.release)

    def release(self):
        if self.owned:
            self.nc.clear_and_free_semaphores(self.owned)
            self.nc.all_engine_barrier()

    def sb(self, name, shape, dt=F32):
        return self.ctx.enter_context(self.nc.sbuf_tensor(f"{self.prefix}_{name}", shape, dt))

    def ps(self, name, shape=(P, 512), dt=F32):
        return self.ctx.enter_context(self.nc.psum_tensor(f"{self.prefix}_{name}", list(shape), dt))

    def sem(self, name):
        self.owned.append(self.nc.alloc_semaphore(f"{self.prefix}_{name}"))
        return self.owned[-1]

    def sems(self, name, n):
        return [self.sem(f"{name}{i}") for i in range(n)]


def make_identity(nc, eng, ident, sem):
    eng.memset(ident[:], 0.0).then_inc(sem, 1)
    eng.wait_ge(sem, 1)
    eng.affine_select(out=ident[:], in_=ident[:], compare_op=ALU.not_equal, fill=1.0, base=0,
                      pattern=[[-1, P]], channel_multiplier=1).then_inc(sem, 1)


def stage_modulation(nc, w_hi, w_lo, c_all, w_ada, b_ada, w_adaf, b_adaf, ln1_g, ln2_g, lnf_g, w_in, mods):
    NR, NW = 6, 2
    WHALF = IN_COLS // 2
    NC, NWC = 8 * KC, 2 * KC
    vectors = [(w_ada, b_ada, v * D, {1: ln1_g, 4: ln2_g}.get(v)) for v in range(6)] + [
        (w_adaf, b_adaf, 0, None), (w_adaf, b_adaf, D, lnf_g)]
    scales = [v for v in range(8) if vectors[v][3] is not None]
    with ExitStack() as ctx:
        m = Memory(nc, ctx, "mod")
        ring = m.sb("ring", [P, NR, D])
        wraw = m.sb("wraw", [P, NW, WHALF])
        c_sb = m.sb("c", [2, D])
        cT = m.sb("cT", [P, KC, 2])
        ident = m.sb("ident", [2, 2])
        bias, norm_w, row = m.sb("bias", [2, 2, D]), m.sb("norm_w", [2, D]), m.sb("row", [2, 2, D])
        pc = m.ps("pc")
        pm = [m.ps(f"pm{i}", [2, D]) for i in range(2)]
        names = ("c_loaded", "silued", "id_made", "cT_ready", "cT_copied", "ring_used", "hi_ready", "lo_ready", "row_ready",
                 "scaled", "norm_w_loaded")
        (c_loaded, silued, id_made, cT_ready, cT_copied, ring_used, hi_ready, lo_ready, row_ready,
         scaled, norm_w_loaded) = (m.sem(n) for n in names)
        ring_loaded, raw_loaded = m.sems("ring_loaded", NR), m.sems("raw_loaded", NW)
        bias_loaded, row_stored = m.sems("bias_loaded", 2), m.sems("row_stored", 2)
        block = ctx.enter_context(nc.Block())

        @block.sync
        def _(sp):
            sp.dma_start(c_sb[:], c_all).then_inc(c_loaded, 16)

            def load_w_in(n):
                k, half = divmod(n, 2)
                if n >= NW:
                    sp.wait_ge(lo_ready, n - NW + 1)
                sp.dma_start(wraw[:, n % NW, :], w_in.rearrange("(p k) n -> p k n", k=KC)[:, k, half * WHALF:(half + 1) * WHALF]
                             ).then_inc(raw_loaded[n % NW], 16)

            for n in range(NC):
                v, k = divmod(n, KC)
                w, _, col, _ = vectors[v]
                if n >= NR:
                    sp.wait_ge(ring_used, n - NR + 1)
                sp.dma_start(ring[:, n % NR, :], w.rearrange("(p k) n -> p k n", k=KC)[:, k, col:col + D]
                             ).then_inc(ring_loaded[n % NR], 16)
                if n % (NC // NWC) == 0:
                    load_w_in(n // (NC // NWC))

        @block.gpsimd
        def _(pool):
            def load_bias(v):
                _, b, col, norm = vectors[v]
                if v >= 2:
                    pool.wait_ge(row_ready, v - 1)
                pool.dma_start(bias[:, v % 2, :], b[col:col + D].unsqueeze(0).to_broadcast([2, D])).then_inc(bias_loaded[v % 2], 16)
                if norm is not None:
                    if scales.index(v):
                        pool.wait_ge(scaled, scales.index(v))
                    pool.dma_start(norm_w[:], norm[:].unsqueeze(0).to_broadcast([2, D])).then_inc(norm_w_loaded, 16)

            load_bias(0)
            load_bias(1)
            pool.memset(ident[:], 0.0).then_inc(id_made, 1)
            pool.wait_ge(id_made, 1)
            pool.affine_select(out=ident[:], in_=ident[:], compare_op=ALU.not_equal, fill=1.0, base=0,
                               pattern=[[-1, 2]], channel_multiplier=1).then_inc(id_made, 1)
            for v in range(8):
                if v in scales:
                    pool.wait_ge(scaled, scales.index(v) + 1)
                else:
                    pool.wait_ge(row_ready, v + 1)
                pool.dma_start(mods[:, v, :], row[:, v % 2, :]).then_inc(row_stored[v % 2], 16)
                if v + 2 < 8:
                    load_bias(v + 2)
            for b in range(2):
                pool.wait_ge(row_stored[b], 16 * 4)

        @block.scalar
        def _(act):
            act.wait_ge(c_loaded, 16)
            act.activation(row[:, 0, :], c_sb[:], ACT.Silu).then_inc(silued, 1)
            for n in range(NWC):
                k, half = divmod(n, 2)
                act.wait_ge(raw_loaded[n % NW], 16 * (n // NW + 1))
                act.copy(w_hi[:, k, half * WHALF:(half + 1) * WHALF], wraw[:, n % NW, :]).then_inc(hi_ready, 1)

        @block.vector
        def _(dve):
            dve.wait_ge(cT_ready, 1)
            dve.tensor_copy(cT[:].rearrange("p k s -> p (k s)"), pc[:, 0:2 * KC]).then_inc(cT_copied, 1)

            def split_lo(n):
                k, half = divmod(n, 2)
                cols = slice(half * WHALF, (half + 1) * WHALF)
                dve.wait_ge(hi_ready, n + 1)
                dve.tensor_tensor(w_lo[:, k, cols], wraw[:, n % NW, :], w_hi[:, k, cols].bitcast(F32),
                                  ALU.subtract).then_inc(lo_ready, 1)

            for v in range(8):
                for n in range(v * NWC // 8, (v + 1) * NWC // 8):
                    split_lo(n)
                dve.wait_ge(ring_used, (v + 1) * KC)
                dve.wait_ge(bias_loaded[v % 2], 16 * (v // 2 + 1))
                if v >= 2:
                    dve.wait_ge(row_stored[v % 2], 16 * (v // 2))
                dve.tensor_tensor(row[:, v % 2, :], pm[v % 2][:], bias[:, v % 2, :], ALU.add).then_inc(row_ready, 1)
                if v in scales:
                    dve.wait_ge(row_ready, v + 1)
                    dve.wait_ge(norm_w_loaded, 16 * (scales.index(v) + 1))
                    dve.scalar_tensor_tensor(out=row[:, v % 2, :], in0=row[:, v % 2, :], scalar=1.0, in1=norm_w[:], op0=ALU.add,
                                             op1=ALU.mult).then_inc(scaled, 1)

        @block.tensor
        def _(pe):
            pe.wait_ge(silued, 1)
            pe.wait_ge(id_made, 2)
            for k in range(KC):
                mm = pe.transpose(pc[:, 2 * k:2 * k + 2], row[:, 0, k:D:KC], ident[:])
            mm.then_inc(cT_ready, 1)
            pe.wait_ge(cT_copied, 1)
            for n in range(NC):
                v, k = divmod(n, KC)
                pe.wait_ge(ring_loaded[n % NR], 16 * (n // NR + 1))
                if v >= 2 and k == 0:
                    pe.wait_ge(row_ready, v - 1)
                for j in range(D // HALF):
                    mm = pe.matmul(pm[v % 2][:, j * HALF:(j + 1) * HALF], cT[:, k, :], ring[:, n % NR, j * HALF:(j + 1) * HALF],
                                   start=(k == 0), stop=(k == KC - 1))
                mm.then_inc(ring_used, 1)


def stage_projection(nc, w_hi, w_lo, x_all, mods, rope_tab, qn_g, kn_g, q_dram, k_dram, v_dram):
    with ExitStack() as ctx:
        m = Memory(nc, ctx, "prj")
        x = m.sb("x", [P, 2, D])
        rope = m.sb("rope", [P, 2, 160])
        h = m.sb("h", [P, D])
        hT_hi, hT_lo = m.sb("hT_hi", [P, 2, KC, P], F32R), m.sb("hT_lo", [P, 2, KC, P], F32R)
        stage = m.sb("stage", [P, IN_COLS])
        a1, sh1 = m.sb("a1", [P, D]), m.sb("sh1", [P, D])
        sq, t1 = m.sb("sq", [P, 512]), m.sb("t1", [P, 512])
        t1b = m.sb("t1b", [P, 128])
        gqk = m.sb("gqk", [P, 2, HD])
        ident = m.sb("ident", [P, P])
        ss, ms, rstd = m.sb("ss", [P, 2]), m.sb("ms", [P, 2]), m.sb("rstd", [P, 2])
        ss8, ms8, rs8 = m.sb("ss8", [P, 8]), m.sb("ms8", [P, 8]), m.sb("rs8", [P, 8])
        neghalf, eps = m.sb("neghalf", [P, 8]), m.sb("eps", [P, 8])
        tp = m.ps("tp", (P, D))
        pp = [m.ps(f"pp{n}") for n in range(5)]
        names = ("const_made", "mods_loaded", "ss_ready", "ms_ready", "rstd_ready", "h_mul", "h_ready", "tp_ready",
                 "hi_ready", "hT_ready", "reduced", "ms8_ready", "rs8_ready", "dve_own")
        (const_made, mods_loaded, ss_ready, ms_ready, rstd_ready, h_mul, h_ready, tp_ready, hi_ready, hT_ready, reduced,
         ms8_ready, rs8_ready, dve_own) = (m.sem(n) for n in names)
        x_loaded, rope_loaded = m.sems("x_loaded", 2), m.sems("rope_loaded", 2)
        proj_ready, copied, squared = m.sems("proj_ready", 5), m.sems("copied", 5), m.sems("squared", 5)
        staged, stored = m.sems("staged", 5), m.sems("stored", 5)
        block = ctx.enter_context(nc.Block())
        bank_read = copied[:3] + squared[3:]
        LOOPS, LAST = 3, NT - 1

        def tiles(eng, body, steps=None, per=None):
            with eng.Fori(0, LOOPS) as i:
                if steps:
                    steps.enter(i, per)
                for b in range(2):
                    body(2 * i + b, b, i, 0, False)
                if steps:
                    steps.leave(LOOPS)
            for t in range(2 * LOOPS, NT):
                body(t, t % 2, t // 2, int(t + 1 >= NT0), t == LAST)

        stores = [(q_dram, 0, 0, 512), (k_dram, 0, 512, 1024), (v_dram, 0, 1024, 1536), (q_dram, 512, 1536, 2048)]

        @block.sync
        def _(sp):
            def load_x(t, b):
                sp.dma_start(x[:, b, :], x_all[bass.ts(t, P), :]).then_inc(x_loaded[b], 16)

            def load_rope(t, b):
                sp.dma_start(rope[:, b, :], rope_tab[bass.ts(t, P), :]).then_inc(rope_loaded[b], 16)

            def load_mods(s):
                sp.dma_start(sh1[:], mods[s, 0, :].unsqueeze(0).to_broadcast([P, D])).then_inc(mods_loaded, 16)
                sp.dma_start(a1[:], mods[s, 1, :].unsqueeze(0).to_broadcast([P, D])).then_inc(mods_loaded, 16)

            load_x(0, 0)
            load_mods(0)
            load_x(1, 1)
            load_rope(0, 0)
            load_rope(1, 1)
            sp.dma_start(gqk[:, 0, :], qn_g[:].unsqueeze(0).to_broadcast([P, HD])).then_inc(mods_loaded, 16)
            sp.dma_start(gqk[:, 1, :], kn_g[:].unsqueeze(0).to_broadcast([P, HD])).then_inc(mods_loaded, 16)

            def body(t, b, u, s_next, last):
                peeled = isinstance(t, int)
                if not peeled or t + 2 < NT:
                    sp.wait_ge(h_ready, t + 1)
                    load_x(t + 2, b)
                if peeled and t == NT0 - 2:
                    sp.wait_ge(h_ready, NT0)
                    load_mods(1)
                for n, (dst, c, lo, hi) in enumerate(stores):
                    if n == 2:
                        sp.wait_ge(copied[n], t + 2)
                    else:
                        sp.wait_ge(staged[n], t + 1)
                    sp.dma_start(dst[bass.ts(t, P), c:c + hi - lo], stage[:, lo:hi]).then_inc(stored[n], 16)
                sp.wait_ge(staged[4], t + 2)
                sp.dma_start(k_dram[bass.ts(t, P), WA:WA + 128], stage[:, 2048:2176]).then_inc(stored[4], 16)
                sp.dma_start(v_dram[bass.ts(t, P), WA:WA + 128], stage[:, 2176:2304]).then_inc(stored[4], 16)
                if not peeled or t + 2 < NT:
                    load_rope(t + 2, b)

            tiles(sp, body)
            for n in range(4):
                sp.wait_ge(stored[n], 16 * (NT + 1))
            sp.wait_ge(stored[4], 32 * (NT + 1))

        @block.gpsimd
        def _(pool):
            pool.memset(neghalf[:], -0.5)
            pool.memset(eps[:], EPS)
            make_identity(nc, pool, ident, const_made)

            def rstd_of(t, b):
                pool.wait_ge(ss_ready, t + 1)
                pool.tensor_tensor(ms[:, b:b + 1], ss[:, b:b + 1], eps[:, 0:1], ALU.add).then_inc(ms_ready, 1)
                pool.wait_ge(ms_ready, t + 1)
                pool.tensor_tensor(rstd[:, b:b + 1], ms[:, b:b + 1], neghalf[:, 0:1], ALU.pow).then_inc(rstd_ready, 1)

            rstd_of(0, 0)

            def body(t, b, u, s_next, last):
                if not last:
                    rstd_of(t + 1, 1 - b)
                for j in range(2):
                    w = (8, NKVB)[j]
                    pool.wait_ge(reduced, 2 * t + j + 1)
                    pool.tensor_tensor(ms8[:, 0:w], ss8[:, 0:w], eps[:, 0:w], ALU.add).then_inc(ms8_ready, 1)
                    pool.wait_ge(ms8_ready, 2 * t + j + 1)
                    pool.tensor_tensor(rs8[:, 0:w], ms8[:, 0:w], neghalf[:, 0:w], ALU.pow).then_inc(rs8_ready, 1)

            tiles(pool, body)

        @block.scalar
        def _(act):
            def square(t, b, u):
                act.wait_ge(x_loaded[b], (u + 1) * 16)
                if not isinstance(t, int) or t:
                    act.wait_ge(tp_ready, t)
                act.activation(h[:], x[:, b, :], ACT.Square, scale=D ** -0.5, accum_out=ss[:, b:b + 1]).then_inc(ss_ready, 1)

            def split_hi(t, b):
                act.wait_ge(tp_ready, t + 1)
                act.copy(hT_hi[:, b].rearrange("p k t -> p (k t)")[:, 0:HALF], tp[:, 0:HALF])
                act.copy(hT_hi[:, b].rearrange("p k t -> p (k t)")[:, HALF:D], tp[:, HALF:D]).then_inc(hi_ready, 1)

            square(0, 0, 0)
            split_hi(0, 0)

            def body(t, b, u, s_next, last):
                if not last:
                    square(t + 1, 1 - b, u + b)
                for n, (lo, hi) in enumerate(BLOCKS):
                    act.wait_ge(proj_ready[n], t + 1)
                    act.wait_ge(stored[n], (t + 1) * (16 if n < 4 else 32))
                    act.copy(stage[:, lo:hi], pp[n][:, 0:hi - lo]).then_inc(copied[n], 1)
                    if n >= 3:
                        w = (512, 128)[n - 3]
                        act.wait_ge(staged[7 - n], t + 1)
                        act.activation(sq[:, 0:w], pp[n][:, 0:w], ACT.Square, scale=HD ** -0.5).then_inc(squared[n], 1)
                    if n == 2 and not last:
                        split_hi(t + 1, 1 - b)

            for n in range(5):
                act.sem_inc(stored[n], 16 if n < 4 else 32)
            act.sem_inc(staged[4], 1)
            tiles(act, body)

        @block.vector
        def _(dve):
            own = Steps(dve, dve_own)

            def make_h(t, b, u, s):
                dve.wait_ge(rstd_ready, t + 1)
                dve.wait_ge(mods_loaded, 64 + 32 * s)
                dve.scalar_tensor_tensor(out=h[:], in0=x[:, b, :], scalar=rstd[:, b:b + 1], in1=a1[:], op0=ALU.mult,
                                         op1=ALU.mult).then_inc(h_mul, 1)
                dve.wait_ge(h_mul, t + 1)
                dve.tensor_tensor(h[:], h[:], sh1[:], ALU.add).then_inc(h_ready, 1)

            def split_lo(t, b):
                dve.wait_ge(hi_ready, t + 1)
                dve.tensor_tensor(hT_lo[:, b].rearrange("p k t -> p (k t)"), tp[:],
                                  hT_hi[:, b].rearrange("p k t -> p (k t)").bitcast(F32), ALU.subtract).then_inc(hT_ready, 1)

            def rope_a(t, b, u, n):
                v = stage[:, BLOCKS[n][0]:BLOCKS[n][1]].rearrange("p (h d) -> p h d", d=HD)
                a, c = (z[:, 0:128].rearrange("p (h d) -> p h d", d=16) for z in (t1, t1b))
                cos = rope[:, b, 0:16].unsqueeze(1).to_broadcast([P, 8, 16])
                sin = rope[:, b, 16:32].unsqueeze(1).to_broadcast([P, 8, 16])
                dve.wait_ge(copied[n], t + 2)
                dve.wait_ge(staged[(4, 0)[n]], t + 1)
                dve.wait_ge(rope_loaded[b], (u + 1) * 16)
                dve.tensor_tensor(a, v[:, :, 0:16], cos, ALU.mult)
                dve.tensor_tensor(c[:, :, 0:8], v[:, :, 8:16], sin[:, :, 0:8], ALU.mult)
                own.did(dve.tensor_tensor(c[:, :, 8:16], v[:, :, 0:8], sin[:, :, 8:16], ALU.mult))
                own.wait()
                dve.tensor_tensor(v[:, :, 0:16], a, c, ALU.add).then_inc(staged[n], 1)

            def norm_b(t, b, u, n):
                j = n - 3
                H = (8, NKVB)[j]
                W = H * HD
                v = stage[:, BLOCKS[n][0]:BLOCKS[n][0] + W]
                v3 = v.rearrange("p (h d) -> p h d", d=HD)
                dve.wait_ge(squared[n], t + 2)
                dve.tensor_reduce(ss8[:, 0:H], sq[:, 0:W].rearrange("p (h d) -> p h d", d=HD), AX.X, ALU.add).then_inc(reduced, 1)
                dve.wait_ge(rs8_ready, 2 * t + j + 1)
                dve.wait_ge(staged[(1, 3)[j]], t + 1)
                own.did(dve.tensor_tensor(v3, v3, rs8[:, 0:H].unsqueeze(2).to_broadcast([P, H, HD]), ALU.mult))
                own.wait()
                own.did(dve.tensor_tensor(v3, v3, gqk[:, j, :].unsqueeze(1).to_broadcast([P, H, HD]), ALU.mult))
                own.wait()
                cos = rope[:, b, 32:96].unsqueeze(1).to_broadcast([P, H, HD])
                sin = rope[:, b, 96:160].rearrange("p (a c d) -> p a c d", a=2, c=2)
                v5 = v.rearrange("p (h a c d) -> p h a c d", a=2, c=2, d=16)
                s5 = sq[:, 0:W].rearrange("p (h a c d) -> p h a c d", a=2, c=2, d=16)
                dve.tensor_tensor(t1[:, 0:W].rearrange("p (h d) -> p h d", d=HD), v3, cos, ALU.mult)
                for c in range(2):
                    step = dve.tensor_tensor(s5[:, :, :, c, :], v5[:, :, :, 1 - c, :],
                                             sin[:, :, c, :].unsqueeze(1).to_broadcast([P, H, 2, 16]), ALU.mult)
                own.did(step)
                own.wait()
                dve.tensor_tensor(v, t1[:, 0:W], sq[:, 0:W], ALU.add).then_inc(staged[n], 1)

            make_h(0, 0, 0, 0)
            split_lo(0, 0)

            def body(t, b, u, s_next, last):
                if not last:
                    make_h(t + 1, 1 - b, u + b, s_next)
                rope_a(t, b, u, 0)
                rope_a(t, b, u, 1)
                if not last:
                    split_lo(t + 1, 1 - b)
                norm_b(t, b, u, 3)
                norm_b(t, b, u, 4)

            tiles(dve, body, own, 2 * 8)

        @block.tensor
        def _(pe):
            def transposes(t):
                pe.wait_ge(h_ready, t + 1)
                if not isinstance(t, int) or t:
                    pe.wait_ge(hT_ready, t)
                for k in range(KC):
                    mm = pe.transpose(tp[:, k * P:(k + 1) * P], h[:, k:D:KC], ident[:])
                mm.then_inc(tp_ready, 1)

            pe.wait_ge(const_made, 2)
            transposes(0)
            for n in range(5):
                pe.sem_inc(bank_read[n], 1)

            def body(t, b, u, s_next, last):
                pe.wait_ge(hT_ready, t + 1)
                for n, (lo, hi) in enumerate(BLOCKS):
                    pe.wait_ge(bank_read[n], t + 1)
                    for k in range(KC):
                        for a, w in ((hT_hi, w_hi), (hT_hi, w_lo), (hT_lo, w_hi)):
                            mm = pe.matmul(pp[n][:, 0:hi - lo], a[:, b, k, :], w[:, k, lo:hi],
                                           start=(k == 0 and w is w_hi and a is hT_hi),
                                           stop=(k == KC - 1 and a is hT_lo))
                    mm.then_inc(proj_ready[n], 1)
                    if n == 2 and not last:
                        transposes(t + 1)

            tiles(pe, body)


def stage_keys(nc, kT, v_sb, k_dram, v_dram):
    with ExitStack() as ctx:
        m = Memory(nc, ctx, "key")
        KW = NKH * HD
        raw = m.sb("raw", [P, 2, KW])
        parts = m.sb("parts", [P, 2, NKH, 2, HD], F32R)
        ident_f, ident = m.sb("ident_f", [P, P]), m.sb("ident", [P, P], F32R)
        tp = [m.ps(f"tp{i}", (P, 512)) for i in range(3)]
        HEADS = [(0, 4), (4, 8), (8, 10)]
        id_made, id_ready, hi_ready, lo_ready, v_loaded = (m.sem(n) for n in ("id_made", "id_ready", "hi_ready", "lo_ready", "v_loaded"))
        raw_loaded, tp_ready, kept = m.sems("raw_loaded", 2), m.sems("tp_ready", 3), m.sems("kept", 3)
        block = ctx.enter_context(nc.Block())

        def tiles(eng, body):
            with eng.Fori(0, NT // 2 - 1) as i:
                for b in range(2):
                    body(2 * i + b, b, i, False)
            for b in range(2):
                body(NT - 2 + b, b, NT // 2 - 1, b == 1)


        @block.sync
        def _(sp):
            def load(t, b):
                sp.dma_start(raw[:, b, :], k_dram[bass.ts(t, P), :]).then_inc(raw_loaded[b], 16)

            load(0, 0)
            load(1, 1)
            with sp.Fori(0, NT // 2 - 1) as i:
                for b in range(2):
                    sp.wait_ge(lo_ready, 2 * i + b + 1)
                    load(2 * i + b + 2, b)
            sp.dma_start(v_sb[:], v_dram.rearrange("(t p) n -> p t n", p=P)).then_inc(v_loaded, 16)
            sp.wait_ge(v_loaded, 16)

        @block.gpsimd
        def _(pool):
            make_identity(nc, pool, ident_f, id_made)

        @block.scalar
        def _(act):
            def split_hi(t, b, u):
                act.wait_ge(raw_loaded[b], (u + 1) * 16)
                act.wait_ge(tp_ready[2], t + 1)
                act.copy(parts[:, b, :, 0, :], raw[:, b, :].rearrange("p (h d) -> p h d", d=HD)).then_inc(hi_ready, 1)

            act.sem_inc(tp_ready[2], 2)
            split_hi(0, 0, 0)

            def body(t, b, u, last):
                if not last:
                    split_hi(t + 1, 1 - b, u + b)
                for n in (0, 2):
                    h0, h1 = HEADS[n]
                    act.wait_ge(tp_ready[n], t + (3 if n == 2 else 1))
                    act.copy(kT[:, h0:h1, bass.ds(t * P, P)],
                             tp[n][:, 0:(h1 - h0) * P].rearrange("p (h t) -> p h t", t=P)).then_inc(kept[n], 1)

            tiles(act, body)

        @block.vector
        def _(dve):
            dve.wait_ge(id_made, 2)
            dve.tensor_copy(ident[:], ident_f[:]).then_inc(id_ready, 1)

            def split_lo(t, b):
                dve.wait_ge(hi_ready, t + 1)
                dve.tensor_tensor(parts[:, b, :, 1, :], raw[:, b, :].rearrange("p (h d) -> p h d", d=HD),
                                  parts[:, b, :, 0, :].bitcast(F32), ALU.subtract).then_inc(lo_ready, 1)

            split_lo(0, 0)

            def body(t, b, u, last):
                if not last:
                    split_lo(t + 1, 1 - b)
                dve.wait_ge(tp_ready[1], t + 1)
                dve.tensor_copy(kT[:, 4:8, bass.ds(t * P, P)],
                                tp[1][:].rearrange("p (h t) -> p h t", t=P)).then_inc(kept[1], 1)

            tiles(dve, body)

        @block.tensor
        def _(pe):
            pe.wait_ge(id_ready, 1)
            for n in range(3):
                pe.sem_inc(kept[n], 1)
            with pe.Fori(0, NT // 2) as i:
                for b in range(2):
                    t = 2 * i + b
                    pe.wait_ge(lo_ready, t + 1)
                    for n, (h0, h1) in enumerate(HEADS):
                        pe.wait_ge(kept[n], t + 1)
                        for h in range(h0, h1):
                            mm = pe.transpose(tp[n][:, (h - h0) * P:(h - h0 + 1) * P].bitcast(F32R),
                                              parts[:, b, h].rearrange("p a d -> p (a d)"), ident[:])
                        mm.then_inc(tp_ready[n], 1)


def stage_attention(nc, kT, v_sb, q_dram, count_tab, o_dram, y_dram):
    NH = NHA + NHB
    with ExitStack() as ctx:
        m = Memory(nc, ctx, "att")
        q = m.sb("q", [P, 2, NH * HD])
        parts = m.sb("parts", [P, NH, 2, 2, HD], F32R)
        qT = m.sb("qT", [P, 2, NH, 2, P], F32R)
        counts = m.sb("counts", [P, 2, S0])
        s = m.sb("s", [P, 2, S0])
        prob = m.sb("prob", [P, 2, S0])
        pT = m.sb("pT", [P, 2, 2, 4, P])
        o = m.sb("o", [P, 2, WA])
        osq = m.sb("osq", [P, WA])
        zero, zeros = m.sb("zero", [P, 1]), m.sb("zeros", [P, D])
        neg_max = m.sb("neg_max", [P, 2])
        den, rden = m.sb("den", [P, NH]), m.sb("rden", [P, NH])
        mso, rso = m.sb("mso", [P, 2]), m.sb("rso", [P, 2])
        neghalf = m.sb("neghalf", [P, 1])
        ident_f, ident = m.sb("ident_f", [P, P]), m.sb("ident", [P, P], F32R)
        sc = [m.ps(f"sc{i}", (P, S0)) for i in range(2)]
        tp = [m.ps(f"tp{i}") for i in range(2)]
        op, qp = m.ps("op"), m.ps("qp")
        names = ("id_made", "id_ready", "consts", "hi_ready", "parts_ready", "qT_kept", "qp_ready", "scores_ready",
                 "masked", "exped", "pv_ready", "o_read", "rden_ready", "mso_ready", "rso_ready", "normed", "mask_begun", "load_begun", "carried",
                 "zeros_made", "zeros_stored")
        (id_made, id_ready, consts, hi_ready, parts_ready, qT_kept, qp_ready, scores_ready, masked, exped, pv_ready,
         o_read, rden_ready, mso_ready, rso_ready, normed, mask_begun, load_begun,
         carried, zeros_made, zeros_stored) = (m.sem(n) for n in names)
        q_loaded, counts_loaded = m.sems("q_loaded", 2), m.sems("counts_loaded", 2)
        tp_ready, pT_kept, stored = m.sems("tp_ready", 2), m.sems("pT_kept", 2), m.sems("stored", 2)
        block = ctx.enter_context(nc.Block())
        LOOPS = 3

        def keys(t):
            return (0, S0, 0) if not isinstance(t, int) or t < NT0 else (S0, S1, NT0)

        def tiles(eng, body):
            with eng.Fori(0, LOOPS) as i:
                for b in range(2):
                    body(2 * i + b, b, i, 2 * i + b + 1)
            for t in range(2 * LOOPS, NT):
                body(t, t % 2, t // 2, t + 1 if t + 1 < NT else None)

        def ahead(t, nxt, j, n):
            if j + n < NH:
                return t, j + n
            return None if nxt is None else (nxt, j + n - NH)

        @block.sync
        def _(sp):
            def load_q(t, b):
                sp.dma_start(q[:, b, :], q_dram[bass.ts(t, P), :]).then_inc(q_loaded[b], 16)

            def load_counts(t, b):
                _, S, v0 = keys(t)
                sp.dma_start(counts[:, b, 0:S], count_tab[:, bass.ds(S0 - P - (t - v0) * P, S)]).then_inc(counts_loaded[b], 16)

            load_q(0, 0)
            load_counts(0, 0)
            load_q(1, 1)
            load_counts(1, 1)
            sp.wait_ge(zeros_made, 1)
            sp.dma_start(y_dram[NE * P:NBLK * P, :].rearrange("(b p) d -> p b d", p=P), zeros[:].unsqueeze(1).to_broadcast([P, NOV, D])
                         ).then_inc(zeros_stored, 16)

            def body(t, b, u, nxt):
                more = not isinstance(t, int) or t + 2 < NT
                if more:
                    sp.wait_ge(masked, NH * t + NHA)
                    sp.sem_inc(load_begun, 1)
                    sp.wait_ge(parts_ready, t + 1)
                    sp.sem_inc(load_begun, 1)
                    load_q(t + 2, b)
                    load_counts(t + 2, b)
                for g in range(2):
                    sp.wait_ge(normed, 2 * t + g + 1)
                    sp.dma_start(o_dram[bass.ts(t, P), g * WA:(g + 1) * WA], o[:, g, :]).then_inc(stored[g], 16)

            tiles(sp, body)
            for g in range(2):
                sp.wait_ge(stored[g], 16 * (NT + 1))
            sp.wait_ge(zeros_stored, 16)

        @block.gpsimd
        def _(pool):
            make_identity(nc, pool, ident_f, id_made)
            pool.memset(zeros[:], 0.0).then_inc(zeros_made, 1)
            pool.memset(zero[:], 0.0).then_inc(consts, 1)
            pool.memset(neghalf[:], -0.5).then_inc(consts, 1)
            pool.wait_ge(consts, 2)

            def split(t, b, u):
                pool.wait_ge(q_loaded[b], (u + 1) * 16)
                pool.wait_ge(qp_ready, t * (NH // 2))
                pool.sem_inc(carried, 1)
                v = q[:, b, :].rearrange("p (h d) -> p h d", d=HD)
                for c in range(2):
                    step = pool.tensor_copy(parts[:, :, 0, c, :], v)
                step.then_inc(hi_ready, 1)
                pool.wait_ge(hi_ready, t + 1)
                for c in range(2):
                    step = pool.tensor_tensor(parts[:, :, 1, c, :], v, parts[:, :, 0, c, :].bitcast(F32), ALU.subtract)
                step.then_inc(parts_ready, 1)

            def norm_o(t, g):
                n = 2 * t + g + 1
                pool.wait_ge(mso_ready, n)
                pool.tensor_tensor(rso[:, g:g + 1], mso[:, g:g + 1], neghalf[:], ALU.pow).then_inc(rso_ready, 1)
                pool.wait_ge(rso_ready, n)
                pool.sem_inc(carried, 1)
                pool.tensor_scalar(o[:, g, :], o[:, g, :], rso[:, g:g + 1], None, ALU.mult).then_inc(normed, 1)

            def body(t, b, u, nxt):
                if nxt is not None:
                    split(t + 1, 1 - b, u + b)
                for g in range(2):
                    norm_o(t, g)

            tiles(pool, body)

        @block.scalar
        def _(act):
            def keep_qT(t, b, pair):
                act.wait_ge(qp_ready, t * (NH // 2) + pair + 1)
                act.copy(qT[:, b, 2 * pair:2 * pair + 2].rearrange("p h c t -> p (h c t)"), qp[:]).then_inc(qT_kept, 1)

            def exp(t, j):
                n, S = NH * t + j + 1, keys(t)[1]
                act.wait_ge(masked, n)
                act.wait_ge(tp_ready[1], n)
                act.activation(prob[:, j % 2, 0:S], s[:, j % 2, 0:S], ACT.Exp, bias=neg_max[:, j % 2:j % 2 + 1], scale=-1.0,
                               accum_out=den[:, j:j + 1]).then_inc(exped, 1)

            def keep_pT(t, j):
                c = keys(t)[1] // (2 * P)
                act.wait_ge(tp_ready[1], NH * t + j + 3)
                act.copy(pT[:, j % 2, 1, 0:c].rearrange("p c t -> p (c t)"), tp[1][:, 0:c * P]).then_inc(pT_kept[1], 1)

            act.sem_inc(tp_ready[1], 2)
            for g in range(2):
                act.sem_inc(stored[g], 16)
            act.wait_ge(q_loaded[0], 16)
            for c in range(2):
                step = act.copy(parts[:, :, 0, c, :], q[:, 0, :].rearrange("p (h d) -> p h d", d=HD))
            step.then_inc(hi_ready, 1)
            for pair in range(NH // 2):
                keep_qT(0, 0, pair)
            exp(0, 0)

            def body(t, b, u, nxt):
                for j in range(NH):
                    nx = ahead(t, nxt, j, 1)
                    if nx:
                        exp(*nx)
                    keep_pT(t, j)
                    if j >= NH // 2 and nxt is not None:
                        keep_qT(t + 1, 1 - b, j - NH // 2)

            tiles(act, body)

        @block.vector
        def _(dve):
            dve.wait_ge(id_made, 2)
            dve.tensor_copy(ident[:], ident_f[:]).then_inc(id_ready, 1)
            dve.sem_inc(exped, 2)
            dve.wait_ge(consts, 2)
            dve.wait_ge(hi_ready, 1)
            for c in range(2):
                step = dve.tensor_tensor(parts[:, :, 1, c, :], q[:, 0, :].rearrange("p (h d) -> p h d", d=HD),
                                         parts[:, :, 0, c, :].bitcast(F32), ALU.subtract)
            step.then_inc(parts_ready, 1)

            def mask(t, b, u, j):
                n, S = NH * t + j + 1, keys(t)[1]
                if j == 0:
                    dve.wait_ge(counts_loaded[b], (u + 1) * 16)
                dve.wait_ge(scores_ready, n)
                dve.wait_ge(exped, n)
                dve.sem_inc(mask_begun, 1)
                held = counts[:, b, 0:S] if j < NHA else zero[:].to_broadcast([P, S])
                dve.tensor_tensor_reduce(s[:, j % 2, 0:S], sc[j % 2][:, 0:S], held, -SCALE, 3e38, ALU.add, ALU.min,
                                         neg_max[:, j % 2:j % 2 + 1]).then_inc(masked, 1)

            def keep_pT(t, j):
                c = keys(t)[1] // (2 * P)
                dve.wait_ge(tp_ready[0], NH * t + j + 1)
                dve.tensor_copy(pT[:, j % 2, 0, 0:c].rearrange("p c t -> p (c t)"), tp[0][:, 0:c * P]).then_inc(pT_kept[0], 1)

            def take_o(t, g):
                heads = slice(g * NHA, (g + 1) * NHA)
                n = 2 * t + g + 1
                dve.wait_ge(pv_ready, n)
                dve.reciprocal(rden[:, heads], den[:, heads]).then_inc(rden_ready, 1)
                dve.wait_ge(rden_ready, n)
                dve.wait_ge(stored[g], (t + 1) * 16)
                dve.tensor_tensor(o[:, g, :].rearrange("p (h d) -> p h d", d=HD), op[:].rearrange("p (h d) -> p h d", d=HD),
                                  rden[:, heads].unsqueeze(2).to_broadcast([P, NHA, HD]), ALU.mult).then_inc(o_read, 1)
                dve.wait_ge(o_read, n + 1)
                dve.tensor_tensor_reduce(osq[:], o[:, g, :], o[:, g, :], 1.0 / WA, EPS, ALU.mult, ALU.add, mso[:, g:g + 1]
                                         ).then_inc(mso_ready, 1)

            mask(0, 0, 0, 0)
            mask(0, 0, 0, 1)

            def body(t, b, u, nxt):
                for j in range(NH):
                    nx = ahead(t, nxt, j, 2)
                    if nx:
                        if j + 2 < NH:
                            mask(t, b, u, j + 2)
                        else:
                            mask(t + 1, 1 - b, u + b, j + 2 - NH)
                    keep_pT(t, j)
                    if j == 8:
                        take_o(t, 0)
                take_o(t, 1)

            tiles(dve, body)

        @block.tensor
        def _(pe):
            def q_transposes(t, pair):
                if pair == 0:
                    pe.wait_ge(parts_ready, t + 1)
                n = t * (NH // 2) + pair
                if not isinstance(n, int) or n:
                    pe.wait_ge(qT_kept, n)
                for h in (0, 1):
                    for c in (0, 1):
                        mm = pe.transpose(qp[:, (2 * h + c) * P:(2 * h + c + 1) * P].bitcast(F32R),
                                          parts[:, 2 * pair + h, c].rearrange("p a d -> p (a d)"), ident[:])
                mm.then_inc(qp_ready, 1)

            def scores(t, b, j):
                k0, S, _ = keys(t)
                kh = j if j < NHA else NHA + (j - NHA) // (NHB // NKVB)
                pe.wait_ge(qT_kept, t * (NH // 2) + j // 2 + 1)
                n = NH * t + j - 1
                if not isinstance(n, int) or n > 0:
                    pe.wait_ge(masked, n)
                for c in range(0, S, HALF):
                    w = min(HALF, S - c)
                    for part in (0, 1):
                        mm = pe.matmul(sc[j % 2][:, c:c + w], qT[:, b, j, part, :], kT[:, kh, k0 + c:k0 + c + w],
                                       start=(part == 0), stop=(part == 1))
                mm.then_inc(scores_ready, 1)

            def p_transposes(t, j):
                c = keys(t)[1] // (2 * P)
                pe.wait_ge(exped, NH * t + j + 3)
                for half in (0, 1):
                    pe.wait_ge(pT_kept[half], NH * t + j + 1)
                    for i in range(c):
                        mm = pe.transpose(tp[half][:, i * P:(i + 1) * P], prob[:, j % 2, (half * c + i) * P:(half * c + i + 1) * P],
                                          ident_f[:])
                    mm.then_inc(tp_ready[half], 1)

            def values(t, j):
                _, S, v0 = keys(t)
                c = S // (2 * P)
                h = j % NHA
                col = j * HD if j < NHA else WA + (j - NHA) // (NHB // NKVB) * HD
                if h == 0:
                    pe.wait_ge(o_read, 2 * t + j // NHA + 1)
                for half in (0, 1):
                    pe.wait_ge(pT_kept[half], NH * t + j + 2)
                    for i in range(c):
                        mm = pe.matmul(op[:, h * HD:(h + 1) * HD], pT[:, j % 2, half, i, :],
                                       v_sb[:, v0 + half * c + i, col:col + HD],
                                       start=(half == 0 and i == 0), stop=(half == 1 and i == c - 1))
                if h == NHA - 1:
                    mm.then_inc(pv_ready, 1)

            pe.wait_ge(id_ready, 1)
            pe.sem_inc(pT_kept[0], 1)
            pe.sem_inc(pT_kept[1], 1)
            pe.sem_inc(o_read, 1)
            q_transposes(0, 0)
            scores(0, 0, 0)
            scores(0, 0, 1)
            for pair in range(1, NH // 2):
                q_transposes(0, pair)

            def body(t, b, u, nxt):
                for j in range(NH):
                    nx = ahead(t, nxt, j, 2)
                    if nx:
                        scores(nx[0], b if j + 2 < NH else 1 - b, nx[1])
                    p_transposes(t, j)
                    if j >= NH // 2 and nxt is not None:
                        q_transposes(t + 1, j - NH // 2)
                    if j:
                        values(t, j - 1)
                values(t, NH - 1)

            tiles(pe, body)


def stage_output(nc, ring, ring_loaded, w1, w3, logits, o_dram, x_all, mods, w_out, on_a_g, on_b_g, w_rg, b_rg, w_re, b_re, x1_dram, h2_dram):
    NL = NG + NE
    with ExitStack() as ctx:
        m = Memory(nc, ctx, "out")
        w_hi, w_lo = m.sb("w_hi", [P, KC, D], F32R), m.sb("w_lo", [P, KC, D], F32R)
        wraw = m.sb("wraw", [P, 2, D])
        gain = m.sb("gain", [P, KC])
        w_r, b_r = m.sb("w_r", [P, KC, NL]), m.sb("b_r", [P, NL])
        o, x = m.sb("o", [P, 2, D]), m.sb("x", [P, 2, D])
        oT_hi, oT_lo = m.sb("oT_hi", [P, 2, KC, P], F32R), m.sb("oT_lo", [P, 2, KC, P], F32R)
        g1, a2, sh2 = m.sb("g1", [P, D]), m.sb("a2", [P, D]), m.sb("sh2", [P, D])
        x1, h2 = m.sb("x1", [P, D]), m.sb("h2", [P, D])
        sq, h2T = m.sb("sq", [P, D]), m.sb("h2T", [P, KC, P])
        ss, ms, rstd = m.sb("ss", [P, 1]), m.sb("ms", [P, 1]), m.sb("rstd", [P, 1])
        neghalf, eps = m.sb("neghalf", [P, 1]), m.sb("eps", [P, 1])
        ident = m.sb("ident", [P, P])
        tp, tp2 = m.ps("tp", (P, D)), m.ps("tp2", (P, D))
        yp = [m.ps(f"yp{i}") for i in range(2)]
        lp = m.ps("lp")
        names = ("id_made", "consts", "w_consts", "hi_ready", "lo_ready", "mods_loaded", "tp_ready", "oT_hi_ready", "oT_ready",
                 "gated", "x1_ready", "ss_ready", "ms_ready", "rstd_ready", "h2_mul", "h2_ready", "tp2_ready", "h2T_ready",
                 "logits_ready", "logits_kept", "x1_stored", "h2_stored")
        (id_made, consts, w_consts, hi_ready, lo_ready, mods_loaded, tp_ready, oT_hi_ready, oT_ready, gated, x1_ready, ss_ready,
         ms_ready, rstd_ready, h2_mul, h2_ready, tp2_ready, h2T_ready, logits_ready, logits_kept, x1_stored, h2_stored
         ) = (m.sem(n) for n in names)
        raw_loaded, o_loaded, x_loaded = m.sems("raw_loaded", 2), m.sems("o_loaded", 2), m.sems("x_loaded", 2)
        yp_ready = m.sems("yp_ready", 2)
        block = ctx.enter_context(nc.Block())
        LOOPS = 3

        def tiles(eng, body):
            body(0, 0, 0, 0)
            with eng.Fori(0, LOOPS) as i:
                body(2 * i + 1, 1, i, 0)
                body(2 * i + 2, 0, i + 1, 0)
            for t in range(2 * LOOPS + 1, NT):
                body(t, t % 2, t // 2, int(t >= NT0))

        def is_last(t):
            return isinstance(t, int) and t == NT - 1

        @block.sync
        def _(sp):
            def load(t, b):
                sp.dma_start(o[:, b, :], o_dram[bass.ts(t, P), :]).then_inc(o_loaded[b], 16)
                sp.dma_start(x[:, b, :], x_all[bass.ts(t, P), :]).then_inc(x_loaded[b], 16)

            def load_mods(s):
                for dst, v in ((g1, 2), (sh2, 3), (a2, 4)):
                    sp.dma_start(dst[:], mods[s, v, :].unsqueeze(0).to_broadcast([P, D])).then_inc(mods_loaded, 16)

            half = P // 2
            sp.dma_start(gain[0:half, :], on_a_g.rearrange("(p k) -> p k", k=KC)).then_inc(w_consts, 16)
            sp.dma_start(gain[half:P, :], on_b_g.rearrange("(p k) -> p k", k=KC)).then_inc(w_consts, 16)
            load(0, 0)
            for k in range(KC):
                if k >= 2:
                    sp.wait_ge(lo_ready, k - 1)
                sp.dma_start(wraw[:, k % 2, :], w_out.rearrange("(p k) n -> p k n", k=KC)[:, k, :]).then_inc(raw_loaded[k % 2], 16)
            load_mods(0)
            load(1, 1)
            sp.dma_start(w_r[:, :, 0:NG], w_rg.rearrange("(p k) n -> p k n", k=KC)).then_inc(w_consts, 16)
            sp.dma_start(w_r[:, :, NG:NL], w_re.rearrange("(p k) n -> p k n", k=KC)).then_inc(w_consts, 16)
            sp.dma_start(b_r[:, 0:NG], b_rg.unsqueeze(0).to_broadcast([P, NG])).then_inc(w_consts, 16)
            sp.dma_start(b_r[:, NG:NL], b_re.unsqueeze(0).to_broadcast([P, NE])).then_inc(w_consts, 16)

            def body(t, b, u, s):
                sp.wait_ge(x1_ready, t + 1)
                sp.dma_start(x1_dram[bass.ts(t, P), :], x1[:]).then_inc(x1_stored, 16)
                if not isinstance(t, int) or t + 2 < NT:
                    load(t + 2, b)
                sp.wait_ge(h2_ready, t + 1)
                sp.dma_start(h2_dram[bass.ts(t, P), :], h2[:]).then_inc(h2_stored, 16)
                if isinstance(t, int) and t == NT0 - 1:
                    load_mods(1)

            tiles(sp, body)
            for slot in range(NRAW):
                w = (w1, w3, w1)[slot // 4]
                c = slot % 4
                sp.dma_start(ring[:, slot, :], w[slot // 8].rearrange("(p k) n -> p k n", k=KC)[:, 2 * c:2 * c + 2, :].rearrange("p k n -> p (k n)")
                             ).then_inc(ring_loaded[slot], 16)
            sp.wait_ge(x1_stored, 16 * (NT + 1))
            sp.wait_ge(h2_stored, 16 * (NT + 1))

        @block.gpsimd
        def _(pool):
            make_identity(nc, pool, ident, id_made)
            pool.memset(neghalf[:], -0.5).then_inc(consts, 1)
            pool.memset(eps[:], EPS).then_inc(consts, 1)
            pool.wait_ge(consts, 2)

            def body(t, b, u, s):
                pool.wait_ge(ss_ready, t + 1)
                pool.tensor_tensor(ms[:], ss[:], eps[:], ALU.add).then_inc(ms_ready, 1)
                pool.wait_ge(ms_ready, t + 1)
                pool.tensor_tensor(rstd[:], ms[:], neghalf[:], ALU.pow).then_inc(rstd_ready, 1)

            tiles(pool, body)

        @block.scalar
        def _(act):
            act.wait_ge(w_consts, 32)
            for k in range(KC):
                act.wait_ge(raw_loaded[k % 2], 16 * (k // 2 + 1))
                act.activation(w_hi[:, k, :], wraw[:, k % 2, :], ACT.Copy, scale=gain[:, k:k + 1]).then_inc(hi_ready, 1)
            act.sem_inc(x1_stored, 16)
            act.sem_inc(h2_stored, 16)

            def split_hi(t, b):
                act.wait_ge(tp_ready, t + 1)
                for c in (0, HALF):
                    step = act.copy(oT_hi[:, b].rearrange("p k t -> p (k t)")[:, c:c + HALF], tp[:, c:c + HALF])
                step.then_inc(oT_hi_ready, 1)

            def keep_h2T(t):
                act.wait_ge(tp2_ready, t + 1)
                for c in (0, HALF):
                    step = act.copy(h2T[:].rearrange("p k t -> p (k t)")[:, c:c + HALF], tp2[:, c:c + HALF])
                step.then_inc(h2T_ready, 1)

            split_hi(0, 0)

            def body(t, b, u, s):
                if not is_last(t):
                    split_hi(t + 1, 1 - b)
                if not isinstance(t, int) or t:
                    keep_h2T(t - 1)
                act.wait_ge(x1_ready, t + 1)
                act.activation(sq[:], x1[:], ACT.Square, scale=D ** -0.5, accum_out=ss[:]).then_inc(ss_ready, 1)

            tiles(act, body)
            keep_h2T(NT - 1)

        @block.vector
        def _(dve):
            for k in range(KC):
                dve.wait_ge(hi_ready, k + 1)
                dve.scalar_tensor_tensor(out=w_lo[:, k, :], in0=wraw[:, k % 2, :], scalar=gain[:, k:k + 1],
                                         in1=w_hi[:, k, :].bitcast(F32), op0=ALU.mult, op1=ALU.subtract).then_inc(lo_ready, 1)
            dve.sem_inc(logits_kept, 1)

            def split_lo(t, b):
                dve.wait_ge(oT_hi_ready, t + 1)
                dve.tensor_tensor(oT_lo[:, b].rearrange("p k t -> p (k t)"), tp[:],
                                  oT_hi[:, b].rearrange("p k t -> p (k t)").bitcast(F32), ALU.subtract).then_inc(oT_ready, 1)

            def keep_logits(t):
                dve.wait_ge(logits_ready, t + 1)
                dve.tensor_tensor(logits[:, bass.ds(t, 1), :], lp[:, 0:NL].unsqueeze(1), b_r[:].unsqueeze(1), ALU.add
                                  ).then_inc(logits_kept, 1)

            dve.wait_ge(w_consts, 96)
            split_lo(0, 0)

            def body(t, b, u, s):
                n = t + 1
                if not isinstance(t, int) or t:
                    dve.wait_ge(ss_ready, t)
                dve.wait_ge(x1_stored, 16 * n)
                dve.wait_ge(mods_loaded, 48 * (s + 1))
                for c in range(2):
                    dve.wait_ge(yp_ready[c], n)
                    dve.tensor_tensor(x1[:, c * HALF:(c + 1) * HALF], yp[c][:], g1[:, c * HALF:(c + 1) * HALF], ALU.mult
                                      ).then_inc(gated, 1)
                    if c == 0 and not is_last(t):
                        split_lo(t + 1, 1 - b)
                dve.wait_ge(x_loaded[b], (u + 1) * 16)
                dve.wait_ge(gated, 2 * n)
                dve.tensor_tensor(x1[:], x1[:], x[:, b, :], ALU.add).then_inc(x1_ready, 1)
                if not isinstance(t, int) or t:
                    keep_logits(t - 1)
                    dve.wait_ge(tp2_ready, t)
                dve.wait_ge(rstd_ready, n)
                dve.wait_ge(h2_stored, 16 * n)
                dve.scalar_tensor_tensor(out=h2[:], in0=x1[:], scalar=rstd[:], in1=a2[:], op0=ALU.mult, op1=ALU.mult
                                         ).then_inc(h2_mul, 1)
                dve.wait_ge(h2_mul, n)
                dve.tensor_tensor(h2[:], h2[:], sh2[:], ALU.add).then_inc(h2_ready, 1)

            tiles(dve, body)
            keep_logits(NT - 1)

        @block.tensor
        def _(pe):
            def transposes(t, b, u):
                pe.wait_ge(o_loaded[b], (u + 1) * 16)
                if not isinstance(t, int) or t:
                    pe.wait_ge(oT_ready, t)
                for k in range(KC):
                    mm = pe.transpose(tp[:, k * P:(k + 1) * P], o[:, b, k:D:KC], ident[:])
                mm.then_inc(tp_ready, 1)

            def router(t):
                pe.wait_ge(h2_ready, t + 1)
                if not isinstance(t, int) or t:
                    pe.wait_ge(h2T_ready, t)
                for k in range(KC):
                    mm = pe.transpose(tp2[:, k * P:(k + 1) * P], h2[:, k:D:KC], ident[:])
                mm.then_inc(tp2_ready, 1)
                pe.wait_ge(logits_kept, t + 1)
                pe.wait_ge(h2T_ready, t + 1)
                for k in range(KC):
                    mm = pe.matmul(lp[:, 0:NL], h2T[:, k, :], w_r[:, k, :], start=(k == 0), stop=(k == KC - 1))
                mm.then_inc(logits_ready, 1)

            pe.wait_ge(id_made, 2)
            transposes(0, 0, 0)
            pe.wait_ge(w_consts, 96)
            pe.wait_ge(lo_ready, KC)

            def body(t, b, u, s):
                pe.wait_ge(oT_ready, t + 1)
                for c in range(2):
                    if not isinstance(t, int) or t:
                        pe.wait_ge(gated, 2 * t - 1 + c)
                    for k in range(KC):
                        for a, w in ((oT_hi, w_hi), (oT_hi, w_lo), (oT_lo, w_hi)):
                            mm = pe.matmul(yp[c][:], a[:, b, k, :], w[:, k, c * HALF:(c + 1) * HALF],
                                           start=(k == 0 and w is w_hi and a is oT_hi), stop=(k == KC - 1 and a is oT_lo))
                    mm.then_inc(yp_ready[c], 1)
                    if c == 0 and not is_last(t):
                        transposes(t + 1, 1 - b, u + b)
                if not isinstance(t, int) or t:
                    router(t - 1)

            tiles(pe, body)
            router(NT - 1)


def stage_route(nc, logits, gates, slots, tokens, overflow, slot_tok):
    NCH = 2
    THR = T // P - 1
    with ExitStack() as ctx:
        m = Memory(nc, ctx, "rt")
        rev4, rev8 = m.sb("rev4", [P, NG]), m.sb("rev8", [P, EPG])
        iota_e, iota_b, thr = m.sb("iota_e", [P, NE]), m.sb("iota_b", [P, NOV]), m.sb("thr", [P, THR])
        tok = m.sb("tok", [P, NT])
        upper, ones = m.sb("upper", [P, P], BF16), m.sb("ones", [P, P], BF16)
        ident = m.sb("ident", [P, P])
        blank = m.sb("blank", [NBLK, P])
        back = m.sb("back", [NBLK, P])
        t4, goh = m.sb("t4", [P, NT, NG]), m.sb("goh", [P, NT, NG])
        v1, v2, v3 = (m.sb(n, [P, NT]) for n in ("v1", "v2", "v3"))
        gsum = m.sb("gsum", [P, NT])
        es, k8, oh = m.sb("es", [P, NT, EPG]), m.sb("k8", [P, NT, EPG]), m.sb("oh", [P, NCH, NT, EPG])
        top = m.sb("top", [P, NCH, NT])
        full = m.sb("full", [P, NCH, NT, NE])
        prod = m.sb("prod", [P, NT, NE])
        sel = m.sb("sel", [P, NT, NE], BF16)
        before = m.sb("before", [P, NT + 1, NE], BF16)
        pos = m.sb("pos", [P, NT + 1, NE])
        over = m.sb("over", [P, NE, THR])
        nblk, inc, adj = m.sb("nblk", [P, NE]), m.sb("inc", [P, 2, NE]), m.sb("adj", [P, NE])
        cmp = m.sb("cmp", [P, NOV, NE])
        ov = m.sb("ov", [P, NOV + 1])
        slot = m.sb("slot", [P, NCH, NT])
        pp = m.ps("pp", (P, (NT + 1) * NE))
        tp = m.ps("tp")
        own_sem, consts, subbed, exped, d_ready, e_ready, sel_ready, pos_ready, slots_ready, blanked, back_ready, back_t = (
            m.sem(n) for n in ("own", "consts", "subbed", "exped", "d_ready", "e_ready", "sel_ready", "pos_ready", "slots_ready",
                               "blanked", "back_ready", "back_t"))
        scattered = m.sem("scattered")
        block = ctx.enter_context(nc.Block())

        @block.gpsimd
        def _(pool):
            steps = Steps(pool, consts)
            steps.did(pool.iota(rev4[:], [[-1, NG]], base=NG, channel_multiplier=0, allow_small_or_imprecise_dtypes=True))
            steps.did(pool.iota(rev8[:], [[-1, EPG]], base=EPG, channel_multiplier=0, allow_small_or_imprecise_dtypes=True))
            steps.did(pool.iota(iota_e[:], [[1, NE]], base=0, channel_multiplier=0, allow_small_or_imprecise_dtypes=True))
            steps.did(pool.iota(iota_b[:], [[1, NOV]], base=0, channel_multiplier=0, allow_small_or_imprecise_dtypes=True))
            steps.did(pool.iota(thr[:], [[P, THR]], base=P, channel_multiplier=0, allow_small_or_imprecise_dtypes=True))
            steps.did(pool.iota(tok[:], [[P, NT]], base=0, channel_multiplier=1, allow_small_or_imprecise_dtypes=True))
            steps.did(pool.memset(ones[:], 1.0))
            steps.did(pool.memset(upper[:], 1.0))
            steps.did(pool.memset(ident[:], 0.0))
            steps.did(pool.memset(blank[:], 0.0))
            steps.wait()
            steps.did(pool.affine_select(out=upper[:], in_=upper[:], compare_op=ALU.is_gt, fill=0.0, base=0,
                                         pattern=[[1, P]], channel_multiplier=-1))
            steps.did(pool.affine_select(out=ident[:], in_=ident[:], compare_op=ALU.not_equal, fill=1.0, base=0,
                                         pattern=[[-1, P]], channel_multiplier=1))
            assert steps.n == 12
            pool.wait_ge(blanked, 16)
            pool.wait_ge(slots_ready, 1)
            for i in range(NCH):
                for t in range(NT):
                    pool.indirect_dma_start(slot_tok, bass.IndirectOffsetOnAxis(ap=slots[:, i, t:t + 1], axis=0),
                                            tok[:, t:t + 1], None).then_inc(scattered, 16)

        @block.sync
        def _(sp):
            sp.wait_ge(consts, 12)
            sp.dma_start(slot_tok.rearrange("(b p) a -> b (p a)", p=P), blank[:]).then_inc(blanked, 16)
            sp.wait_ge(scattered, 16 * NCH * NT)
            sp.dma_start(back[:], slot_tok.rearrange("(b p) a -> b (p a)", p=P)).then_inc(back_ready, 16)
            sp.wait_ge(back_ready, 16)

        @block.scalar
        def _(act):
            act.wait_ge(subbed, 1)
            act.activation(t4[:], t4[:], ACT.Exp).then_inc(exped, 1)
            act.wait_ge(d_ready, 1)
            act.activation(v2[:], v2[:], ACT.Exp).then_inc(e_ready, 1)

        @block.vector
        def _(dve):
            own = Steps(dve, own_sem)

            def do(ins):
                own.did(ins)
                own.wait()

            def first_max(out_onehot, values, best, key, rev, width):
                wide = lambda z: z.unsqueeze(2).to_broadcast([P, NT, width])
                do(dve.tensor_reduce(best, values, AX.X, ALU.max))
                do(dve.tensor_tensor(key, values, wide(best), ALU.is_equal))
                do(dve.tensor_tensor(key, key, rev.unsqueeze(1).to_broadcast([P, NT, width]), ALU.mult))
                do(dve.tensor_reduce(v3[:], key, AX.X, ALU.max))
                do(dve.tensor_tensor(out_onehot, key, wide(v3[:]), ALU.is_equal))

            dve.wait_ge(consts, 12)
            gl = logits[:, :, 0:NG]
            el = logits[:, :, NG:NG + NE].rearrange("p t (g e) -> p t g e", g=NG)
            first_max(goh[:], gl, v1[:], t4[:], rev4[:], NG)
            dve.tensor_tensor(t4[:], gl, v1[:].unsqueeze(2).to_broadcast([P, NT, NG]), ALU.subtract).then_inc(subbed, 1)
            p4 = prod[:].rearrange("p t (g e) -> p t g e", g=NG)
            do(dve.tensor_tensor(p4, el, goh[:].unsqueeze(3).to_broadcast([P, NT, NG, EPG]), ALU.mult))
            do(dve.tensor_reduce(es[:], prod[:].rearrange("p t (g e) -> p t e g", g=NG), AX.X, ALU.add))
            first_max(oh[:, 0], es[:], top[:, 0], k8[:], rev8[:], EPG)
            do(dve.scalar_tensor_tensor(out=es[:], in0=oh[:, 0], scalar=-1e30, in1=es[:], op0=ALU.mult, op1=ALU.add))
            first_max(oh[:, 1], es[:], top[:, 1], k8[:], rev8[:], EPG)
            dve.tensor_tensor(v2[:], top[:, 1], top[:, 0], ALU.subtract).then_inc(d_ready, 1)
            dve.wait_ge(exped, 1)
            do(dve.tensor_reduce(gsum[:], t4[:], AX.X, ALU.add))
            dve.wait_ge(e_ready, 1)
            do(dve.tensor_scalar(v3[:], v2[:], 1.0, None, ALU.add))
            do(dve.tensor_tensor(v3[:], v3[:], gsum[:], ALU.mult))
            do(dve.reciprocal(gates[:, 0], v3[:]))
            do(dve.tensor_tensor(gates[:, 1], gates[:, 0], v2[:], ALU.mult))
            for i in range(NCH):
                f4 = full[:, i].rearrange("p t (g e) -> p t g e", g=NG)
                do(dve.tensor_tensor(f4, goh[:].unsqueeze(3).to_broadcast([P, NT, NG, EPG]),
                                     oh[:, i].unsqueeze(2).to_broadcast([P, NT, NG, EPG]), ALU.mult))
            do(dve.tensor_tensor(sel[:], full[:, 0], full[:, 1], ALU.add))
            do(dve.memset(before[:, 0, :], 0.0))
            for t in range(NT):
                step = dve.tensor_tensor(before[:, t + 1, :], before[:, t, :], sel[:, t, :], ALU.add)
                if t < NT - 1:
                    do(step)
            step.then_inc(sel_ready, 1)
            dve.wait_ge(pos_ready, 1)
            do(dve.tensor_copy(pos[:].rearrange("p t e -> p (t e)"), pp[:]))
            count = pos[:, NT, :]
            do(dve.tensor_tensor(over[:], count.unsqueeze(2).to_broadcast([P, NE, THR]),
                                 thr[:].unsqueeze(1).to_broadcast([P, NE, THR]), ALU.is_gt))
            do(dve.tensor_reduce(nblk[:], over[:], AX.X, ALU.add))
            do(dve.tensor_copy(inc[:, 0, :], nblk[:]))
            shift, cur = 1, 0
            while shift < NE:
                dve.tensor_tensor(inc[:, 1 - cur, shift:NE], inc[:, cur, shift:NE], inc[:, cur, 0:NE - shift], ALU.add)
                do(dve.tensor_copy(inc[:, 1 - cur, 0:shift], inc[:, cur, 0:shift]))
                shift, cur = 2 * shift, 1 - cur
            do(dve.tensor_tensor(adj[:], inc[:, cur, :], nblk[:], ALU.subtract))
            do(dve.tensor_tensor(adj[:], adj[:], iota_e[:], ALU.subtract))
            do(dve.tensor_scalar(adj[:], adj[:], float(NE - 1), float(P), ALU.add, ALU.mult))

            def of_choice(out, table):
                do(dve.tensor_tensor(prod[:], full[:, i], table, ALU.mult))
                do(dve.tensor_reduce(out, prod[:], AX.X, ALU.add))

            for i in range(NCH):
                of_choice(v1[:], pos[:, 0:NT, :])
                of_choice(v2[:], iota_e[:].unsqueeze(1).to_broadcast([P, NT, NE]))
                of_choice(v3[:], adj[:].unsqueeze(1).to_broadcast([P, NT, NE]))
                do(dve.scalar_tensor_tensor(out=v3[:], in0=v1[:], scalar=float(P), in1=v3[:], op0=ALU.is_ge, op1=ALU.mult))
                do(dve.scalar_tensor_tensor(out=v1[:], in0=v2[:], scalar=float(P), in1=v1[:], op0=ALU.mult, op1=ALU.add))
                do(dve.tensor_tensor(slot[:, i], v1[:], v3[:], ALU.add))
            dve.tensor_copy(slots[:], slot[:]).then_inc(slots_ready, 1)
            do(dve.tensor_tensor(cmp[:], inc[:, cur, :].unsqueeze(1).to_broadcast([P, NOV, NE]),
                                 iota_b[:].unsqueeze(2).to_broadcast([P, NOV, NE]), ALU.is_le))
            do(dve.tensor_reduce(ov[:, 0:NOV], cmp[:], AX.X, ALU.add))
            do(dve.tensor_scalar(ov[:, 0:NOV], ov[:, 0:NOV], float(NE - 1), None, ALU.min))
            do(dve.tensor_copy(ov[:, NOV:NOV + 1], inc[:, cur, NE - 1:NE]))
            do(dve.tensor_copy(overflow[:], ov[0:1, :]))
            dve.wait_ge(back_t, 1)
            dve.tensor_copy(tokens[:], tp[:, 0:NBLK])

        @block.tensor
        def _(pe):
            pe.wait_ge(consts, 12)
            pe.wait_ge(sel_ready, 1)
            pe.matmul(pp[:], ones[:], before[:].rearrange("p t e -> p (t e)"), start=True, stop=False, skip_group_check=True)
            pe.matmul(pp[:, 0:NT * NE], upper[:], sel[:].rearrange("p t e -> p (t e)"), start=False, stop=True,
                      skip_group_check=True).then_inc(pos_ready, 1)
            pe.wait_ge(back_ready, 16)
            pe.transpose(tp[:, 0:NBLK], back[:], ident[0:NBLK, 0:NBLK]).then_inc(back_t, 1)


def stage_experts(nc, raw, raw_loaded, tokens, h2_dram, w1, w3, w2, y_dram):
    FC = FE // P
    CH, NSPL = D, 6
    with ExitStack() as ctx:
        m = Memory(nc, ctx, "exp")
        w_hi, w_lo = m.sb("w_hi", [P, NSPL, CH], F32R), m.sb("w_lo", [P, NSPL, CH], F32R)
        rows = m.sb("rows", [P, 2], I32)
        xg = m.sb("xg", [P, 2, D])
        xT_hi, xT_lo = m.sb("xT_hi", [P, 2, KC, P], F32R), m.sb("xT_lo", [P, 2, KC, P], F32R)
        u, hm = m.sb("u", [P, FE]), m.sb("hm", [P, FE])
        hT_hi, hT_lo = m.sb("hT_hi", [P, FC, P], F32R), m.sb("hT_lo", [P, FC, P], F32R)
        y = m.sb("y", [P, D])
        ident = m.sb("ident", [P, P])
        pa, pb, thp = m.ps("pa"), m.ps("pb"), m.ps("thp")
        py, txp = m.ps("py", (P, D)), m.ps("txp", (P, D))
        names = ("id_made", "rows_ready", "carried", "hi_done", "lo_done", "used", "tx_ready", "xT_hi_ready", "xT_ready",
                 "silued", "hm_ready", "th_ready", "hT_hi_ready", "hT_ready", "y_kept", "y_stored")
        (id_made, rows_ready, carried, hi_done, lo_done, used, tx_ready, xT_hi_ready, xT_ready,
         silued, hm_ready, th_ready, hT_hi_ready, hT_ready, y_kept, y_stored) = (m.sem(n) for n in names)
        x_loaded = m.sems("x_loaded", 2)
        block = ctx.enter_context(nc.Block())
        LOOPS = (NE - 4) // 2

        def experts(eng, body, tail=None):
            body(0, 0, 0)
            body(1, 1, 0)
            with eng.Fori(0, LOOPS) as i:
                body(2 * i + 2, 0, i + 1)
                body(2 * i + 3, 1, i + 1)
            body(NE - 2, 0, NE // 2 - 1)
            body(NE - 1, 1, NE // 2 - 1)
            if tail:
                tail()

        def first(e):
            return isinstance(e, int) and e == 0

        def more(e, n):
            return not isinstance(e, int) or e + n < NE

        def number(e, c):
            if isinstance(e, int) and e in (0, NE):
                return (c if c < 4 else c - 4) + (12 * NE - 4 if e else 0)
            return 12 * e + c - 4

        def place(e, c, size):
            if isinstance(e, int):
                return number(e, c) % size, number(e, c) // size
            return (c + 8) % size, (12 // size) * (e - 1) + (c + 8) // size

        def chunks(e):
            if isinstance(e, int) and e == NE:
                return range(4, 8)
            return [c for c in range(12) if not (first(e) and 4 <= c < 8)]

        @block.sync
        def _(sp):
            def body(e, b=None, turn=None):
                for c in chunks(e):
                    n = number(e, c)
                    slot, _ = place(e, c, NRAW)
                    if isinstance(n, int) and n < NRAW:
                        continue
                    if not isinstance(n, int) or n >= NRAW:
                        sp.wait_ge(lo_done, n - NRAW + 1)
                        sp.sem_inc(carried, 1)
                    j = c % 4
                    if 4 <= c < 8:
                        src = w2[bass.ds(e - 1, 1)].rearrange("e (p k) n -> (e p) k n", k=FC)[:, j:j + 1, :]
                    else:
                        src = (w1 if c < 4 else w3)[bass.ds(e, 1)].rearrange("e (p k) n -> (e p) k n", k=KC)[:, 2 * j:2 * j + 2, :]
                    sp.dma_start(raw[:, slot, :], src.rearrange("p k n -> p (k n)")).then_inc(raw_loaded[slot], 16)

            experts(sp, body, lambda: body(NE))

        @block.gpsimd
        def _(pool):
            make_identity(nc, pool, ident, id_made)

            def gather(e, b):
                pool.tensor_copy(rows[:, b:b + 1], tokens[:, bass.ds(e, 1)]).then_inc(rows_ready, 1)
                pool.wait_ge(rows_ready, e + 1)
                pool.sem_inc(carried, 1)
                pool.indirect_dma_start(xg[:, b, :], None, h2_dram, bass.IndirectOffsetOnAxis(ap=rows[:, b:b + 1], axis=0)
                                        ).then_inc(x_loaded[b], 16)

            gather(0, 0)
            gather(1, 1)

            def body(e, b, turn):
                if more(e, 2):
                    pool.wait_ge(tx_ready, e + 1)
                    pool.sem_inc(carried, 1)
                    gather(e + 2, b)

            experts(pool, body)

        @block.scalar
        def _(act):
            act.sem_inc(y_stored, 16)

            def split_hi(e, c):
                n = number(e, c)
                (slot, turn), (to, _) = place(e, c, NRAW), place(e, c, NSPL)
                act.wait_ge(raw_loaded[slot], 16 * (turn + 1))
                if not isinstance(n, int) or n >= NSPL:
                    act.wait_ge(used, n - NSPL + 1)
                act.copy(w_hi[:, to, :], raw[:, slot, :]).then_inc(hi_done, 1)

            def split_xT(e, b):
                act.wait_ge(tx_ready, e + 1)
                act.copy(xT_hi[:, b].rearrange("p k t -> p (k t)"), txp[:]).then_inc(xT_hi_ready, 1)

            def split_hT(e):
                act.wait_ge(th_ready, e + 1)
                act.copy(hT_hi[:].rearrange("p k t -> p (k t)"), thp[:]).then_inc(hT_hi_ready, 1)

            def silu(e):
                act.wait_ge(used, number(e, 3) + 1)
                if not first(e):
                    act.wait_ge(hm_ready, e)
                act.activation(u[:], pa[:], ACT.Silu).then_inc(silued, 1)

            def keep_y(e):
                act.wait_ge(used, number(e + 1, 7) + 1)
                act.wait_ge(y_stored, 16 * (e + 1))
                act.copy(y[:], py[:]).then_inc(y_kept, 1)
                act.wait_ge(y_kept, e + 2)
                act.sem_inc(carried, 1)
                act.dma_start(y_dram[bass.ts(e, P), :], y[:]).then_inc(y_stored, 16)

            split_xT(0, 0)

            def body(e, b, turn):
                for c in chunks(e):
                    split_hi(e, c)
                    if c == 0 and not (isinstance(e, int) and e < 2):
                        keep_y(e - 2)
                    if c == 5:
                        split_hT(e - 1)
                    if c == 8:
                        if more(e, 1):
                            split_xT(e + 1, 1 - b)
                        silu(e)

            def tail():
                for c in chunks(NE):
                    split_hi(NE, c)
                    if c == 4:
                        keep_y(NE - 2)
                    if c == 5:
                        split_hT(NE - 1)
                keep_y(NE - 1)
                act.wait_ge(y_stored, 16 * (NE + 1))

            experts(act, body, tail)

        @block.vector
        def _(dve):
            def split_lo(e, c):
                (slot, _), (to, _) = place(e, c, NRAW), place(e, c, NSPL)
                dve.wait_ge(hi_done, number(e, c) + 1)
                dve.tensor_tensor(w_lo[:, to, :], raw[:, slot, :], w_hi[:, to, :].bitcast(F32), ALU.subtract).then_inc(lo_done, 1)

            def split_xT(e, b):
                dve.wait_ge(xT_hi_ready, e + 1)
                dve.tensor_tensor(xT_lo[:, b].rearrange("p k t -> p (k t)"), txp[:],
                                  xT_hi[:, b].rearrange("p k t -> p (k t)").bitcast(F32), ALU.subtract).then_inc(xT_ready, 1)

            def split_hT(e):
                dve.wait_ge(hT_hi_ready, e + 1)
                dve.tensor_tensor(hT_lo[:].rearrange("p k t -> p (k t)"), thp[:],
                                  hT_hi[:].rearrange("p k t -> p (k t)").bitcast(F32), ALU.subtract).then_inc(hT_ready, 1)

            def gate_up(e):
                dve.wait_ge(used, number(e, 11) + 1)
                dve.wait_ge(silued, e + 1)
                if not first(e):
                    dve.wait_ge(th_ready, e)
                dve.tensor_tensor(hm[:], u[:], pb[:], ALU.mult).then_inc(hm_ready, 1)

            dve.sem_inc(y_kept, 1)
            split_xT(0, 0)

            def body(e, b, turn):
                for c in chunks(e):
                    split_lo(e, c)
                    if c == 2 and not first(e):
                        gate_up(e - 1)
                    if c == 5:
                        split_hT(e - 1)
                    if c == 8 and more(e, 1):
                        split_xT(e + 1, 1 - b)

            def tail():
                gate_up(NE - 1)
                for c in chunks(NE):
                    split_lo(NE, c)
                    if c == 5:
                        split_hT(NE - 1)

            experts(dve, body, tail)

        @block.tensor
        def _(pe):
            def tx(e, b, turn):
                pe.wait_ge(x_loaded[b], 16 * (turn + 1))
                if not first(e):
                    pe.wait_ge(xT_ready, e)
                for k in range(KC):
                    mm = pe.transpose(txp[:, k * P:(k + 1) * P], xg[:, b, k:D:KC], ident[:])
                mm.then_inc(tx_ready, 1)

            def th(e):
                pe.wait_ge(hm_ready, e + 1)
                for k in range(FC):
                    mm = pe.transpose(thp[:, k * P:(k + 1) * P], hm[:, k:FE:FC], ident[:])
                mm.then_inc(th_ready, 1)

            def up(e, b, c, out):
                to, _ = place(e, c, NSPL)
                pe.wait_ge(lo_done, number(e, c) + 1)
                for r in range(2):
                    k = 2 * (c % 4) + r
                    for a, w in ((xT_hi, w_hi), (xT_hi, w_lo), (xT_lo, w_hi)):
                        mm = pe.matmul(out[:], a[:, b, k, :], w[:, to, r * FE:(r + 1) * FE],
                                       start=(k == 0 and w is w_hi and a is xT_hi), stop=(k == KC - 1 and a is xT_lo))
                mm.then_inc(used, 1)

            def down(e, c):
                to, _ = place(e, c, NSPL)
                k = c % 4
                pe.wait_ge(lo_done, number(e, c) + 1)
                for a, w in ((hT_hi, w_hi), (hT_hi, w_lo), (hT_lo, w_hi)):
                    for half in range(2):
                        mm = pe.matmul(py[:, half * HALF:(half + 1) * HALF], a[:, k, :], w[:, to, half * HALF:(half + 1) * HALF],
                                       start=(k == 0 and w is w_hi and a is hT_hi), stop=(k == FC - 1 and a is hT_lo))
                mm.then_inc(used, 1)

            def before_down(e):
                pe.wait_ge(hT_ready, e)
                pe.wait_ge(y_kept, e)

            pe.wait_ge(id_made, 2)
            tx(0, 0, 0)

            def body(e, b, turn):
                pe.wait_ge(xT_ready, e + 1)
                if not first(e):
                    pe.wait_ge(silued, e)
                for c in chunks(e):
                    if c == 4:
                        before_down(e)
                    if c == 8 and not first(e):
                        pe.wait_ge(hm_ready, e)
                    if 4 <= c < 8:
                        down(e, c)
                    else:
                        up(e, b, c, pa if c < 4 else pb)
                    if c == 1 and not first(e):
                        th(e - 1)
                    if c == 3 and more(e, 1):
                        tx(e + 1, 1 - b, turn + b)

            def tail():
                th(NE - 1)
                before_down(NE)
                for c in chunks(NE):
                    down(NE, c)

            experts(pe, body, tail)


def stage_overflow(nc, tokens, overflow, h2_dram, w1, w3, w2, y_dram):
    FC = FE // P
    with ExitStack() as ctx:
        m = Memory(nc, ctx, "ovf")
        w1_sb, w3_sb, w2_sb = m.sb("w1", [P, KC, FE]), m.sb("w3", [P, KC, FE]), m.sb("w2", [P, FC, D])
        rows = m.sb("rows", [P, 1], I32)
        xg, xT = m.sb("xg", [P, D]), m.sb("xT", [P, KC, P])
        u, hm, hT, y = m.sb("u", [P, FE]), m.sb("hm", [P, FE]), m.sb("hT", [P, FC, P]), m.sb("y", [P, D])
        ident = m.sb("ident", [P, P])
        pa, pb, thp = m.ps("pa"), m.ps("pb"), m.ps("thp")
        py, txp = m.ps("py", (P, D)), m.ps("txp", (P, D))
        names = ("id_made", "w_loaded", "rows_ready", "x_loaded", "tx_ready", "xT_ready", "ab_ready", "silued", "hm_ready",
                 "th_ready", "hT_ready", "y_ready", "y_kept", "y_stored", "carried")
        (id_made, w_loaded, rows_ready, x_loaded, tx_ready, xT_ready, ab_ready, silued, hm_ready, th_ready, hT_ready, y_ready,
         y_kept, y_stored, carried) = (m.sem(n) for n in names)
        block = ctx.enter_context(nc.Block())

        def blocks(eng, body):
            number = eng.value_load(overflow[0:1, NOV:NOV + 1], min_val=0, max_val=NOV)
            with eng.If(number > 0):
                with eng.Fori(0, NOV) as j:
                    with eng.If(j < number):
                        body(j)

        @block.sync
        def _(sp):
            sp.sem_inc(y_stored, 16)

            def body(j):
                sp.wait_ge(y_stored, 16 * (j + 1))
                sp.sem_inc(carried, 1)
                e = sp.value_load(overflow[0:1, bass.ds(j, 1)], min_val=0, max_val=NE - 1)
                for dst, w, k in ((w1_sb, w1, KC), (w3_sb, w3, KC), (w2_sb, w2, FC)):
                    sp.dma_start(dst[:].rearrange("p k n -> p (k n)"),
                                 w[bass.ds(e, 1)].rearrange("e (p k) n -> (e p) (k n)", k=k)).then_inc(w_loaded, 16)
                sp.wait_ge(y_kept, j + 1)
                sp.sem_inc(carried, 1)
                sp.dma_start(y_dram[bass.ts(NE + j, P), :], y[:]).then_inc(y_stored, 16)
                sp.wait_ge(y_stored, 16 * (j + 2))
                sp.sem_inc(carried, 1)

            blocks(sp, body)

        @block.gpsimd
        def _(pool):
            make_identity(nc, pool, ident, id_made)

            def body(j):
                pool.wait_ge(y_stored, 16 * (j + 1))
                pool.sem_inc(carried, 1)
                pool.tensor_copy(rows[:], tokens[:, bass.ds(NE + j, 1)]).then_inc(rows_ready, 1)
                pool.wait_ge(rows_ready, j + 1)
                pool.sem_inc(carried, 1)
                pool.indirect_dma_start(xg[:], None, h2_dram, bass.IndirectOffsetOnAxis(ap=rows[:], axis=0)
                                        ).then_inc(x_loaded, 16)

            blocks(pool, body)

        @block.scalar
        def _(act):
            def body(j):
                act.wait_ge(ab_ready, 2 * j + 1)
                act.activation(u[:], pa[:], ACT.Silu).then_inc(silued, 1)
                act.wait_ge(y_ready, j + 1)
                act.copy(y[:], py[:]).then_inc(y_kept, 1)

            blocks(act, body)

        @block.vector
        def _(dve):
            def body(j):
                dve.wait_ge(tx_ready, j + 1)
                dve.tensor_copy(xT[:].rearrange("p k t -> p (k t)"), txp[:]).then_inc(xT_ready, 1)
                dve.wait_ge(ab_ready, 2 * j + 2)
                dve.wait_ge(silued, j + 1)
                dve.tensor_tensor(hm[:], u[:], pb[:], ALU.mult).then_inc(hm_ready, 1)
                dve.wait_ge(th_ready, j + 1)
                dve.tensor_copy(hT[:].rearrange("p k t -> p (k t)"), thp[:]).then_inc(hT_ready, 1)

            blocks(dve, body)

        @block.tensor
        def _(pe):
            pe.wait_ge(id_made, 2)

            def body(j):
                pe.wait_ge(x_loaded, 16 * (j + 1))
                for k in range(KC):
                    mm = pe.transpose(txp[:, k * P:(k + 1) * P], xg[:, k:D:KC], ident[:])
                mm.then_inc(tx_ready, 1)
                pe.wait_ge(xT_ready, j + 1)
                pe.wait_ge(w_loaded, 48 * (j + 1))
                for out, w in ((pa, w1_sb), (pb, w3_sb)):
                    for k in range(KC):
                        mm = pe.matmul(out[:], xT[:, k, :], w[:, k, :], start=(k == 0), stop=(k == KC - 1))
                    mm.then_inc(ab_ready, 1)
                pe.wait_ge(hm_ready, j + 1)
                for k in range(FC):
                    mm = pe.transpose(thp[:, k * P:(k + 1) * P], hm[:, k:FE:FC], ident[:])
                mm.then_inc(th_ready, 1)
                pe.wait_ge(hT_ready, j + 1)
                for half in range(2):
                    for k in range(FC):
                        mm = pe.matmul(py[:, half * HALF:(half + 1) * HALF], hT[:, k, :],
                                       w2_sb[:, k, half * HALF:(half + 1) * HALF], start=(k == 0), stop=(k == FC - 1))
                mm.then_inc(y_ready, 1)

            blocks(pe, body)


def stage_combine(nc, gates, slots, x1_dram, y_dram, mods, out):
    NY = 3
    with ExitStack() as ctx:
        m = Memory(nc, ctx, "fin")
        g2, shf, af = m.sb("g2", [P, 2, D]), m.sb("shf", [P, 2, D]), m.sb("af", [P, 2, D])
        x1, ya, yb = m.sb("x1", [P, NT, D]), m.sb("ya", [P, NT, D]), m.sb("yb", [P, NT, D])
        ys, sq, res = m.sb("ys", [P, NY, D]), m.sb("sq", [P, D]), m.sb("res", [P, 2, D])
        ss, ms, rstd = m.sb("ss", [P, 2]), m.sb("ms", [P, 2]), m.sb("rstd", [P, 2])
        neghalf, eps = m.sb("neghalf", [P, 1]), m.sb("eps", [P, 1])
        rows = m.sb("rows", [P, NT, 2], I32)
        names = ("consts", "rows_ready", "weighed", "summed", "gated", "x2_ready", "ss_ready", "ms_ready", "rstd_ready",
                 "scaled", "res_ready")
        (consts, rows_ready, weighed, summed, gated, x2_ready, ss_ready, ms_ready, rstd_ready, scaled, res_ready
         ) = (m.sem(n) for n in names)
        ya_loaded, yb_loaded, x1_loaded = (m.sems(n, NT) for n in ("ya_loaded", "yb_loaded", "x1_loaded"))
        stored, mods_loaded = m.sems("stored", 2), m.sems("mods_loaded", 2)
        block = ctx.enter_context(nc.Block())

        def seq(t):
            return int(t >= NT0)

        @block.sync
        def _(sp):
            def load_mods(s):
                for dst, v in ((g2, 5), (shf, 6), (af, 7)):
                    sp.dma_start(dst[:, s, :], mods[s, v, :].unsqueeze(0).to_broadcast([P, D])).then_inc(mods_loaded[s], 16)

            def store(t):
                sp.wait_ge(res_ready, t + 1)
                sp.dma_start(out[t * P:(t + 1) * P, :], res[:, t % 2, :]).then_inc(stored[t % 2], 16)

            load_mods(0)
            for t in range(NT):
                if t == 3:
                    load_mods(1)
                if t >= 3:
                    store(t - 3)
                sp.dma_start(x1[:, t, :], x1_dram[t * P:(t + 1) * P, :]).then_inc(x1_loaded[t], 16)
            for t in range(NT - 3, NT):
                store(t)
            for b in range(2):
                sp.wait_ge(stored[b], 16 * (NT // 2))

        @block.gpsimd
        def _(pool):
            pool.memset(neghalf[:], -0.5).then_inc(consts, 1)
            pool.memset(eps[:], EPS).then_inc(consts, 1)
            pool.tensor_copy(rows[:].rearrange("p t i -> p i t"), slots[:]).then_inc(rows_ready, 1)
            pool.wait_ge(consts, 2)
            pool.wait_ge(rows_ready, 1)

            def gather(t):
                for i, (dst, loaded) in enumerate(((ya, ya_loaded), (yb, yb_loaded))):
                    pool.indirect_dma_start(dst[:, t, :], None, y_dram, bass.IndirectOffsetOnAxis(ap=rows[:, t, i:i + 1], axis=0)
                                            ).then_inc(loaded[t], 16)

            for t in range(3):
                gather(t)
            for t in range(NT):
                v = ys[:, t % NY, :]
                if t + 3 < NT:
                    gather(t + 3)
                pool.wait_ge(x1_loaded[t], 16)
                pool.wait_ge(gated, t + 1)
                pool.tensor_tensor(v, v, x1[:, t, :], ALU.add).then_inc(x2_ready, 1)
                pool.wait_ge(ss_ready, t + 1)
                if t >= 2:
                    pool.wait_ge(scaled, t - 1)
                c = slice(t % 2, t % 2 + 1)
                pool.tensor_tensor(ms[:, c], ss[:, c], eps[:], ALU.add).then_inc(ms_ready, 1)
                pool.wait_ge(ms_ready, t + 1)
                pool.tensor_tensor(rstd[:, c], ms[:, c], neghalf[:], ALU.pow).then_inc(rstd_ready, 1)

        @block.scalar
        def _(act):
            def weigh(t):
                act.wait_ge(ya_loaded[t], 16)
                if t >= NY:
                    act.wait_ge(scaled, t - NY + 1)
                act.activation(ys[:, t % NY, :], ya[:, t, :], ACT.Copy, scale=gates[:, 0, t:t + 1]).then_inc(weighed, 1)

            weigh(0)
            for t in range(NT):
                if t + 1 < NT:
                    weigh(t + 1)
                act.wait_ge(x2_ready, t + 1)
                if t >= 2:
                    act.wait_ge(ms_ready, t - 1)
                act.activation(sq[:], ys[:, t % NY, :], ACT.Square, scale=D ** -0.5, accum_out=ss[:, t % 2:t % 2 + 1]
                               ).then_inc(ss_ready, 1)

        @block.vector
        def _(dve):
            def sum_rows(t):
                v = ys[:, t % NY, :]
                dve.wait_ge(yb_loaded[t], 16)
                dve.wait_ge(weighed, t + 1)
                dve.scalar_tensor_tensor(out=v, in0=yb[:, t, :], scalar=gates[:, 1, t:t + 1], in1=v, op0=ALU.mult, op1=ALU.add
                                         ).then_inc(summed, 1)
                dve.wait_ge(summed, t + 1)
                if t in (0, NT0):
                    dve.wait_ge(mods_loaded[seq(t)], 48)
                dve.tensor_tensor(v, v, g2[:, seq(t), :], ALU.mult).then_inc(gated, 1)

            sum_rows(0)
            for t in range(NT):
                if t + 1 < NT:
                    sum_rows(t + 1)
                dve.wait_ge(rstd_ready, t + 1)
                if t >= 2:
                    dve.wait_ge(stored[t % 2], t // 2 * 16)
                r = res[:, t % 2, :]
                dve.scalar_tensor_tensor(out=r, in0=ys[:, t % NY, :], scalar=rstd[:, t % 2:t % 2 + 1], in1=af[:, seq(t), :],
                                         op0=ALU.mult, op1=ALU.mult).then_inc(scaled, 1)
                dve.wait_ge(scaled, t + 1)
                dve.tensor_tensor(r, r, shf[:, seq(t), :], ALU.add).then_inc(res_ready, 1)


def hybrid_encoder_kernel(nc, x_all, c_all, ln1_g, ln2_g, w_ada, b_ada, w_in, w_out, qn_g, kn_g, on_a_g, on_b_g,
                          w_rg, b_rg, w_re, b_re, w1, w3, w2, lnf_g, w_adaf, b_adaf, rope_tab, count_tab, out):
    def scratch(name, shape):
        return nc.dram_tensor(name, shape, F32, kind="Internal").ap()

    mods = scratch("mods", (2, 8, D))
    q, k, v = scratch("q", (T, WA + NHB * HD)), scratch("k", (T, NKH * HD)), scratch("v", (T, NKH * HD))
    o, x1, h2 = scratch("o", (T, D)), scratch("x1", (T, D)), scratch("h2", (T, D))
    slot_tok, y = scratch("slot_tok", (NBLK * P, 1)), scratch("y", (NBLK * P, D))
    with ExitStack() as ctx:
        m = Memory(nc, ctx, "in")
        w_hi, w_lo = m.sb("w_hi", [P, KC, IN_COLS], F32R), m.sb("w_lo", [P, KC, IN_COLS], F32R)
        stage_modulation(nc, w_hi, w_lo, c_all, w_ada, b_ada, w_adaf, b_adaf, ln1_g, ln2_g, lnf_g, w_in, mods)
        stage_projection(nc, w_hi, w_lo, x_all, mods, rope_tab, qn_g, kn_g, q, k, v)
    with ExitStack() as ctx:
        m = Memory(nc, ctx, "kv")
        kT, v_sb = m.sb("kT", [P, NKH, T], F32R), m.sb("v", [P, NT, NKH * HD])
        stage_keys(nc, kT, v_sb, k, v)
        stage_attention(nc, kT, v_sb, q, count_tab, o, y)
    with ExitStack() as ctx:
        m = Memory(nc, ctx, "route")
        logits, gates = m.sb("logits", [P, NT, NG + NE]), m.sb("gates", [P, 2, NT])
        slots, tokens = m.sb("slots", [P, 2, NT], I32), m.sb("tokens", [P, NBLK], I32)
        overflow = m.sb("overflow", [1, NOV + 1], I32)
        with ExitStack() as ring_ctx:
            ring = Memory(nc, ring_ctx, "ring")
            raw, raw_loaded = ring.sb("raw", [P, NRAW, D]), ring.sems("raw_loaded", NRAW)
            stage_output(nc, raw, raw_loaded, w1, w3, logits, o, x_all, mods, w_out, on_a_g, on_b_g, w_rg, b_rg, w_re, b_re,
                         x1, h2)
            stage_route(nc, logits, gates, slots, tokens, overflow, slot_tok)
            stage_experts(nc, raw, raw_loaded, tokens, h2, w1, w3, w2, y)
        stage_overflow(nc, tokens, overflow, h2, w1, w3, w2, y)
        stage_combine(nc, gates, slots, x1, y, mods, out)


def rope_table():
    def angles(pos, n, theta):
        inv = (theta ** (-np.arange(0, n, 2, dtype=np.float64) / n)).astype(np.float32)
        ang = (pos.astype(np.float32)[:, None] * inv[None, :]).astype(np.float64)
        return np.cos(ang), np.sin(ang)

    parts = []
    for S in (S0, S1):
        pos = np.arange(S)
        c, s = angles(pos, HD // 4, 500000.0)
        cr, sr = angles(pos // 64, HD // 2, 10000.0)
        cc, sc = angles(pos % 64, HD // 2, 10000.0)
        parts.append(np.concatenate([c, c, -s, s, cr, cr, cc, cc, -sr, sr, -sc, sc], axis=1))
    return np.concatenate(parts).astype(np.float32)


def count_table():
    delta = np.arange(MSPAN)[None, :] - (S0 - P) - np.arange(P)[:, None]
    times = sum(((delta % dil == 0) & (np.abs(delta) <= dil * (window // (2 * dil)))).astype(np.float64)
                for window, dil in ((128, 1), (512, 4), (2048, 16)))
    return np.where(times > 0, np.log(np.maximum(times, 1)) / SCALE, -1e30).astype(np.float32)


_LAYER = ("ln1_g", "ln2_g", "w_ada", "b_ada", "w_in", "w_out", "qn_g", "kn_g", "on_a_g", "on_b_g", "w_rg", "b_rg", "w_re",
          "b_re", "w1", "w3", "w2")
_FINAL = ("lnf_g", "w_adaf", "b_adaf")


def kernel(**inputs):
    import concourse.bacc as _bacc
    from concourse.bass_utils import run_bass_kernel_spmd as _run

    arrays = {
        "x_all": np.concatenate([np.asarray(inputs["x_prompt"])[0], np.asarray(inputs["x_sample"])[0]]),
        "c_all": np.concatenate([np.asarray(inputs["c_prompt"]), np.asarray(inputs["c_sample"])]),
    }
    for name in _LAYER:
        arrays[name] = np.ascontiguousarray(np.asarray(inputs[name])[0])
    for name in _FINAL:
        arrays[name] = np.ascontiguousarray(np.asarray(inputs[name]))
    arrays["rope_tab"] = rope_table()
    arrays["count_tab"] = count_table()
    nc = _bacc.Bacc("TRN2", target_bir_lowering=False, num_devices=1)
    args = [nc.dram_tensor(f"in_{n}", a.shape, mybir.dt.from_np(a.dtype), kind="ExternalInput").ap() for n, a in arrays.items()]
    out = nc.dram_tensor("out_all", (T, D), F32, kind="ExternalOutput").ap()
    hybrid_encoder_kernel(nc, *args, out)
    r = _run(nc, [{f"in_{n}": a for n, a in arrays.items()}], core_ids=[0])
    y = r.results[0]["out_all"]
    return y[None, :S0], y[None, S0:]
```

```python
from contextlib import ExitStack

import numpy as np

import concourse.bass as bass
from concourse import mybir

F32 = mybir.dt.float32
F32R = mybir.dt.float32r
BF16 = mybir.dt.bfloat16
I32 = mybir.dt.int32
ALU = mybir.AluOpType
ACT = mybir.ActivationFunctionType
AX = mybir.AxisListType

P = 128
D = 1024
KC = D // P
S0, S1 = 1024, 256
T = S0 + S1
NT = T // P
NT0 = S0 // P
HD = 64
NHA = NHB = 8
NKVB = 2
NKH = NHA + NKVB
WA = NHA * HD
IN_COLS = 3 * WA + WA + 2 * NKVB * HD
EPS = 1e-6
NG, EPG, NE, FE = 4, 8, 32, 512
HALF = 512
SCALE = HD ** -0.5
MSPAN = S0 + S0 - P
NOV = (2 * T) // P - 1
NBLK = NE + NOV
NRAW, NEXTRA = 12, 8
BLOCKS = [(0, 512), (512, 1024), (1024, 1536), (1536, 2048), (2048, 2304)]


class Steps:

    def __init__(self, eng, sem):
        self.eng, self.sem, self.base, self.n = eng, sem, 0, 0

    def did(self, ins):
        ins.then_inc(self.sem, 1)
        self.n += 1

    def wait(self):
        self.eng.wait_ge(self.sem, self.base + self.n)

    def enter(self, i, per):
        self.kept, self.per = self.base + self.n, per
        self.base, self.n = i * per + self.kept, 0

    def leave(self, times):
        assert self.n == self.per, (self.n, self.per)
        self.base, self.n = self.kept + times * self.per, 0


class Memory:

    def __init__(self, nc, ctx, prefix):
        self.nc, self.ctx, self.prefix, self.owned = nc, ctx, prefix, []
        ctx.callback(self.release)

    def release(self):
        if self.owned:
            self.nc.clear_and_free_semaphores(self.owned)
            self.nc.all_engine_barrier()

    def sb(self, name, shape, dt=F32):
        return self.ctx.enter_context(self.nc.sbuf_tensor(f"{self.prefix}_{name}", shape, dt))

    def ps(self, name, shape=(P, 512), dt=F32):
        return self.ctx.enter_context(self.nc.psum_tensor(f"{self.prefix}_{name}", list(shape), dt))

    def sem(self, name):
        self.owned.append(self.nc.alloc_semaphore(f"{self.prefix}_{name}"))
        return self.owned[-1]

    def sems(self, name, n):
        return [self.sem(f"{name}{i}") for i in range(n)]


def make_identity(nc, eng, ident, sem):
    eng.memset(ident[:], 0.0).then_inc(sem, 1)
    eng.wait_ge(sem, 1)
    eng.affine_select(out=ident[:], in_=ident[:], compare_op=ALU.not_equal, fill=1.0, base=0,
                      pattern=[[-1, P]], channel_multiplier=1).then_inc(sem, 1)


def stage_modulation(nc, w_hi, w_lo, c_all, w_ada, b_ada, w_adaf, b_adaf, ln1_g, ln2_g, lnf_g, w_in, mods):
    NR, NW = 6, 2
    WHALF = IN_COLS // 2
    NC, NWC = 8 * KC, 2 * KC
    vectors = [(w_ada, b_ada, v * D, {1: ln1_g, 4: ln2_g}.get(v)) for v in range(6)] + [
        (w_adaf, b_adaf, 0, None), (w_adaf, b_adaf, D, lnf_g)]
    scales = [v for v in range(8) if vectors[v][3] is not None]
    with ExitStack() as ctx:
        m = Memory(nc, ctx, "mod")
        ring = m.sb("ring", [P, NR, D])
        wraw = m.sb("wraw", [P, NW, WHALF])
        c_sb = m.sb("c", [2, D])
        cT = m.sb("cT", [P, KC, 2])
        ident = m.sb("ident", [2, 2])
        bias, norm_w, row = m.sb("bias", [2, 2, D]), m.sb("norm_w", [2, D]), m.sb("row", [2, 2, D])
        pc = m.ps("pc")
        pm = [m.ps(f"pm{i}", [2, D]) for i in range(2)]
        names = ("c_loaded", "silued", "id_made", "cT_ready", "cT_copied", "ring_used", "hi_ready", "lo_ready", "row_ready",
                 "scaled", "norm_w_loaded")
        (c_loaded, silued, id_made, cT_ready, cT_copied, ring_used, hi_ready, lo_ready, row_ready,
         scaled, norm_w_loaded) = (m.sem(n) for n in names)
        ring_loaded, raw_loaded = m.sems("ring_loaded", NR), m.sems("raw_loaded", NW)
        bias_loaded, row_stored = m.sems("bias_loaded", 2), m.sems("row_stored", 2)
        block = ctx.enter_context(nc.Block())

        @block.sync
        def _(sp):
            sp.dma_start(c_sb[:], c_all).then_inc(c_loaded, 16)

            def load_w_in(n):
                k, half = divmod(n, 2)
                if n >= NW:
                    sp.wait_ge(lo_ready, n - NW + 1)
                sp.dma_start(wraw[:, n % NW, :], w_in.rearrange("(p k) n -> p k n", k=KC)[:, k, half * WHALF:(half + 1) * WHALF]
                             ).then_inc(raw_loaded[n % NW], 16)

            for n in range(NC):
                v, k = divmod(n, KC)
                w, _, col, _ = vectors[v]
                if n >= NR:
                    sp.wait_ge(ring_used, n - NR + 1)
                sp.dma_start(ring[:, n % NR, :], w.rearrange("(p k) n -> p k n", k=KC)[:, k, col:col + D]
                             ).then_inc(ring_loaded[n % NR], 16)
                if n % (NC // NWC) == 0:
                    load_w_in(n // (NC // NWC))

        @block.gpsimd
        def _(pool):
            def load_bias(v):
                _, b, col, norm = vectors[v]
                if v >= 2:
                    pool.wait_ge(row_ready, v - 1)
                pool.dma_start(bias[:, v % 2, :], b[col:col + D].unsqueeze(0).to_broadcast([2, D])).then_inc(bias_loaded[v % 2], 16)
                if norm is not None:
                    if scales.index(v):
                        pool.wait_ge(scaled, scales.index(v))
                    pool.dma_start(norm_w[:], norm[:].unsqueeze(0).to_broadcast([2, D])).then_inc(norm_w_loaded, 16)

            load_bias(0)
            load_bias(1)
            pool.memset(ident[:], 0.0).then_inc(id_made, 1)
            pool.wait_ge(id_made, 1)
            pool.affine_select(out=ident[:], in_=ident[:], compare_op=ALU.not_equal, fill=1.0, base=0,
                               pattern=[[-1, 2]], channel_multiplier=1).then_inc(id_made, 1)
            for v in range(8):
                if v in scales:
                    pool.wait_ge(scaled, scales.index(v) + 1)
                else:
                    pool.wait_ge(row_ready, v + 1)
                pool.dma_start(mods[:, v, :], row[:, v % 2, :]).then_inc(row_stored[v % 2], 16)
                if v + 2 < 8:
                    load_bias(v + 2)
            for b in range(2):
                pool.wait_ge(row_stored[b], 16 * 4)

        @block.scalar
        def _(act):
            act.wait_ge(c_loaded, 16)
            act.activation(row[:, 0, :], c_sb[:], ACT.Silu).then_inc(silued, 1)
            for n in range(NWC):
                k, half = divmod(n, 2)
                act.wait_ge(raw_loaded[n % NW], 16 * (n // NW + 1))
                act.copy(w_hi[:, k, half * WHALF:(half + 1) * WHALF], wraw[:, n % NW, :]).then_inc(hi_ready, 1)

        @block.vector
        def _(dve):
            dve.wait_ge(cT_ready, 1)
            dve.tensor_copy(cT[:].rearrange("p k s -> p (k s)"), pc[:, 0:2 * KC]).then_inc(cT_copied, 1)

            def split_lo(n):
                k, half = divmod(n, 2)
                cols = slice(half * WHALF, (half + 1) * WHALF)
                dve.wait_ge(hi_ready, n + 1)
                dve.tensor_tensor(w_lo[:, k, cols], wraw[:, n % NW, :], w_hi[:, k, cols].bitcast(F32),
                                  ALU.subtract).then_inc(lo_ready, 1)

            for v in range(8):
                for n in range(v * NWC // 8, (v + 1) * NWC // 8):
                    split_lo(n)
                dve.wait_ge(ring_used, (v + 1) * KC)
                dve.wait_ge(bias_loaded[v % 2], 16 * (v // 2 + 1))
                if v >= 2:
                    dve.wait_ge(row_stored[v % 2], 16 * (v // 2))
                dve.tensor_tensor(row[:, v % 2, :], pm[v % 2][:], bias[:, v % 2, :], ALU.add).then_inc(row_ready, 1)
                if v in scales:
                    dve.wait_ge(row_ready, v + 1)
                    dve.wait_ge(norm_w_loaded, 16 * (scales.index(v) + 1))
                    dve.scalar_tensor_tensor(out=row[:, v % 2, :], in0=row[:, v % 2, :], scalar=1.0, in1=norm_w[:], op0=ALU.add,
                                             op1=ALU.mult).then_inc(scaled, 1)

        @block.tensor
        def _(pe):
            pe.wait_ge(silued, 1)
            pe.wait_ge(id_made, 2)
            for k in range(KC):
                mm = pe.transpose(pc[:, 2 * k:2 * k + 2], row[:, 0, k:D:KC], ident[:])
            mm.then_inc(cT_ready, 1)
            pe.wait_ge(cT_copied, 1)
            for n in range(NC):
                v, k = divmod(n, KC)
                pe.wait_ge(ring_loaded[n % NR], 16 * (n // NR + 1))
                if v >= 2 and k == 0:
                    pe.wait_ge(row_ready, v - 1)
                for j in range(D // HALF):
                    mm = pe.matmul(pm[v % 2][:, j * HALF:(j + 1) * HALF], cT[:, k, :], ring[:, n % NR, j * HALF:(j + 1) * HALF],
                                   start=(k == 0), stop=(k == KC - 1))
                mm.then_inc(ring_used, 1)


def stage_projection(nc, w_hi, w_lo, x_all, mods, rope_tab, qn_g, kn_g, q_dram, k_dram, v_dram):
    with ExitStack() as ctx:
        m = Memory(nc, ctx, "prj")
        x = m.sb("x", [P, 2, D])
        rope = m.sb("rope", [P, 2, 160])
        h = m.sb("h", [P, D])
        hT_hi, hT_lo = m.sb("hT_hi", [P, 2, KC, P], F32R), m.sb("hT_lo", [P, 2, KC, P], F32R)
        stage = m.sb("stage", [P, IN_COLS])
        a1, sh1 = m.sb("a1", [P, D]), m.sb("sh1", [P, D])
        sq, t1 = m.sb("sq", [P, 512]), m.sb("t1", [P, 512])
        t1b = m.sb("t1b", [P, 128])
        gqk = m.sb("gqk", [P, 2, HD])
        ident = m.sb("ident", [P, P])
        ss, ms, rstd = m.sb("ss", [P, 2]), m.sb("ms", [P, 2]), m.sb("rstd", [P, 2])
        ss8, ms8, rs8 = m.sb("ss8", [P, 8]), m.sb("ms8", [P, 8]), m.sb("rs8", [P, 8])
        neghalf, eps = m.sb("neghalf", [P, 8]), m.sb("eps", [P, 8])
        tp = m.ps("tp", (P, D))
        pp = [m.ps(f"pp{n}") for n in range(5)]
        names = ("const_made", "mods_loaded", "ss_ready", "ms_ready", "rstd_ready", "h_mul", "h_ready", "tp_ready",
                 "hi_ready", "hT_ready", "reduced", "ms8_ready", "rs8_ready", "dve_own")
        (const_made, mods_loaded, ss_ready, ms_ready, rstd_ready, h_mul, h_ready, tp_ready, hi_ready, hT_ready, reduced,
         ms8_ready, rs8_ready, dve_own) = (m.sem(n) for n in names)
        x_loaded, rope_loaded = m.sems("x_loaded", 2), m.sems("rope_loaded", 2)
        proj_ready, copied, squared = m.sems("proj_ready", 5), m.sems("copied", 5), m.sems("squared", 5)
        staged, stored = m.sems("staged", 5), m.sems("stored", 5)
        block = ctx.enter_context(nc.Block())
        bank_read = copied[:3] + squared[3:]
        LOOPS, LAST = 3, NT - 1

        def tiles(eng, body, steps=None, per=None):
            with eng.Fori(0, LOOPS) as i:
                if steps:
                    steps.enter(i, per)
                for b in range(2):
                    body(2 * i + b, b, i, 0, False)
                if steps:
                    steps.leave(LOOPS)
            for t in range(2 * LOOPS, NT):
                body(t, t % 2, t // 2, int(t + 1 >= NT0), t == LAST)

        def order(last):
            return (3, 4, 0, 1, 2) if last else (0, 1, 2, 3, 4)

        stores = [(q_dram, 0, 0, 512), (k_dram, 0, 512, 1024), (v_dram, 0, 1024, 1536), (q_dram, 512, 1536, 2048)]

        @block.sync
        def _(sp):
            def load_x(t, b):
                sp.dma_start(x[:, b, :], x_all[bass.ts(t, P), :]).then_inc(x_loaded[b], 16)

            def load_rope(t, b):
                sp.dma_start(rope[:, b, :], rope_tab[bass.ts(t, P), :]).then_inc(rope_loaded[b], 16)

            def load_mods(s):
                sp.dma_start(sh1[:], mods[s, 0, :].unsqueeze(0).to_broadcast([P, D])).then_inc(mods_loaded, 16)
                sp.dma_start(a1[:], mods[s, 1, :].unsqueeze(0).to_broadcast([P, D])).then_inc(mods_loaded, 16)

            load_x(0, 0)
            load_mods(0)
            sp.dma_start(gqk[:, 0, :], qn_g[:].unsqueeze(0).to_broadcast([P, HD])).then_inc(mods_loaded, 16)
            sp.dma_start(gqk[:, 1, :], kn_g[:].unsqueeze(0).to_broadcast([P, HD])).then_inc(mods_loaded, 16)
            load_rope(0, 0)
            load_x(1, 1)
            load_rope(1, 1)

            def body(t, b, u, s_next, last):
                peeled = isinstance(t, int)
                if not peeled or t + 2 < NT:
                    sp.wait_ge(h_ready, t + 1)
                    load_x(t + 2, b)
                if peeled and t == NT0 - 2:
                    sp.wait_ge(h_ready, NT0)
                    load_mods(1)
                for n in order(last):
                    if n == 4:
                        sp.wait_ge(staged[4], t + 2)
                        sp.dma_start(k_dram[bass.ts(t, P), WA:WA + 128], stage[:, 2048:2176]).then_inc(stored[4], 16)
                        sp.dma_start(v_dram[bass.ts(t, P), WA:WA + 128], stage[:, 2176:2304]).then_inc(stored[4], 16)
                        continue
                    dst, c, lo, hi = stores[n]
                    if n == 2:
                        sp.wait_ge(copied[n], t + 2)
                    else:
                        sp.wait_ge(staged[n], t + 1)
                    sp.dma_start(dst[bass.ts(t, P), c:c + hi - lo], stage[:, lo:hi]).then_inc(stored[n], 16)
                if not peeled or t + 2 < NT:
                    load_rope(t + 2, b)

            tiles(sp, body)
            for n in range(4):
                sp.wait_ge(stored[n], 16 * (NT + 1))
            sp.wait_ge(stored[4], 32 * (NT + 1))

        @block.gpsimd
        def _(pool):
            pool.memset(neghalf[:], -0.5)
            pool.memset(eps[:], EPS)
            make_identity(nc, pool, ident, const_made)

            def rstd_of(t, b):
                pool.wait_ge(ss_ready, t + 1)
                pool.tensor_tensor(ms[:, b:b + 1], ss[:, b:b + 1], eps[:, 0:1], ALU.add).then_inc(ms_ready, 1)
                pool.wait_ge(ms_ready, t + 1)
                pool.tensor_tensor(rstd[:, b:b + 1], ms[:, b:b + 1], neghalf[:, 0:1], ALU.pow).then_inc(rstd_ready, 1)

            rstd_of(0, 0)

            def body(t, b, u, s_next, last):
                if not last:
                    rstd_of(t + 1, 1 - b)
                for j in range(2):
                    w = (8, NKVB)[j]
                    pool.wait_ge(reduced, 2 * t + j + 1)
                    pool.tensor_tensor(ms8[:, 0:w], ss8[:, 0:w], eps[:, 0:w], ALU.add).then_inc(ms8_ready, 1)
                    pool.wait_ge(ms8_ready, 2 * t + j + 1)
                    pool.tensor_tensor(rs8[:, 0:w], ms8[:, 0:w], neghalf[:, 0:w], ALU.pow).then_inc(rs8_ready, 1)

            tiles(pool, body)

        @block.scalar
        def _(act):
            def square(t, b, u):
                act.wait_ge(x_loaded[b], (u + 1) * 16)
                if not isinstance(t, int) or t:
                    act.wait_ge(tp_ready, t)
                act.activation(h[:], x[:, b, :], ACT.Square, scale=D ** -0.5, accum_out=ss[:, b:b + 1]).then_inc(ss_ready, 1)

            def split_hi(t, b):
                act.wait_ge(tp_ready, t + 1)
                act.copy(hT_hi[:, b].rearrange("p k t -> p (k t)")[:, 0:HALF], tp[:, 0:HALF])
                act.copy(hT_hi[:, b].rearrange("p k t -> p (k t)")[:, HALF:D], tp[:, HALF:D]).then_inc(hi_ready, 1)

            square(0, 0, 0)
            split_hi(0, 0)

            def body(t, b, u, s_next, last):
                if not last:
                    square(t + 1, 1 - b, u + b)
                for n in order(last):
                    lo, hi = BLOCKS[n]
                    act.wait_ge(proj_ready[n], t + 1)
                    act.wait_ge(stored[n], (t + 1) * (16 if n < 4 else 32))
                    act.copy(stage[:, lo:hi], pp[n][:, 0:hi - lo]).then_inc(copied[n], 1)
                    if n >= 3:
                        w = (512, 128)[n - 3]
                        act.wait_ge(staged[7 - n], t + 1)
                        act.activation(sq[:, 0:w], pp[n][:, 0:w], ACT.Square, scale=HD ** -0.5).then_inc(squared[n], 1)
                    if n == 2 and not last:
                        split_hi(t + 1, 1 - b)

            for n in range(5):
                act.sem_inc(stored[n], 16 if n < 4 else 32)
            act.sem_inc(staged[4], 1)
            tiles(act, body)

        @block.vector
        def _(dve):
            own = Steps(dve, dve_own)

            def make_h(t, b, u, s):
                dve.wait_ge(rstd_ready, t + 1)
                dve.wait_ge(mods_loaded, 64 + 32 * s)
                dve.scalar_tensor_tensor(out=h[:], in0=x[:, b, :], scalar=rstd[:, b:b + 1], in1=a1[:], op0=ALU.mult,
                                         op1=ALU.mult).then_inc(h_mul, 1)
                dve.wait_ge(h_mul, t + 1)
                dve.tensor_tensor(h[:], h[:], sh1[:], ALU.add).then_inc(h_ready, 1)

            def split_lo(t, b):
                dve.wait_ge(hi_ready, t + 1)
                dve.tensor_tensor(hT_lo[:, b].rearrange("p k t -> p (k t)"), tp[:],
                                  hT_hi[:, b].rearrange("p k t -> p (k t)").bitcast(F32), ALU.subtract).then_inc(hT_ready, 1)

            def rope_a(t, b, u, n, last):
                v = stage[:, BLOCKS[n][0]:BLOCKS[n][1]].rearrange("p (h d) -> p h d", d=HD)
                a, c = (z[:, 0:128].rearrange("p (h d) -> p h d", d=16) for z in (t1, t1b))
                cos = rope[:, b, 0:16].unsqueeze(1).to_broadcast([P, 8, 16])
                sin = rope[:, b, 16:32].unsqueeze(1).to_broadcast([P, 8, 16])
                dve.wait_ge(copied[n], t + 2)
                dve.wait_ge(staged[(4, 0)[n]], t + 1 + int(last and n == 0))
                dve.wait_ge(rope_loaded[b], (u + 1) * 16)
                dve.tensor_tensor(a, v[:, :, 0:16], cos, ALU.mult)
                dve.tensor_tensor(c[:, :, 0:8], v[:, :, 8:16], sin[:, :, 0:8], ALU.mult)
                own.did(dve.tensor_tensor(c[:, :, 8:16], v[:, :, 0:8], sin[:, :, 8:16], ALU.mult))
                own.wait()
                dve.tensor_tensor(v[:, :, 0:16], a, c, ALU.add).then_inc(staged[n], 1)

            def norm_b(t, b, u, n, last):
                j = n - 3
                H = (8, NKVB)[j]
                W = H * HD
                v = stage[:, BLOCKS[n][0]:BLOCKS[n][0] + W]
                v3 = v.rearrange("p (h d) -> p h d", d=HD)
                dve.wait_ge(squared[n], t + 2)
                dve.tensor_reduce(ss8[:, 0:H], sq[:, 0:W].rearrange("p (h d) -> p h d", d=HD), AX.X, ALU.add).then_inc(reduced, 1)
                dve.wait_ge(rs8_ready, 2 * t + j + 1)
                dve.wait_ge(staged[3 if j else 4 if last else 1], t + 1)
                own.did(dve.tensor_tensor(v3, v3, rs8[:, 0:H].unsqueeze(2).to_broadcast([P, H, HD]), ALU.mult))
                own.wait()
                own.did(dve.tensor_tensor(v3, v3, gqk[:, j, :].unsqueeze(1).to_broadcast([P, H, HD]), ALU.mult))
                own.wait()
                cos = rope[:, b, 32:96].unsqueeze(1).to_broadcast([P, H, HD])
                sin = rope[:, b, 96:160].rearrange("p (a c d) -> p a c d", a=2, c=2)
                v5 = v.rearrange("p (h a c d) -> p h a c d", a=2, c=2, d=16)
                s5 = sq[:, 0:W].rearrange("p (h a c d) -> p h a c d", a=2, c=2, d=16)
                dve.tensor_tensor(t1[:, 0:W].rearrange("p (h d) -> p h d", d=HD), v3, cos, ALU.mult)
                for c in range(2):
                    step = dve.tensor_tensor(s5[:, :, :, c, :], v5[:, :, :, 1 - c, :],
                                             sin[:, :, c, :].unsqueeze(1).to_broadcast([P, H, 2, 16]), ALU.mult)
                own.did(step)
                own.wait()
                dve.tensor_tensor(v, t1[:, 0:W], sq[:, 0:W], ALU.add).then_inc(staged[n], 1)

            make_h(0, 0, 0, 0)
            split_lo(0, 0)

            def body(t, b, u, s_next, last):
                if not last:
                    make_h(t + 1, 1 - b, u + b, s_next)
                for n in order(last):
                    if n != 2:
                        (norm_b if n >= 3 else rope_a)(t, b, u, n, last)
                    elif not last:
                        split_lo(t + 1, 1 - b)

            tiles(dve, body, own, 2 * 8)

        @block.tensor
        def _(pe):
            def transposes(t):
                pe.wait_ge(h_ready, t + 1)
                if not isinstance(t, int) or t:
                    pe.wait_ge(hT_ready, t)
                for k in range(KC):
                    mm = pe.transpose(tp[:, k * P:(k + 1) * P], h[:, k:D:KC], ident[:])
                mm.then_inc(tp_ready, 1)

            pe.wait_ge(const_made, 2)
            transposes(0)
            for n in range(5):
                pe.sem_inc(bank_read[n], 1)

            def body(t, b, u, s_next, last):
                pe.wait_ge(hT_ready, t + 1)
                for n in order(last):
                    lo, hi = BLOCKS[n]
                    pe.wait_ge(bank_read[n], t + 1)
                    for k in range(KC):
                        for a, w in ((hT_hi, w_hi), (hT_hi, w_lo), (hT_lo, w_hi)):
                            mm = pe.matmul(pp[n][:, 0:hi - lo], a[:, b, k, :], w[:, k, lo:hi],
                                           start=(k == 0 and w is w_hi and a is hT_hi),
                                           stop=(k == KC - 1 and a is hT_lo))
                    mm.then_inc(proj_ready[n], 1)
                    if n == 2 and not last:
                        transposes(t + 1)

            tiles(pe, body)


def stage_keys(nc, kT, v_sb, k_dram, v_dram):
    with ExitStack() as ctx:
        m = Memory(nc, ctx, "key")
        KW = NKH * HD
        raw = m.sb("raw", [P, NT, KW])
        parts = m.sb("parts", [P, 2, NKH, 2, HD], F32R)
        ident_f, ident = m.sb("ident_f", [P, P]), m.sb("ident", [P, P], F32R)
        tp = [[m.ps(f"tp{b}_{i}", (P, 512)) for i in range(3)] for b in range(2)]
        HEADS = [(0, 4), (4, 8), (8, 10)]
        id_made, id_ready, hi_ready, lo_ready, v_loaded = (m.sem(n) for n in ("id_made", "id_ready", "hi_ready", "lo_ready", "v_loaded"))
        raw_loaded, tp_ready, kept = m.sems("raw_loaded", 2), m.sems("tp_ready", 3), m.sems("kept", 3)
        block = ctx.enter_context(nc.Block())

        def tiles(eng, body):
            body(0, 0)
            with eng.Fori(0, NT // 2 - 1) as i:
                body(2 * i + 1, 1)
                body(2 * i + 2, 0)
            body(NT - 1, 1)

        def last(t):
            return isinstance(t, int) and t == NT - 1


        @block.sync
        def _(sp):
            for n, (t0, t1) in enumerate(((0, 2), (2, NT))):
                sp.dma_start(raw[:, t0:t1, :], k_dram[t0 * P:t1 * P, :].rearrange("(t p) n -> p t n", p=P)).then_inc(raw_loaded[n], 16)
            sp.dma_start(v_sb[:], v_dram.rearrange("(t p) n -> p t n", p=P)).then_inc(v_loaded, 16)
            sp.wait_ge(v_loaded, 16)

        @block.gpsimd
        def _(pool):
            make_identity(nc, pool, ident_f, id_made)

        @block.scalar
        def _(act):
            def split_hi(t, b):
                act.wait_ge(raw_loaded[0 if isinstance(t, int) and t < 2 else 1], 16)
                act.wait_ge(tp_ready[2], t + 1)
                act.copy(parts[:, b, :, 0, :], raw[:, bass.ds(t, 1), :].rearrange("p t (h d) -> p (t h) d", d=HD)).then_inc(hi_ready, 1)

            act.sem_inc(tp_ready[2], 2)
            split_hi(0, 0)

            def body(t, b):
                if not last(t):
                    split_hi(t + 1, 1 - b)
                for n in (0, 2):
                    h0, h1 = HEADS[n]
                    act.wait_ge(tp_ready[n], t + (3 if n == 2 else 1))
                    act.copy(kT[:, h0:h1, bass.ds(t * P, P)],
                             tp[b][n][:, 0:(h1 - h0) * P].rearrange("p (h t) -> p h t", t=P)).then_inc(kept[n], 1)

            tiles(act, body)

        @block.vector
        def _(dve):
            dve.wait_ge(id_made, 2)
            dve.tensor_copy(ident[:], ident_f[:]).then_inc(id_ready, 1)

            def split_lo(t, b):
                dve.wait_ge(hi_ready, t + 1)
                dve.tensor_tensor(parts[:, b, :, 1, :], raw[:, bass.ds(t, 1), :].rearrange("p t (h d) -> p (t h) d", d=HD),
                                  parts[:, b, :, 0, :].bitcast(F32), ALU.subtract).then_inc(lo_ready, 1)

            split_lo(0, 0)

            def body(t, b):
                if not last(t):
                    split_lo(t + 1, 1 - b)
                dve.wait_ge(tp_ready[1], t + 1)
                dve.tensor_copy(kT[:, 4:8, bass.ds(t * P, P)],
                                tp[b][1][:].rearrange("p (h t) -> p h t", t=P)).then_inc(kept[1], 1)

            tiles(dve, body)

        @block.tensor
        def _(pe):
            pe.wait_ge(id_ready, 1)
            for n in range(3):
                pe.sem_inc(kept[n], 2)
            with pe.Fori(0, NT // 2) as i:
                for b in range(2):
                    t = 2 * i + b
                    pe.wait_ge(lo_ready, t + 1)
                    for n, (h0, h1) in enumerate(HEADS):
                        pe.wait_ge(kept[n], t + 1)
                        for h in range(h0, h1):
                            mm = pe.transpose(tp[b][n][:, (h - h0) * P:(h - h0 + 1) * P].bitcast(F32R),
                                              parts[:, b, h].rearrange("p a d -> p (a d)"), ident[:])
                        mm.then_inc(tp_ready[n], 1)


def stage_attention(nc, kT, v_sb, q_dram, count_tab, o_dram, y_dram):
    NH = NHA + NHB
    with ExitStack() as ctx:
        m = Memory(nc, ctx, "att")
        q = m.sb("q", [P, 2, NH * HD])
        parts = m.sb("parts", [P, NH, 2, 2, HD], F32R)
        qT = m.sb("qT", [P, 2, NH, 2, P], F32R)
        counts = m.sb("counts", [P, 2, S0])
        s = m.sb("s", [P, 2, S0])
        prob = m.sb("prob", [P, 2, S0])
        pT = m.sb("pT", [P, 2, 2, 4, P])
        o = m.sb("o", [P, 2, WA])
        osq = m.sb("osq", [P, WA])
        zero, zeros, warm = m.sb("zero", [P, 1]), m.sb("zeros", [P, D]), m.sb("warm", [P, 1])
        neg_max = m.sb("neg_max", [P, 2])
        den, rden = m.sb("den", [P, NH]), m.sb("rden", [P, NH])
        mso, rso = m.sb("mso", [P, 2]), m.sb("rso", [P, 2])
        neghalf = m.sb("neghalf", [P, 1])
        ident_f, ident = m.sb("ident_f", [P, P]), m.sb("ident", [P, P], F32R)
        sc = [m.ps(f"sc{i}", (P, S0)) for i in range(2)]
        tp = [m.ps(f"tp{i}") for i in range(2)]
        op, qp = m.ps("op"), m.ps("qp")
        names = ("id_made", "id_ready", "consts", "hi_ready", "parts_ready", "qT_kept", "qp_ready", "scores_ready",
                 "masked", "exped", "pv_ready", "o_read", "rden_ready", "mso_ready", "rso_ready", "normed", "mask_begun", "load_begun", "carried",
                 "zeros_made", "zeros_stored")
        (id_made, id_ready, consts, hi_ready, parts_ready, qT_kept, qp_ready, scores_ready, masked, exped, pv_ready,
         o_read, rden_ready, mso_ready, rso_ready, normed, mask_begun, load_begun,
         carried, zeros_made, zeros_stored) = (m.sem(n) for n in names)
        first_hi, first_parts = m.sem("first_hi"), m.sem("first_parts")
        q_loaded, counts_loaded = m.sems("q_loaded", 2), m.sems("counts_loaded", 2)
        tp_ready, pT_kept, stored = m.sems("tp_ready", 2), m.sems("pT_kept", 2), m.sems("stored", 2)
        block = ctx.enter_context(nc.Block())
        LOOPS = 3

        def keys(t):
            return (0, S0, 0) if not isinstance(t, int) or t < NT0 else (S0, S1, NT0)

        def tiles(eng, body):
            with eng.Fori(0, LOOPS) as i:
                for b in range(2):
                    body(2 * i + b, b, i, 2 * i + b + 1)
            for t in range(2 * LOOPS, NT):
                body(t, t % 2, t // 2, t + 1 if t + 1 < NT else None)

        FIRST = (((0, 2), True), ((2, NH), False))

        def q_bank(t, pair):
            return op if isinstance(t, int) and t == 0 and pair % 2 else qp

        def ahead(t, nxt, j, n):
            if j + n < NH:
                return t, j + n
            return None if nxt is None else (nxt, j + n - NH)

        @block.sync
        def _(sp):
            def load_q(t, b):
                sp.dma_start(q[:, b, :], q_dram[bass.ts(t, P), :]).then_inc(q_loaded[b], 16)

            def load_counts(t, b):
                _, S, v0 = keys(t)
                sp.dma_start(counts[:, b, 0:S], count_tab[:, bass.ds(S0 - P - (t - v0) * P, S)]).then_inc(counts_loaded[b], 16)

            load_q(0, 0)
            load_counts(0, 0)
            load_q(1, 1)
            load_counts(1, 1)
            sp.wait_ge(zeros_made, 1)
            sp.dma_start(y_dram[NE * P:NBLK * P, :].rearrange("(b p) d -> p b d", p=P), zeros[:].unsqueeze(1).to_broadcast([P, NOV, D])
                         ).then_inc(zeros_stored, 16)

            def body(t, b, u, nxt):
                more = not isinstance(t, int) or t + 2 < NT
                if more:
                    sp.wait_ge(masked, NH * t + NHA)
                    sp.sem_inc(load_begun, 1)
                    sp.wait_ge(parts_ready, t + 1)
                    sp.sem_inc(load_begun, 1)
                    load_q(t + 2, b)
                    load_counts(t + 2, b)
                for g in range(2):
                    sp.wait_ge(normed, 2 * t + g + 1)
                    sp.dma_start(o_dram[bass.ts(t, P), g * WA:(g + 1) * WA], o[:, g, :]).then_inc(stored[g], 16)

            tiles(sp, body)
            for g in range(2):
                sp.wait_ge(stored[g], 16 * (NT + 1))
            sp.wait_ge(zeros_stored, 16)

        @block.gpsimd
        def _(pool):
            pool.memset(zero[:], 0.0).then_inc(consts, 1)
            pool.memset(neghalf[:], -0.5).then_inc(consts, 1)
            make_identity(nc, pool, ident_f, id_made)
            pool.memset(zeros[:], 0.0).then_inc(zeros_made, 1)
            pool.wait_ge(consts, 2)

            def split(t, b, u):
                pool.wait_ge(q_loaded[b], (u + 1) * 16)
                pool.wait_ge(qp_ready, t * (NH // 2))
                pool.sem_inc(carried, 1)
                v = q[:, b, :].rearrange("p (h d) -> p h d", d=HD)
                for c in range(2):
                    step = pool.tensor_copy(parts[:, :, 0, c, :], v)
                step.then_inc(hi_ready, 1)
                pool.wait_ge(hi_ready, t + 1)
                for c in range(2):
                    step = pool.tensor_tensor(parts[:, :, 1, c, :], v, parts[:, :, 0, c, :].bitcast(F32), ALU.subtract)
                step.then_inc(parts_ready, 1)

            def norm_o(t, g):
                n = 2 * t + g + 1
                pool.wait_ge(mso_ready, n)
                pool.tensor_tensor(rso[:, g:g + 1], mso[:, g:g + 1], neghalf[:], ALU.pow).then_inc(rso_ready, 1)
                pool.wait_ge(rso_ready, n)
                pool.sem_inc(carried, 1)
                pool.tensor_scalar(o[:, g, :], o[:, g, :], rso[:, g:g + 1], None, ALU.mult).then_inc(normed, 1)

            def body(t, b, u, nxt):
                if nxt is not None:
                    split(t + 1, 1 - b, u + b)
                for g in range(2):
                    norm_o(t, g)

            tiles(pool, body)

        @block.scalar
        def _(act):
            def keep_qT(t, b, pair):
                act.wait_ge(qp_ready, t * (NH // 2) + pair + 1)
                act.copy(qT[:, b, 2 * pair:2 * pair + 2].rearrange("p h c t -> p (h c t)"), q_bank(t, pair)[:]).then_inc(qT_kept, 1)

            def exp(t, j):
                n, S = NH * t + j + 1, keys(t)[1]
                act.wait_ge(masked, n)
                act.wait_ge(tp_ready[1], n)
                act.activation(prob[:, j % 2, 0:S], s[:, j % 2, 0:S], ACT.Exp, bias=neg_max[:, j % 2:j % 2 + 1], scale=-1.0,
                               accum_out=den[:, j:j + 1]).then_inc(exped, 1)

            def keep_pT(t, j):
                c = keys(t)[1] // (2 * P)
                act.wait_ge(tp_ready[1], NH * t + j + 3)
                act.copy(pT[:, j % 2, 1, 0:c].rearrange("p c t -> p (c t)"), tp[1][:, 0:c * P]).then_inc(pT_kept[1], 1)

            act.sem_inc(tp_ready[1], 2)
            for g in range(2):
                act.sem_inc(stored[g], 16)
            act.wait_ge(consts, 2)
            act.activation(warm[:], zero[:], ACT.Exp)
            act.wait_ge(q_loaded[0], 16)
            for (h0, h1), ahead_of_rest in FIRST:
                for c in range(2):
                    step = act.copy(parts[:, h0:h1, 0, c, :], q[:, 0, h0 * HD:h1 * HD].rearrange("p (h d) -> p h d", d=HD))
                step.then_inc(first_hi if ahead_of_rest else hi_ready, 1)
            for pair in range(NH // 2):
                keep_qT(0, 0, pair)
            exp(0, 0)

            def body(t, b, u, nxt):
                for j in range(NH):
                    nx = ahead(t, nxt, j, 1)
                    if nx:
                        exp(*nx)
                    keep_pT(t, j)
                    if j >= NH // 2 and nxt is not None:
                        keep_qT(t + 1, 1 - b, j - NH // 2)

            tiles(act, body)

        @block.vector
        def _(dve):
            dve.wait_ge(id_made, 2)
            dve.tensor_copy(ident[:], ident_f[:]).then_inc(id_ready, 1)
            dve.sem_inc(exped, 2)
            dve.wait_ge(consts, 2)
            for (h0, h1), ahead_of_rest in FIRST:
                dve.wait_ge(first_hi if ahead_of_rest else hi_ready, 1)
                for c in range(2):
                    step = dve.tensor_tensor(parts[:, h0:h1, 1, c, :], q[:, 0, h0 * HD:h1 * HD].rearrange("p (h d) -> p h d", d=HD),
                                             parts[:, h0:h1, 0, c, :].bitcast(F32), ALU.subtract)
                step.then_inc(first_parts if ahead_of_rest else parts_ready, 1)

            def mask(t, b, u, j):
                n, S = NH * t + j + 1, keys(t)[1]
                if j == 0:
                    dve.wait_ge(counts_loaded[b], (u + 1) * 16)
                dve.wait_ge(scores_ready, n)
                dve.wait_ge(exped, n)
                dve.sem_inc(mask_begun, 1)
                held = counts[:, b, 0:S] if j < NHA else zero[:].to_broadcast([P, S])
                dve.tensor_tensor_reduce(s[:, j % 2, 0:S], sc[j % 2][:, 0:S], held, -SCALE, 3e38, ALU.add, ALU.min,
                                         neg_max[:, j % 2:j % 2 + 1]).then_inc(masked, 1)

            def keep_pT(t, j):
                c = keys(t)[1] // (2 * P)
                dve.wait_ge(tp_ready[0], NH * t + j + 1)
                dve.tensor_copy(pT[:, j % 2, 0, 0:c].rearrange("p c t -> p (c t)"), tp[0][:, 0:c * P]).then_inc(pT_kept[0], 1)

            def take_o(t, g):
                heads = slice(g * NHA, (g + 1) * NHA)
                n = 2 * t + g + 1
                dve.wait_ge(pv_ready, n)
                dve.reciprocal(rden[:, heads], den[:, heads]).then_inc(rden_ready, 1)
                dve.wait_ge(rden_ready, n)
                dve.wait_ge(stored[g], (t + 1) * 16)
                dve.tensor_tensor(o[:, g, :].rearrange("p (h d) -> p h d", d=HD), op[:].rearrange("p (h d) -> p h d", d=HD),
                                  rden[:, heads].unsqueeze(2).to_broadcast([P, NHA, HD]), ALU.mult).then_inc(o_read, 1)
                dve.wait_ge(o_read, n + 1)
                dve.tensor_tensor_reduce(osq[:], o[:, g, :], o[:, g, :], 1.0 / WA, EPS, ALU.mult, ALU.add, mso[:, g:g + 1]
                                         ).then_inc(mso_ready, 1)

            mask(0, 0, 0, 0)
            mask(0, 0, 0, 1)

            def body(t, b, u, nxt):
                for j in range(NH):
                    nx = ahead(t, nxt, j, 2)
                    if nx:
                        if j + 2 < NH:
                            mask(t, b, u, j + 2)
                        else:
                            mask(t + 1, 1 - b, u + b, j + 2 - NH)
                    keep_pT(t, j)
                    if j == 8:
                        take_o(t, 0)
                take_o(t, 1)

            tiles(dve, body)

        @block.tensor
        def _(pe):
            def q_transposes(t, pair):
                if isinstance(t, int) and t == 0:
                    pe.wait_ge(parts_ready if pair else first_parts, 1)
                elif pair == 0:
                    pe.wait_ge(parts_ready, t + 1)
                n = t * (NH // 2) + pair
                if not isinstance(t, int) or t:
                    pe.wait_ge(qT_kept, n)
                elif pair >= 2:
                    pe.wait_ge(qT_kept, n - 1)
                for h in (0, 1):
                    for c in (0, 1):
                        mm = pe.transpose(q_bank(t, pair)[:, (2 * h + c) * P:(2 * h + c + 1) * P].bitcast(F32R),
                                          parts[:, 2 * pair + h, c].rearrange("p a d -> p (a d)"), ident[:])
                mm.then_inc(qp_ready, 1)

            def scores(t, b, j):
                k0, S, _ = keys(t)
                kh = j if j < NHA else NHA + (j - NHA) // (NHB // NKVB)
                pe.wait_ge(qT_kept, t * (NH // 2) + j // 2 + 1)
                n = NH * t + j - 1
                if not isinstance(n, int) or n > 0:
                    pe.wait_ge(masked, n)
                for c in range(0, S, HALF):
                    w = min(HALF, S - c)
                    for part in (0, 1):
                        mm = pe.matmul(sc[j % 2][:, c:c + w], qT[:, b, j, part, :], kT[:, kh, k0 + c:k0 + c + w],
                                       start=(part == 0), stop=(part == 1))
                mm.then_inc(scores_ready, 1)

            def p_transposes(t, j):
                c = keys(t)[1] // (2 * P)
                pe.wait_ge(exped, NH * t + j + 3)
                for half in (0, 1):
                    pe.wait_ge(pT_kept[half], NH * t + j + 1)
                    for i in range(c):
                        mm = pe.transpose(tp[half][:, i * P:(i + 1) * P], prob[:, j % 2, (half * c + i) * P:(half * c + i + 1) * P],
                                          ident_f[:])
                    mm.then_inc(tp_ready[half], 1)

            def values(t, j):
                _, S, v0 = keys(t)
                c = S // (2 * P)
                h = j % NHA
                col = j * HD if j < NHA else WA + (j - NHA) // (NHB // NKVB) * HD
                if h == 0:
                    pe.wait_ge(o_read, 2 * t + j // NHA + 1)
                for half in (0, 1):
                    pe.wait_ge(pT_kept[half], NH * t + j + 2)
                    for i in range(c):
                        mm = pe.matmul(op[:, h * HD:(h + 1) * HD], pT[:, j % 2, half, i, :],
                                       v_sb[:, v0 + half * c + i, col:col + HD],
                                       start=(half == 0 and i == 0), stop=(half == 1 and i == c - 1))
                if h == NHA - 1:
                    mm.then_inc(pv_ready, 1)

            pe.wait_ge(id_ready, 1)
            pe.sem_inc(pT_kept[0], 1)
            pe.sem_inc(pT_kept[1], 1)
            pe.sem_inc(o_read, 1)
            q_transposes(0, 0)
            scores(0, 0, 0)
            scores(0, 0, 1)
            for pair in range(1, NH // 2):
                q_transposes(0, pair)
            pe.wait_ge(qT_kept, NH // 2)

            def body(t, b, u, nxt):
                for j in range(NH):
                    nx = ahead(t, nxt, j, 2)
                    if nx:
                        scores(nx[0], b if j + 2 < NH else 1 - b, nx[1])
                    p_transposes(t, j)
                    if j >= NH // 2 and nxt is not None:
                        q_transposes(t + 1, j - NH // 2)
                    if j:
                        values(t, j - 1)
                values(t, NH - 1)

            tiles(pe, body)


def stage_output(nc, ring, ring_loaded, w1, w3, logits, o_dram, x_all, mods, w_out, on_a_g, on_b_g, w_rg, b_rg, w_re, b_re,
                 x1, h2_dram):
    NL = NG + NE
    with ExitStack() as ctx:
        m = Memory(nc, ctx, "out")
        w_hi, w_lo = m.sb("w_hi", [P, KC, D], F32R), m.sb("w_lo", [P, KC, D], F32R)
        wraw, o, x = ring[:, 0:KC, :], ring[:, KC:KC + 2, :], ring[:, KC + 2:KC + 4, :]
        gain = m.sb("gain", [P, KC])
        w_r, b_r = m.sb("w_r", [P, KC, NL]), m.sb("b_r", [P, NL])
        oT_hi, oT_lo = m.sb("oT_hi", [P, 2, KC, P], F32R), m.sb("oT_lo", [P, 2, KC, P], F32R)
        g1, a2, sh2 = m.sb("g1", [P, D]), m.sb("a2", [P, D]), m.sb("sh2", [P, D])
        h2 = m.sb("h2", [P, D])
        sq, h2T = m.sb("sq", [P, D]), m.sb("h2T", [P, KC, P])
        ss, ms, rstd = m.sb("ss", [P, 1]), m.sb("ms", [P, 1]), m.sb("rstd", [P, 1])
        neghalf, eps = m.sb("neghalf", [P, 1]), m.sb("eps", [P, 1])
        ident = m.sb("ident", [P, P])
        tp, tp2 = m.ps("tp", (P, D)), m.ps("tp2", (P, D))
        yp = [m.ps(f"yp{i}") for i in range(2)]
        lp = m.ps("lp")
        names = ("id_made", "consts", "w_consts", "hi_ready", "lo_ready", "mods_loaded", "tp_ready", "oT_hi_ready", "oT_ready",
                 "gated", "x1_ready", "ss_ready", "ms_ready", "rstd_ready", "h2_mul", "h2_ready", "tp2_ready", "h2T_ready",
                 "logits_ready", "logits_kept", "carried", "gain_loaded", "h2_stored")
        (id_made, consts, w_consts, hi_ready, lo_ready, mods_loaded, tp_ready, oT_hi_ready, oT_ready, gated, x1_ready, ss_ready,
         ms_ready, rstd_ready, h2_mul, h2_ready, tp2_ready, h2T_ready, logits_ready, logits_kept, carried,
         gain_loaded, h2_stored
         ) = (m.sem(n) for n in names)
        raw_loaded, o_loaded, x_loaded = m.sems("raw_loaded", KC), m.sems("o_loaded", 2), m.sems("x_loaded", 2)
        yp_ready = m.sems("yp_ready", 2)
        block = ctx.enter_context(nc.Block())
        LOOPS = 3

        def tiles(eng, body):
            body(0, 0, 0, 0)
            with eng.Fori(0, LOOPS) as i:
                body(2 * i + 1, 1, i, 0)
                body(2 * i + 2, 0, i + 1, 0)
            for t in range(2 * LOOPS + 1, NT):
                body(t, t % 2, t // 2, int(t >= NT0))

        def is_last(t):
            return isinstance(t, int) and t == NT - 1

        @block.sync
        def _(sp):
            def load(t, b):
                sp.dma_start(o[:, b, :], o_dram[bass.ts(t, P), :]).then_inc(o_loaded[b], 16)
                sp.dma_start(x[:, b, :], x_all[bass.ts(t, P), :]).then_inc(x_loaded[b], 16)

            def load_mods(s):
                for dst, v in ((g1, 2), (sh2, 3), (a2, 4)):
                    sp.dma_start(dst[:], mods[s, v, :].unsqueeze(0).to_broadcast([P, D])).then_inc(mods_loaded, 16)

            half = P // 2
            sp.dma_start(gain[0:half, :], on_a_g.rearrange("(p k) -> p k", k=KC)).then_inc(gain_loaded, 16)
            sp.dma_start(gain[half:P, :], on_b_g.rearrange("(p k) -> p k", k=KC)).then_inc(gain_loaded, 16)
            load(0, 0)
            for k in range(KC):
                sp.dma_start(wraw[:, k, :], w_out.rearrange("(p k) n -> p k n", k=KC)[:, k, :]).then_inc(raw_loaded[k], 16)
            sp.dma_start(w_r[:, :, 0:NG], w_rg.rearrange("(p k) n -> p k n", k=KC)).then_inc(w_consts, 16)
            sp.dma_start(w_r[:, :, NG:NL], w_re.rearrange("(p k) n -> p k n", k=KC)).then_inc(w_consts, 16)
            sp.dma_start(b_r[:, 0:NG], b_rg.unsqueeze(0).to_broadcast([P, NG])).then_inc(w_consts, 16)
            sp.dma_start(b_r[:, NG:NL], b_re.unsqueeze(0).to_broadcast([P, NE])).then_inc(w_consts, 16)
            load_mods(0)
            load(1, 1)

            def body(t, b, u, s):
                if not isinstance(t, int) or t + 2 < NT:
                    sp.wait_ge(x1_ready, t + 1)
                    sp.sem_inc(carried, 1)
                    load(t + 2, b)
                sp.wait_ge(h2_ready, t + 1)
                sp.dma_start(h2_dram[bass.ts(t, P), :], h2[:]).then_inc(h2_stored, 16)
                if isinstance(t, int) and t == NT0 - 1:
                    load_mods(1)

            tiles(sp, body)
            sp.wait_ge(lo_ready, KC)
            sp.wait_ge(tp_ready, NT)
            sp.wait_ge(x1_ready, NT)
            for slot in range(NRAW):
                w, c = (w1, w3, w1)[slot // 4][slot // 8], slot % 4
                sp.dma_start(ring[:, slot, :], w.rearrange("(p k) n -> p k n", k=KC)[:, 2 * c:2 * c + 2, :].rearrange("p k n -> p (k n)")
                             ).then_inc(ring_loaded[slot], 16)
            sp.wait_ge(h2_stored, 16 * (NT + 1))

        @block.gpsimd
        def _(pool):
            make_identity(nc, pool, ident, id_made)
            pool.memset(neghalf[:], -0.5).then_inc(consts, 1)
            pool.memset(eps[:], EPS).then_inc(consts, 1)
            pool.wait_ge(consts, 2)

            def body(t, b, u, s):
                pool.wait_ge(ss_ready, t + 1)
                pool.tensor_tensor(ms[:], ss[:], eps[:], ALU.add).then_inc(ms_ready, 1)
                pool.wait_ge(ms_ready, t + 1)
                pool.tensor_tensor(rstd[:], ms[:], neghalf[:], ALU.pow).then_inc(rstd_ready, 1)

            tiles(pool, body)

        @block.scalar
        def _(act):
            act.wait_ge(gain_loaded, 32)
            for k in range(KC):
                act.wait_ge(raw_loaded[k], 16)
                act.activation(w_hi[:, k, :], wraw[:, k, :], ACT.Copy, scale=gain[:, k:k + 1]).then_inc(hi_ready, 1)
            act.sem_inc(h2_stored, 16)

            def split_hi(t, b):
                act.wait_ge(tp_ready, t + 1)
                for c in (0, HALF):
                    step = act.copy(oT_hi[:, b].rearrange("p k t -> p (k t)")[:, c:c + HALF], tp[:, c:c + HALF])
                step.then_inc(oT_hi_ready, 1)

            def keep_h2T(t):
                act.wait_ge(tp2_ready, t + 1)
                for c in (0, HALF):
                    step = act.copy(h2T[:].rearrange("p k t -> p (k t)")[:, c:c + HALF], tp2[:, c:c + HALF])
                step.then_inc(h2T_ready, 1)

            split_hi(0, 0)

            def body(t, b, u, s):
                if not is_last(t):
                    split_hi(t + 1, 1 - b)
                if not isinstance(t, int) or t:
                    keep_h2T(t - 1)
                act.wait_ge(x1_ready, t + 1)
                act.sem_inc(carried, 1)
                act.activation(sq[:], x1[:, bass.ts(t, D)], ACT.Square, scale=D ** -0.5, accum_out=ss[:]).then_inc(ss_ready, 1)

            tiles(act, body)
            keep_h2T(NT - 1)

        @block.vector
        def _(dve):
            for k in range(KC):
                dve.wait_ge(hi_ready, k + 1)
                dve.scalar_tensor_tensor(out=w_lo[:, k, :], in0=wraw[:, k, :], scalar=gain[:, k:k + 1],
                                         in1=w_hi[:, k, :].bitcast(F32), op0=ALU.mult, op1=ALU.subtract).then_inc(lo_ready, 1)
            dve.sem_inc(logits_kept, 1)

            def split_lo(t, b):
                dve.wait_ge(oT_hi_ready, t + 1)
                dve.tensor_tensor(oT_lo[:, b].rearrange("p k t -> p (k t)"), tp[:],
                                  oT_hi[:, b].rearrange("p k t -> p (k t)").bitcast(F32), ALU.subtract).then_inc(oT_ready, 1)

            def keep_logits(t):
                dve.wait_ge(logits_ready, t + 1)
                dve.tensor_tensor(logits[:, bass.ds(t, 1), :], lp[:, 0:NL].unsqueeze(1), b_r[:].unsqueeze(1), ALU.add
                                  ).then_inc(logits_kept, 1)

            dve.wait_ge(gain_loaded, 32)
            split_lo(0, 0)
            dve.wait_ge(w_consts, 64)

            def body(t, b, u, s):
                n = t + 1
                dve.wait_ge(mods_loaded, 48 * (s + 1))
                for c in range(2):
                    dve.wait_ge(yp_ready[c], n)
                    dve.tensor_tensor(x1[:, bass.ds(t * D + c * HALF, HALF)], yp[c][:], g1[:, c * HALF:(c + 1) * HALF], ALU.mult
                                      ).then_inc(gated, 1)
                    if c == 0 and not is_last(t):
                        split_lo(t + 1, 1 - b)
                dve.wait_ge(x_loaded[b], (u + 1) * 16)
                dve.wait_ge(gated, 2 * n)
                dve.tensor_tensor(x1[:, bass.ts(t, D)], x1[:, bass.ts(t, D)], x[:, b, :], ALU.add).then_inc(x1_ready, 1)
                if not isinstance(t, int) or t:
                    keep_logits(t - 1)
                    dve.wait_ge(tp2_ready, t)
                dve.wait_ge(rstd_ready, n)
                dve.wait_ge(h2_stored, 16 * n)
                dve.scalar_tensor_tensor(out=h2[:], in0=x1[:, bass.ts(t, D)], scalar=rstd[:], in1=a2[:], op0=ALU.mult, op1=ALU.mult
                                         ).then_inc(h2_mul, 1)
                dve.wait_ge(h2_mul, n)
                dve.tensor_tensor(h2[:], h2[:], sh2[:], ALU.add).then_inc(h2_ready, 1)

            tiles(dve, body)
            keep_logits(NT - 1)

        @block.tensor
        def _(pe):
            def transposes(t, b, u):
                pe.wait_ge(o_loaded[b], (u + 1) * 16)
                if not isinstance(t, int) or t:
                    pe.wait_ge(oT_ready, t)
                for k in range(KC):
                    mm = pe.transpose(tp[:, k * P:(k + 1) * P], o[:, b, k:D:KC], ident[:])
                mm.then_inc(tp_ready, 1)

            def turn_h2(t):
                pe.wait_ge(h2_ready, t + 1)
                if not isinstance(t, int) or t:
                    pe.wait_ge(h2T_ready, t)
                for k in range(KC):
                    mm = pe.transpose(tp2[:, k * P:(k + 1) * P], h2[:, k:D:KC], ident[:])
                mm.then_inc(tp2_ready, 1)

            def router(t):
                pe.wait_ge(logits_kept, t + 1)
                pe.wait_ge(h2T_ready, t + 1)
                for k in range(KC):
                    mm = pe.matmul(lp[:, 0:NL], h2T[:, k, :], w_r[:, k, :], start=(k == 0), stop=(k == KC - 1))
                mm.then_inc(logits_ready, 1)

            pe.wait_ge(id_made, 2)
            transposes(0, 0, 0)
            pe.wait_ge(w_consts, 64)
            pe.wait_ge(lo_ready, KC)

            def body(t, b, u, s):
                pe.wait_ge(oT_ready, t + 1)
                for c in range(2):
                    if not isinstance(t, int) or t:
                        pe.wait_ge(gated, 2 * t - 1 + c)
                    for k in range(KC):
                        if c == 1 and k == KC // 2 and (not isinstance(t, int) or t):
                            turn_h2(t - 1)
                        for a, w in ((oT_hi, w_hi), (oT_hi, w_lo), (oT_lo, w_hi)):
                            mm = pe.matmul(yp[c][:], a[:, b, k, :], w[:, k, c * HALF:(c + 1) * HALF],
                                           start=(k == 0 and w is w_hi and a is oT_hi), stop=(k == KC - 1 and a is oT_lo))
                    mm.then_inc(yp_ready[c], 1)
                    if c == 0 and not is_last(t):
                        transposes(t + 1, 1 - b, u + b)
                if not isinstance(t, int) or t:
                    router(t - 1)

            tiles(pe, body)
            turn_h2(NT - 1)
            router(NT - 1)


def stage_route(nc, extra, extra_loaded, w2, w3, logits, gates, slots, tokens, overflow):
    NCH, CONSTS = 2, 12
    NB2 = NBLK + NBLK % 2
    THR = T // P - 1
    with ExitStack() as ctx:
        m = Memory(nc, ctx, "rt")
        rev4, rev8 = m.sb("rev4", [P, NG]), m.sb("rev8", [P, EPG])
        iota_e, iota_b, thr = m.sb("iota_e", [P, NE]), m.sb("iota_b", [P, NOV]), m.sb("thr", [P, THR])
        tok = m.sb("tok", [P, NT])
        upper, ones = m.sb("upper", [P, P], BF16), m.sb("ones", [P, P], BF16)
        iota_p, iota_k, starts = m.sb("iota_p", [P, P]), m.sb("iota_k", [P, NB2]), m.sb("starts", [P, NB2])
        blk = m.sb("blk", [P, NCH, NT])
        started = m.sb("started", [P, NT, NB2])
        in_blk = m.sb("in_blk", [P, NCH * NT, NB2], F32R)
        at_place = m.sb("at_place", [P, NCH * NT, P], F32R)
        t4, goh = m.sb("t4", [P, NT, NG]), m.sb("goh", [P, NT, NG])
        v1, v2, v3 = (m.sb(n, [P, NT]) for n in ("v1", "v2", "v3"))
        gsum = m.sb("gsum", [P, NT])
        es, k8, oh = m.sb("es", [P, NT, EPG]), m.sb("k8", [P, NT, EPG]), m.sb("oh", [P, NCH, NT, EPG])
        top = m.sb("top", [P, NCH, NT])
        full = m.sb("full", [P, NCH, NT, NE])
        prod = m.sb("prod", [P, NT, NE])
        sel = m.sb("sel", [P, NT, NE], BF16)
        before = m.sb("before", [P, NT + 1, NE], BF16)
        pos = m.sb("pos", [P, NT + 1, NE])
        over = m.sb("over", [P, NE, THR])
        nblk, inc, adj = m.sb("nblk", [P, NE]), m.sb("inc", [P, 2, NE]), m.sb("adj", [P, NE])
        cmp = m.sb("cmp", [P, NOV, NE])
        ov = m.sb("ov", [P, NOV + 1])
        slot = m.sb("slot", [P, NCH, NT])
        pp = m.ps("pp", (P, (NT + 1) * NE))
        tp = m.ps("tp")
        own_sem, consts, subbed, exped, d_ready, e_ready, sel_ready, pos_ready, places_ready, tokens_ready = (
            m.sem(n) for n in ("own", "consts", "subbed", "exped", "d_ready", "e_ready", "sel_ready", "pos_ready",
                               "places_ready", "tokens_ready"))
        block = ctx.enter_context(nc.Block())

        @block.gpsimd
        def _(pool):
            steps = Steps(pool, consts)
            steps.did(pool.iota(rev4[:], [[-1, NG]], base=NG, channel_multiplier=0, allow_small_or_imprecise_dtypes=True))
            steps.did(pool.iota(rev8[:], [[-1, EPG]], base=EPG, channel_multiplier=0, allow_small_or_imprecise_dtypes=True))
            steps.did(pool.iota(iota_e[:], [[1, NE]], base=0, channel_multiplier=0, allow_small_or_imprecise_dtypes=True))
            steps.did(pool.iota(iota_b[:], [[1, NOV]], base=0, channel_multiplier=0, allow_small_or_imprecise_dtypes=True))
            steps.did(pool.iota(thr[:], [[P, THR]], base=P, channel_multiplier=0, allow_small_or_imprecise_dtypes=True))
            steps.did(pool.iota(tok[:], [[P, NT]], base=0, channel_multiplier=1, allow_small_or_imprecise_dtypes=True))
            steps.did(pool.memset(ones[:], 1.0))
            steps.did(pool.memset(upper[:], 1.0))
            steps.did(pool.iota(iota_p[:], [[1, P]], base=0, channel_multiplier=0, allow_small_or_imprecise_dtypes=True))
            steps.did(pool.iota(iota_k[:], [[1, NB2]], base=1, channel_multiplier=0, allow_small_or_imprecise_dtypes=True))
            steps.did(pool.iota(starts[:], [[P, NB2]], base=0, channel_multiplier=0, allow_small_or_imprecise_dtypes=True))
            steps.wait()
            steps.did(pool.affine_select(out=upper[:], in_=upper[:], compare_op=ALU.is_gt, fill=0.0, base=0,
                                         pattern=[[1, P]], channel_multiplier=-1))
            assert steps.n == CONSTS

        @block.sync
        def _(sp):
            for n in range(NEXTRA):
                w, k = (w2[0], FE // P) if n < NEXTRA // 2 else (w3[1], KC)
                rows = slice(n, n + 1) if n < NEXTRA // 2 else slice(2 * n - NEXTRA, 2 * n - NEXTRA + 2)
                sp.dma_start(extra[:, n, :], w.rearrange("(p k) n -> p k n", k=k)[:, rows, :].rearrange("p k n -> p (k n)")
                             ).then_inc(extra_loaded[n], 16)

        @block.scalar
        def _(act):
            act.wait_ge(subbed, 1)
            act.activation(t4[:], t4[:], ACT.Exp).then_inc(exped, 1)
            act.wait_ge(d_ready, 1)
            act.activation(v2[:], v2[:], ACT.Exp).then_inc(e_ready, 1)

        @block.vector
        def _(dve):
            own = Steps(dve, own_sem)

            def do(ins):
                own.did(ins)
                own.wait()

            def first_max(out_onehot, values, best, key, rev, width):
                wide = lambda z: z.unsqueeze(2).to_broadcast([P, NT, width])
                do(dve.tensor_reduce(best, values, AX.X, ALU.max))
                do(dve.tensor_tensor(key, values, wide(best), ALU.is_equal))
                do(dve.tensor_tensor(key, key, rev.unsqueeze(1).to_broadcast([P, NT, width]), ALU.mult))
                do(dve.tensor_reduce(v3[:], key, AX.X, ALU.max))
                do(dve.tensor_tensor(out_onehot, key, wide(v3[:]), ALU.is_equal))

            dve.wait_ge(consts, CONSTS)
            gl = logits[:, :, 0:NG]
            el = logits[:, :, NG:NG + NE].rearrange("p t (g e) -> p t g e", g=NG)
            first_max(goh[:], gl, v1[:], t4[:], rev4[:], NG)
            dve.tensor_tensor(t4[:], gl, v1[:].unsqueeze(2).to_broadcast([P, NT, NG]), ALU.subtract).then_inc(subbed, 1)
            p4 = prod[:].rearrange("p t (g e) -> p t g e", g=NG)
            do(dve.tensor_tensor(p4, el, goh[:].unsqueeze(3).to_broadcast([P, NT, NG, EPG]), ALU.mult))
            do(dve.tensor_reduce(es[:], prod[:].rearrange("p t (g e) -> p t e g", g=NG), AX.X, ALU.add))
            first_max(oh[:, 0], es[:], top[:, 0], k8[:], rev8[:], EPG)
            do(dve.scalar_tensor_tensor(out=es[:], in0=oh[:, 0], scalar=-1e30, in1=es[:], op0=ALU.mult, op1=ALU.add))
            first_max(oh[:, 1], es[:], top[:, 1], k8[:], rev8[:], EPG)
            dve.tensor_tensor(v2[:], top[:, 1], top[:, 0], ALU.subtract).then_inc(d_ready, 1)
            dve.wait_ge(exped, 1)
            do(dve.tensor_reduce(gsum[:], t4[:], AX.X, ALU.add))
            dve.wait_ge(e_ready, 1)
            do(dve.tensor_scalar(v3[:], v2[:], 1.0, None, ALU.add))
            do(dve.tensor_tensor(v3[:], v3[:], gsum[:], ALU.mult))
            do(dve.reciprocal(gates[:, 0], v3[:]))
            do(dve.tensor_tensor(gates[:, 1], gates[:, 0], v2[:], ALU.mult))
            for i in range(NCH):
                f4 = full[:, i].rearrange("p t (g e) -> p t g e", g=NG)
                do(dve.tensor_tensor(f4, goh[:].unsqueeze(3).to_broadcast([P, NT, NG, EPG]),
                                     oh[:, i].unsqueeze(2).to_broadcast([P, NT, NG, EPG]), ALU.mult))
            do(dve.tensor_tensor(sel[:], full[:, 0], full[:, 1], ALU.add))
            do(dve.memset(before[:, 0, :], 0.0))
            for t in range(NT):
                step = dve.tensor_tensor(before[:, t + 1, :], before[:, t, :], sel[:, t, :], ALU.add)
                if t < NT - 1:
                    do(step)
            step.then_inc(sel_ready, 1)
            dve.wait_ge(pos_ready, 1)
            do(dve.tensor_copy(pos[:].rearrange("p t e -> p (t e)"), pp[:]))
            count = pos[:, NT, :]
            do(dve.tensor_tensor(over[:], count.unsqueeze(2).to_broadcast([P, NE, THR]),
                                 thr[:].unsqueeze(1).to_broadcast([P, NE, THR]), ALU.is_gt))
            do(dve.tensor_reduce(nblk[:], over[:], AX.X, ALU.add))
            do(dve.tensor_copy(inc[:, 0, :], nblk[:]))
            shift, cur = 1, 0
            while shift < NE:
                dve.tensor_tensor(inc[:, 1 - cur, shift:NE], inc[:, cur, shift:NE], inc[:, cur, 0:NE - shift], ALU.add)
                do(dve.tensor_copy(inc[:, 1 - cur, 0:shift], inc[:, cur, 0:shift]))
                shift, cur = 2 * shift, 1 - cur
            do(dve.tensor_tensor(adj[:], inc[:, cur, :], nblk[:], ALU.subtract))
            do(dve.tensor_tensor(adj[:], adj[:], iota_e[:], ALU.subtract))
            do(dve.tensor_scalar(adj[:], adj[:], float(NE - 1), float(P), ALU.add, ALU.mult))

            def of_choice(out, table):
                do(dve.tensor_tensor(prod[:], full[:, i], table, ALU.mult))
                do(dve.tensor_reduce(out, prod[:], AX.X, ALU.add))

            for i in range(NCH):
                of_choice(v1[:], pos[:, 0:NT, :])
                of_choice(v2[:], iota_e[:].unsqueeze(1).to_broadcast([P, NT, NE]))
                of_choice(v3[:], adj[:].unsqueeze(1).to_broadcast([P, NT, NE]))
                do(dve.scalar_tensor_tensor(out=v3[:], in0=v1[:], scalar=float(P), in1=v3[:], op0=ALU.is_ge, op1=ALU.mult))
                do(dve.scalar_tensor_tensor(out=v1[:], in0=v2[:], scalar=float(P), in1=v1[:], op0=ALU.mult, op1=ALU.add))
                do(dve.tensor_tensor(slot[:, i], v1[:], v3[:], ALU.add))
            do(dve.tensor_copy(slots[:], slot[:]))
            wide = lambda z, n: z.unsqueeze(2).to_broadcast([P, NT, n])
            each = lambda z, n: z.unsqueeze(1).to_broadcast([P, NT, n])
            for i in range(NCH):
                mine = slice(i * NT, (i + 1) * NT)
                do(dve.tensor_tensor(started[:], wide(slot[:, i], NB2), each(starts[:], NB2), ALU.is_ge))
                do(dve.tensor_reduce(blk[:, i], started[:], AX.X, ALU.add))
                do(dve.tensor_tensor(started[:], wide(blk[:, i], NB2), each(iota_k[:], NB2), ALU.is_equal))
                do(dve.tensor_tensor(in_blk[:, mine], started[:], wide(tok[:], NB2), ALU.mult))
                do(dve.scalar_tensor_tensor(out=blk[:, i], in0=blk[:, i], scalar=-float(P), in1=slot[:, i], op0=ALU.mult,
                                            op1=ALU.add))
                do(dve.tensor_scalar(blk[:, i], blk[:, i], float(P), None, ALU.add))
                dve.tensor_tensor(at_place[:, mine], wide(blk[:, i], P), each(iota_p[:], P), ALU.is_equal
                                  ).then_inc(places_ready, 1)
            do(dve.tensor_tensor(cmp[:], inc[:, cur, :].unsqueeze(1).to_broadcast([P, NOV, NE]),
                                 iota_b[:].unsqueeze(2).to_broadcast([P, NOV, NE]), ALU.is_le))
            do(dve.tensor_reduce(ov[:, 0:NOV], cmp[:], AX.X, ALU.add))
            do(dve.tensor_scalar(ov[:, 0:NOV], ov[:, 0:NOV], float(NE - 1), None, ALU.min))
            do(dve.tensor_copy(ov[:, NOV:NOV + 1], inc[:, cur, NE - 1:NE]))
            do(dve.tensor_copy(overflow[:], ov[0:1, :]))
            dve.wait_ge(tokens_ready, 1)
            dve.tensor_copy(tokens[:], tp[:, 0:NBLK])

        @block.tensor
        def _(pe):
            pe.wait_ge(consts, CONSTS)
            pe.wait_ge(sel_ready, 1)
            pe.matmul(pp[:], ones[:], before[:].rearrange("p t e -> p (t e)"), start=True, stop=False, skip_group_check=True)
            pe.matmul(pp[:, 0:NT * NE], upper[:], sel[:].rearrange("p t e -> p (t e)"), start=False, stop=True,
                      skip_group_check=True).then_inc(pos_ready, 1)
            for n in range(NCH * NT):
                if n % NT == 0:
                    pe.wait_ge(places_ready, n // NT + 1)
                mm = pe.matmul(tp[:, 0:NB2], at_place[:, n, :], in_blk[:, n, :], start=(n == 0), stop=(n == NCH * NT - 1))
            mm.then_inc(tokens_ready, 1)


def stage_experts(nc, raw, raw_loaded, extra, extra_loaded, tokens, h2_dram, w1, w3, w2, y_dram):
    FC = FE // P
    CH, NSPL = D, 6
    with ExitStack() as ctx:
        m = Memory(nc, ctx, "exp")
        w_hi, w_lo = m.sb("w_hi", [P, NSPL, CH], F32R), m.sb("w_lo", [P, NSPL, CH], F32R)
        rows = m.sb("rows", [P, 2], I32)
        xg = m.sb("xg", [P, 2, D])
        xT_hi, xT_lo = m.sb("xT_hi", [P, 2, KC, P], F32R), m.sb("xT_lo", [P, 2, KC, P], F32R)
        u, hm = m.sb("u", [P, FE]), m.sb("hm", [P, FE])
        hT_hi, hT_lo = m.sb("hT_hi", [P, FC, P], F32R), m.sb("hT_lo", [P, FC, P], F32R)
        y = m.sb("y", [P, D])
        ident = m.sb("ident", [P, P])
        pa, pb, thp = m.ps("pa"), m.ps("pb"), m.ps("thp")
        py, txp = m.ps("py", (P, D)), m.ps("txp", (P, D))
        names = ("id_made", "rows_ready", "carried", "hi_done", "lo_done", "used", "tx_ready", "xT_hi_ready", "xT_ready",
                 "silued", "hm_ready", "th_ready", "hT_hi_ready", "hT_ready", "y_kept", "y_stored")
        (id_made, rows_ready, carried, hi_done, lo_done, used, tx_ready, xT_hi_ready, xT_ready,
         silued, hm_ready, th_ready, hT_hi_ready, hT_ready, y_kept, y_stored) = (m.sem(n) for n in names)
        x_loaded = m.sems("x_loaded", 2)
        block = ctx.enter_context(nc.Block())
        LOOPS = (NE - 6) // 2

        def experts(eng, body, tail=None):
            for e in range(4):
                body(e, e % 2, e // 2)
            with eng.Fori(0, LOOPS) as i:
                body(2 * i + 4, 0, i + 2)
                body(2 * i + 5, 1, i + 2)
            body(NE - 2, 0, NE // 2 - 1)
            body(NE - 1, 1, NE // 2 - 1)
            if tail:
                tail()

        def first(e):
            return isinstance(e, int) and e == 0

        def more(e, n):
            return not isinstance(e, int) or e + n < NE

        def number(e, c):
            if isinstance(e, int) and e in (0, NE):
                return (c if c < 4 else c - 4) + (12 * NE - 4 if e else 0)
            return 12 * e + c - 4

        def place(e, c, size):
            if isinstance(e, int):
                return number(e, c) % size, number(e, c) // size
            return (c + 8) % size, (12 // size) * (e - 1) + (c + 8) // size

        def raw_at(e, c):
            if not isinstance(e, int):
                return raw[:, c, :], raw_loaded[c], 16 * e
            n = number(e, c)
            if n < NRAW:
                return raw[:, n, :], raw_loaded[n], 16
            if n < NRAW + NEXTRA:
                return extra[:, n - NRAW, :], extra_loaded[n - NRAW], 16
            turn, slot = divmod(n - NRAW - NEXTRA, NRAW)
            return raw[:, slot, :], raw_loaded[slot], 16 * (turn + 2)

        def chunks(e):
            if isinstance(e, int) and e == NE:
                return range(4, 8)
            return [c for c in range(12) if not (first(e) and 4 <= c < 8)]

        @block.sync
        def _(sp):
            def body(e, b=None, turn=None):
                for c in chunks(e):
                    n = number(e, c)
                    if isinstance(n, int) and n < NRAW + NEXTRA:
                        continue
                    dst, loaded, _ = raw_at(e, c)
                    if isinstance(n, int) and n < 2 * NRAW + NEXTRA:
                        sp.wait_ge(lo_done, n - NRAW - NEXTRA + 1)
                    else:
                        sp.wait_ge(lo_done, n - NRAW + 1)
                        sp.sem_inc(carried, 1)
                    j = c % 4
                    if 4 <= c < 8:
                        src = w2[bass.ds(e - 1, 1)].rearrange("e (p k) n -> (e p) k n", k=FC)[:, j:j + 1, :]
                    else:
                        src = (w1 if c < 4 else w3)[bass.ds(e, 1)].rearrange("e (p k) n -> (e p) k n", k=KC)[:, 2 * j:2 * j + 2, :]
                    sp.dma_start(dst, src.rearrange("p k n -> p (k n)")).then_inc(loaded, 16)

            experts(sp, body, lambda: body(NE))

        @block.gpsimd
        def _(pool):
            make_identity(nc, pool, ident, id_made)

            def gather(e, b):
                pool.tensor_copy(rows[:, b:b + 1], tokens[:, bass.ds(e, 1)]).then_inc(rows_ready, 1)
                pool.wait_ge(rows_ready, e + 1)
                pool.sem_inc(carried, 1)
                pool.indirect_dma_start(xg[:, b, :], None, h2_dram, bass.IndirectOffsetOnAxis(ap=rows[:, b:b + 1], axis=0)
                                        ).then_inc(x_loaded[b], 16)

            gather(0, 0)
            gather(1, 1)

            def body(e, b, turn):
                if more(e, 2):
                    pool.wait_ge(tx_ready, e + 1)
                    pool.sem_inc(carried, 1)
                    gather(e + 2, b)

            experts(pool, body)

        @block.scalar
        def _(act):
            act.sem_inc(y_stored, 16)

            def split_hi(e, c):
                n = number(e, c)
                src, loaded, count = raw_at(e, c)
                to, _ = place(e, c, NSPL)
                act.wait_ge(loaded, count)
                if not isinstance(n, int) or n >= NSPL:
                    act.wait_ge(used, n - NSPL + 1)
                act.copy(w_hi[:, to, :], src).then_inc(hi_done, 1)

            def split_xT(e, b):
                act.wait_ge(tx_ready, e + 1)
                act.copy(xT_hi[:, b].rearrange("p k t -> p (k t)"), txp[:]).then_inc(xT_hi_ready, 1)

            def split_hT(e):
                act.wait_ge(th_ready, e + 1)
                act.copy(hT_hi[:].rearrange("p k t -> p (k t)"), thp[:]).then_inc(hT_hi_ready, 1)

            def silu(e):
                act.wait_ge(used, number(e, 3) + 1)
                if not first(e):
                    act.wait_ge(hm_ready, e)
                act.activation(u[:], pa[:], ACT.Silu).then_inc(silued, 1)

            def keep_y(e):
                act.wait_ge(used, number(e + 1, 7) + 1)
                act.wait_ge(y_stored, 16 * (e + 1))
                act.copy(y[:], py[:]).then_inc(y_kept, 1)
                act.wait_ge(y_kept, e + 2)
                act.sem_inc(carried, 1)
                act.dma_start(y_dram[bass.ts(e, P), :], y[:]).then_inc(y_stored, 16)

            def body(e, b, turn):
                for c in chunks(e):
                    split_hi(e, c)
                    if first(e) and c == 3:
                        split_xT(0, 0)
                    if c == 0 and not (isinstance(e, int) and e < 2):
                        keep_y(e - 2)
                    if c == 5:
                        split_hT(e - 1)
                    if c == 8:
                        if more(e, 1):
                            split_xT(e + 1, 1 - b)
                        silu(e)

            def tail():
                for c in chunks(NE):
                    split_hi(NE, c)
                    if c == 4:
                        keep_y(NE - 2)
                    if c == 5:
                        split_hT(NE - 1)
                keep_y(NE - 1)
                act.wait_ge(y_stored, 16 * (NE + 1))

            experts(act, body, tail)

        @block.vector
        def _(dve):
            def split_lo(e, c):
                to, _ = place(e, c, NSPL)
                dve.wait_ge(hi_done, number(e, c) + 1)
                dve.tensor_tensor(w_lo[:, to, :], raw_at(e, c)[0], w_hi[:, to, :].bitcast(F32), ALU.subtract).then_inc(lo_done, 1)

            def split_xT(e, b):
                dve.wait_ge(xT_hi_ready, e + 1)
                dve.tensor_tensor(xT_lo[:, b].rearrange("p k t -> p (k t)"), txp[:],
                                  xT_hi[:, b].rearrange("p k t -> p (k t)").bitcast(F32), ALU.subtract).then_inc(xT_ready, 1)

            def split_hT(e):
                dve.wait_ge(hT_hi_ready, e + 1)
                dve.tensor_tensor(hT_lo[:].rearrange("p k t -> p (k t)"), thp[:],
                                  hT_hi[:].rearrange("p k t -> p (k t)").bitcast(F32), ALU.subtract).then_inc(hT_ready, 1)

            def gate_up(e):
                dve.wait_ge(used, number(e, 11) + 1)
                dve.wait_ge(silued, e + 1)
                if not first(e):
                    dve.wait_ge(th_ready, e)
                dve.tensor_tensor(hm[:], u[:], pb[:], ALU.mult).then_inc(hm_ready, 1)

            dve.sem_inc(y_kept, 1)
            def body(e, b, turn):
                for c in chunks(e):
                    split_lo(e, c)
                    if first(e) and c == 3:
                        split_xT(0, 0)
                    if c == 2 and not first(e):
                        gate_up(e - 1)
                    if c == 5:
                        split_hT(e - 1)
                    if c == 8 and more(e, 1):
                        split_xT(e + 1, 1 - b)

            def tail():
                gate_up(NE - 1)
                for c in chunks(NE):
                    split_lo(NE, c)
                    if c == 5:
                        split_hT(NE - 1)

            experts(dve, body, tail)

        @block.tensor
        def _(pe):
            def tx(e, b, turn):
                pe.wait_ge(x_loaded[b], 16 * (turn + 1))
                if not first(e):
                    pe.wait_ge(xT_ready, e)
                for k in range(KC):
                    mm = pe.transpose(txp[:, k * P:(k + 1) * P], xg[:, b, k:D:KC], ident[:])
                mm.then_inc(tx_ready, 1)

            def th(e):
                pe.wait_ge(hm_ready, e + 1)
                for k in range(FC):
                    mm = pe.transpose(thp[:, k * P:(k + 1) * P], hm[:, k:FE:FC], ident[:])
                mm.then_inc(th_ready, 1)

            def up(e, b, c, out):
                to, _ = place(e, c, NSPL)
                pe.wait_ge(lo_done, number(e, c) + 1)
                for r in range(2):
                    k = 2 * (c % 4) + r
                    for a, w in ((xT_hi, w_hi), (xT_hi, w_lo), (xT_lo, w_hi)):
                        mm = pe.matmul(out[:], a[:, b, k, :], w[:, to, r * FE:(r + 1) * FE],
                                       start=(k == 0 and w is w_hi and a is xT_hi), stop=(k == KC - 1 and a is xT_lo))
                mm.then_inc(used, 1)

            def down(e, c):
                to, _ = place(e, c, NSPL)
                k = c % 4
                pe.wait_ge(lo_done, number(e, c) + 1)
                for a, w in ((hT_hi, w_hi), (hT_hi, w_lo), (hT_lo, w_hi)):
                    for half in range(2):
                        mm = pe.matmul(py[:, half * HALF:(half + 1) * HALF], a[:, k, :], w[:, to, half * HALF:(half + 1) * HALF],
                                       start=(k == 0 and w is w_hi and a is hT_hi), stop=(k == FC - 1 and a is hT_lo))
                mm.then_inc(used, 1)

            def before_down(e):
                pe.wait_ge(hT_ready, e)
                pe.wait_ge(y_kept, e)

            pe.wait_ge(id_made, 2)
            tx(0, 0, 0)

            def body(e, b, turn):
                pe.wait_ge(xT_ready, e + 1)
                if not first(e):
                    pe.wait_ge(silued, e)
                for c in chunks(e):
                    if c == 4:
                        before_down(e)
                    if c == 8 and not first(e):
                        pe.wait_ge(hm_ready, e)
                    if 4 <= c < 8:
                        down(e, c)
                    else:
                        up(e, b, c, pa if c < 4 else pb)
                    if c == 1 and not first(e):
                        th(e - 1)
                    if c == 3 and more(e, 1):
                        tx(e + 1, 1 - b, turn + b)

            def tail():
                th(NE - 1)
                before_down(NE)
                for c in chunks(NE):
                    down(NE, c)

            experts(pe, body, tail)


def stage_overflow(nc, tokens, overflow, h2_dram, w1, w3, w2, y_dram):
    FC = FE // P
    with ExitStack() as ctx:
        m = Memory(nc, ctx, "ovf")
        w1_sb, w3_sb, w2_sb = m.sb("w1", [P, KC, FE]), m.sb("w3", [P, KC, FE]), m.sb("w2", [P, FC, D])
        rows = m.sb("rows", [P, 1], I32)
        xg, xT = m.sb("xg", [P, D]), m.sb("xT", [P, KC, P])
        u, hm, hT, y = m.sb("u", [P, FE]), m.sb("hm", [P, FE]), m.sb("hT", [P, FC, P]), m.sb("y", [P, D])
        ident = m.sb("ident", [P, P])
        pa, pb, thp = m.ps("pa"), m.ps("pb"), m.ps("thp")
        py, txp = m.ps("py", (P, D)), m.ps("txp", (P, D))
        names = ("id_made", "w_loaded", "rows_ready", "x_loaded", "tx_ready", "xT_ready", "ab_ready", "silued", "hm_ready",
                 "th_ready", "hT_ready", "y_ready", "y_kept", "y_stored", "carried")
        (id_made, w_loaded, rows_ready, x_loaded, tx_ready, xT_ready, ab_ready, silued, hm_ready, th_ready, hT_ready, y_ready,
         y_kept, y_stored, carried) = (m.sem(n) for n in names)
        block = ctx.enter_context(nc.Block())

        def blocks(eng, body):
            number = eng.value_load(overflow[0:1, NOV:NOV + 1], min_val=0, max_val=NOV)
            with eng.If(number > 0):
                with eng.Fori(0, NOV) as j:
                    with eng.If(j < number):
                        body(j)

        @block.sync
        def _(sp):
            sp.sem_inc(y_stored, 16)

            def body(j):
                sp.wait_ge(y_stored, 16 * (j + 1))
                sp.sem_inc(carried, 1)
                e = sp.value_load(overflow[0:1, bass.ds(j, 1)], min_val=0, max_val=NE - 1)
                for dst, w, k in ((w1_sb, w1, KC), (w3_sb, w3, KC), (w2_sb, w2, FC)):
                    sp.dma_start(dst[:].rearrange("p k n -> p (k n)"),
                                 w[bass.ds(e, 1)].rearrange("e (p k) n -> (e p) (k n)", k=k)).then_inc(w_loaded, 16)
                sp.wait_ge(y_kept, j + 1)
                sp.sem_inc(carried, 1)
                sp.dma_start(y_dram[bass.ts(NE + j, P), :], y[:]).then_inc(y_stored, 16)
                sp.wait_ge(y_stored, 16 * (j + 2))
                sp.sem_inc(carried, 1)

            blocks(sp, body)

        @block.gpsimd
        def _(pool):
            make_identity(nc, pool, ident, id_made)

            def body(j):
                pool.wait_ge(y_stored, 16 * (j + 1))
                pool.sem_inc(carried, 1)
                pool.tensor_copy(rows[:], tokens[:, bass.ds(NE + j, 1)]).then_inc(rows_ready, 1)
                pool.wait_ge(rows_ready, j + 1)
                pool.sem_inc(carried, 1)
                pool.indirect_dma_start(xg[:], None, h2_dram, bass.IndirectOffsetOnAxis(ap=rows[:], axis=0)
                                        ).then_inc(x_loaded, 16)

            blocks(pool, body)

        @block.scalar
        def _(act):
            def body(j):
                act.wait_ge(ab_ready, 2 * j + 1)
                act.activation(u[:], pa[:], ACT.Silu).then_inc(silued, 1)
                act.wait_ge(y_ready, j + 1)
                act.copy(y[:], py[:]).then_inc(y_kept, 1)

            blocks(act, body)

        @block.vector
        def _(dve):
            def body(j):
                dve.wait_ge(tx_ready, j + 1)
                dve.tensor_copy(xT[:].rearrange("p k t -> p (k t)"), txp[:]).then_inc(xT_ready, 1)
                dve.wait_ge(ab_ready, 2 * j + 2)
                dve.wait_ge(silued, j + 1)
                dve.tensor_tensor(hm[:], u[:], pb[:], ALU.mult).then_inc(hm_ready, 1)
                dve.wait_ge(th_ready, j + 1)
                dve.tensor_copy(hT[:].rearrange("p k t -> p (k t)"), thp[:]).then_inc(hT_ready, 1)

            blocks(dve, body)

        @block.tensor
        def _(pe):
            pe.wait_ge(id_made, 2)

            def body(j):
                pe.wait_ge(x_loaded, 16 * (j + 1))
                for k in range(KC):
                    mm = pe.transpose(txp[:, k * P:(k + 1) * P], xg[:, k:D:KC], ident[:])
                mm.then_inc(tx_ready, 1)
                pe.wait_ge(xT_ready, j + 1)
                pe.wait_ge(w_loaded, 48 * (j + 1))
                for out, w in ((pa, w1_sb), (pb, w3_sb)):
                    for k in range(KC):
                        mm = pe.matmul(out[:], xT[:, k, :], w[:, k, :], start=(k == 0), stop=(k == KC - 1))
                    mm.then_inc(ab_ready, 1)
                pe.wait_ge(hm_ready, j + 1)
                for k in range(FC):
                    mm = pe.transpose(thp[:, k * P:(k + 1) * P], hm[:, k:FE:FC], ident[:])
                mm.then_inc(th_ready, 1)
                pe.wait_ge(hT_ready, j + 1)
                for half in range(2):
                    for k in range(FC):
                        mm = pe.matmul(py[:, half * HALF:(half + 1) * HALF], hT[:, k, :],
                                       w2_sb[:, k, half * HALF:(half + 1) * HALF], start=(k == 0), stop=(k == FC - 1))
                mm.then_inc(y_ready, 1)

            blocks(pe, body)


def stage_combine(nc, gates, slots, x1, y_dram, mods, out):
    NY = 3
    with ExitStack() as ctx:
        m = Memory(nc, ctx, "fin")
        g2, shf, af = m.sb("g2", [P, 2, D]), m.sb("shf", [P, 2, D]), m.sb("af", [P, 2, D])
        ya, yb = m.sb("ya", [P, NT, D]), m.sb("yb", [P, NT, D])
        ys, sq, res = m.sb("ys", [P, NY, D]), m.sb("sq", [P, D]), m.sb("res", [P, 2, D])
        ss, ms, rstd = m.sb("ss", [P, 2]), m.sb("ms", [P, 2]), m.sb("rstd", [P, 2])
        neghalf, eps = m.sb("neghalf", [P, 1]), m.sb("eps", [P, 1])
        rows = m.sb("rows", [P, NT, 2], I32)
        names = ("consts", "rows_ready", "weighed", "summed", "gated", "x2_ready", "ss_ready", "ms_ready", "rstd_ready",
                 "scaled", "res_ready")
        (consts, rows_ready, weighed, summed, gated, x2_ready, ss_ready, ms_ready, rstd_ready, scaled, res_ready
         ) = (m.sem(n) for n in names)
        ya_loaded, yb_loaded = m.sems("ya_loaded", NT), m.sems("yb_loaded", NT)
        stored, g2_loaded, last_loaded = m.sems("stored", 2), m.sems("g2_loaded", 2), m.sems("last_loaded", 2)
        block = ctx.enter_context(nc.Block())

        def seq(t):
            return int(t >= NT0)

        @block.sync
        def _(sp):
            def load_mods(s, which):
                for dst, v in which:
                    sp.dma_start(dst[:, s, :], mods[s, v, :].unsqueeze(0).to_broadcast([P, D])).then_inc(
                        (g2_loaded if dst is g2 else last_loaded)[s], 16)

            def store(t):
                sp.wait_ge(res_ready, t + 1)
                sp.dma_start(out[t * P:(t + 1) * P, :], res[:, t % 2, :]).then_inc(stored[t % 2], 16)

            load_mods(0, [(g2, 5)])
            sp.wait_ge(yb_loaded[0], 16)
            load_mods(0, [(af, 7), (shf, 6)])
            for t in range(NT):
                store(t)
                if t == 1:
                    load_mods(1, [(g2, 5), (af, 7), (shf, 6)])
            for b in range(2):
                sp.wait_ge(stored[b], 16 * (NT // 2))

        @block.gpsimd
        def _(pool):
            pool.memset(neghalf[:], -0.5).then_inc(consts, 1)
            pool.memset(eps[:], EPS).then_inc(consts, 1)
            pool.tensor_copy(rows[:].rearrange("p t i -> p i t"), slots[:]).then_inc(rows_ready, 1)
            pool.wait_ge(consts, 2)
            pool.wait_ge(rows_ready, 1)

            def gather(t):
                for i, (dst, loaded) in enumerate(((ya, ya_loaded), (yb, yb_loaded))):
                    pool.indirect_dma_start(dst[:, t, :], None, y_dram, bass.IndirectOffsetOnAxis(ap=rows[:, t, i:i + 1], axis=0)
                                            ).then_inc(loaded[t], 16)

            for t in range(3):
                gather(t)
            for t in range(NT):
                v = ys[:, t % NY, :]
                pool.wait_ge(gated, t + 1)
                pool.tensor_tensor(v, v, x1[:, t * D:(t + 1) * D], ALU.add).then_inc(x2_ready, 1)
                if t + 3 < NT:
                    gather(t + 3)
                pool.wait_ge(ss_ready, t + 1)
                if t >= 2:
                    pool.wait_ge(scaled, t - 1)
                c = slice(t % 2, t % 2 + 1)
                pool.tensor_tensor(ms[:, c], ss[:, c], eps[:], ALU.add).then_inc(ms_ready, 1)
                pool.wait_ge(ms_ready, t + 1)
                pool.tensor_tensor(rstd[:, c], ms[:, c], neghalf[:], ALU.pow).then_inc(rstd_ready, 1)

        @block.scalar
        def _(act):
            def weigh(t):
                act.wait_ge(ya_loaded[t], 16)
                if t >= NY:
                    act.wait_ge(scaled, t - NY + 1)
                act.activation(ys[:, t % NY, :], ya[:, t, :], ACT.Copy, scale=gates[:, 0, t:t + 1]).then_inc(weighed, 1)

            weigh(0)
            for t in range(NT):
                if t + 1 < NT:
                    weigh(t + 1)
                act.wait_ge(x2_ready, t + 1)
                if t >= 2:
                    act.wait_ge(ms_ready, t - 1)
                act.activation(sq[:], ys[:, t % NY, :], ACT.Square, scale=D ** -0.5, accum_out=ss[:, t % 2:t % 2 + 1]
                               ).then_inc(ss_ready, 1)

        @block.vector
        def _(dve):
            def sum_rows(t):
                v = ys[:, t % NY, :]
                dve.wait_ge(yb_loaded[t], 16)
                dve.wait_ge(weighed, t + 1)
                dve.scalar_tensor_tensor(out=v, in0=yb[:, t, :], scalar=gates[:, 1, t:t + 1], in1=v, op0=ALU.mult, op1=ALU.add
                                         ).then_inc(summed, 1)
                dve.wait_ge(summed, t + 1)
                if t in (0, NT0):
                    dve.wait_ge(g2_loaded[seq(t)], 16)
                dve.tensor_tensor(v, v, g2[:, seq(t), :], ALU.mult).then_inc(gated, 1)

            sum_rows(0)
            for t in range(NT):
                if t + 1 < NT:
                    sum_rows(t + 1)
                dve.wait_ge(rstd_ready, t + 1)
                if t in (0, NT0):
                    dve.wait_ge(last_loaded[seq(t)], 32)
                if t >= 2:
                    dve.wait_ge(stored[t % 2], t // 2 * 16)
                r = res[:, t % 2, :]
                dve.scalar_tensor_tensor(out=r, in0=ys[:, t % NY, :], scalar=rstd[:, t % 2:t % 2 + 1], in1=af[:, seq(t), :],
                                         op0=ALU.mult, op1=ALU.mult).then_inc(scaled, 1)
                dve.wait_ge(scaled, t + 1)
                dve.tensor_tensor(r, r, shf[:, seq(t), :], ALU.add).then_inc(res_ready, 1)


def hybrid_encoder_kernel(nc, x_all, c_all, ln1_g, ln2_g, w_ada, b_ada, w_in, w_out, qn_g, kn_g, on_a_g, on_b_g,
                          w_rg, b_rg, w_re, b_re, w1, w3, w2, lnf_g, w_adaf, b_adaf, rope_tab, count_tab, out):
    def scratch(name, shape):
        return nc.dram_tensor(name, shape, F32, kind="Internal").ap()

    mods = scratch("mods", (2, 8, D))
    q, k, v = scratch("q", (T, WA + NHB * HD)), scratch("k", (T, NKH * HD)), scratch("v", (T, NKH * HD))
    o, h2 = scratch("o", (T, D)), scratch("h2", (T, D))
    y = scratch("y", (NBLK * P, D))
    with ExitStack() as ctx:
        m = Memory(nc, ctx, "in")
        w_hi, w_lo = m.sb("w_hi", [P, KC, IN_COLS], F32R), m.sb("w_lo", [P, KC, IN_COLS], F32R)
        stage_modulation(nc, w_hi, w_lo, c_all, w_ada, b_ada, w_adaf, b_adaf, ln1_g, ln2_g, lnf_g, w_in, mods)
        stage_projection(nc, w_hi, w_lo, x_all, mods, rope_tab, qn_g, kn_g, q, k, v)
    with ExitStack() as ctx:
        m = Memory(nc, ctx, "kv")
        kT, v_sb = m.sb("kT", [P, NKH, T], F32R), m.sb("v", [P, NT, NKH * HD])
        stage_keys(nc, kT, v_sb, k, v)
        stage_attention(nc, kT, v_sb, q, count_tab, o, y)
    with ExitStack() as ctx:
        m = Memory(nc, ctx, "route")
        x1 = m.sb("x1", [P, NT * D])
        logits, gates = m.sb("logits", [P, NT, NG + NE]), m.sb("gates", [P, 2, NT])
        slots, tokens = m.sb("slots", [P, 2, NT], I32), m.sb("tokens", [P, NBLK], I32)
        overflow = m.sb("overflow", [1, NOV + 1], I32)
        with ExitStack() as ring_ctx:
            ring = Memory(nc, ring_ctx, "ring")
            raw, raw_loaded = ring.sb("raw", [P, NRAW, D]), ring.sems("raw_loaded", NRAW)
            stage_output(nc, raw, raw_loaded, w1, w3, logits, o, x_all, mods, w_out, on_a_g, on_b_g, w_rg, b_rg, w_re, b_re,
                         x1, h2)
            beside = Memory(nc, ring_ctx, "beside")
            extra, extra_loaded = beside.sb("extra", [P, NEXTRA, D]), beside.sems("extra_loaded", NEXTRA)
            stage_route(nc, extra, extra_loaded, w2, w3, logits, gates, slots, tokens, overflow)
            stage_experts(nc, raw, raw_loaded, extra, extra_loaded, tokens, h2, w1, w3, w2, y)
        stage_overflow(nc, tokens, overflow, h2, w1, w3, w2, y)
        stage_combine(nc, gates, slots, x1, y, mods, out)


def rope_table():
    def angles(pos, n, theta):
        inv = (theta ** (-np.arange(0, n, 2, dtype=np.float64) / n)).astype(np.float32)
        ang = (pos.astype(np.float32)[:, None] * inv[None, :]).astype(np.float64)
        return np.cos(ang), np.sin(ang)

    parts = []
    for S in (S0, S1):
        pos = np.arange(S)
        c, s = angles(pos, HD // 4, 500000.0)
        cr, sr = angles(pos // 64, HD // 2, 10000.0)
        cc, sc = angles(pos % 64, HD // 2, 10000.0)
        parts.append(np.concatenate([c, c, -s, s, cr, cr, cc, cc, -sr, sr, -sc, sc], axis=1))
    return np.concatenate(parts).astype(np.float32)


def count_table():
    delta = np.arange(MSPAN)[None, :] - (S0 - P) - np.arange(P)[:, None]
    times = sum(((delta % dil == 0) & (np.abs(delta) <= dil * (window // (2 * dil)))).astype(np.float64)
                for window, dil in ((128, 1), (512, 4), (2048, 16)))
    return np.where(times > 0, np.log(np.maximum(times, 1)) / SCALE, -1e30).astype(np.float32)


_LAYER = ("ln1_g", "ln2_g", "w_ada", "b_ada", "w_in", "w_out", "qn_g", "kn_g", "on_a_g", "on_b_g", "w_rg", "b_rg", "w_re",
          "b_re", "w1", "w3", "w2")
_FINAL = ("lnf_g", "w_adaf", "b_adaf")


def kernel(**inputs):
    import concourse.bacc as _bacc
    from concourse.bass_utils import run_bass_kernel_spmd as _run

    arrays = {
        "x_all": np.concatenate([np.asarray(inputs["x_prompt"])[0], np.asarray(inputs["x_sample"])[0]]),
        "c_all": np.concatenate([np.asarray(inputs["c_prompt"]), np.asarray(inputs["c_sample"])]),
    }
    for name in _LAYER:
        arrays[name] = np.ascontiguousarray(np.asarray(inputs[name])[0])
    for name in _FINAL:
        arrays[name] = np.ascontiguousarray(np.asarray(inputs[name]))
    arrays["rope_tab"] = rope_table()
    arrays["count_tab"] = count_table()
    nc = _bacc.Bacc("TRN2", target_bir_lowering=False, num_devices=1)
    args = [nc.dram_tensor(f"in_{n}", a.shape, mybir.dt.from_np(a.dtype), kind="ExternalInput").ap() for n, a in arrays.items()]
    out = nc.dram_tensor("out_all", (T, D), F32, kind="ExternalOutput").ap()
    hybrid_encoder_kernel(nc, *args, out)
    r = _run(nc, [{f"in_{n}": a for n, a in arrays.items()}], core_ids=[0])
    y = r.results[0]["out_all"]
    return y[None, :S0], y[None, S0:]
```
